# Optimizing a Trainium2 kernel written in Bass

```python
import math, functools
import jax, jax.numpy as jnp
from jax import lax
import numpy as np

D_MODEL = 2048
BATCH = 1
SEQ = 256
DEPTH = 1
DEC_BATCH = 8
DEC_SEQ = 4
PAST_LEN = 256
PAGE_SIZE = 128

GDN_HEADS = 8
GDN_DK = 128
GDN_DV = 128
GDN_CONV = 4
GDN_CHUNK = 64
GDN_QK_W = GDN_HEADS * GDN_DK
GDN_V_W = GDN_HEADS * GDN_DV
DSA_HEADS = 8
DSA_KV_HEADS = 2
DSA_HEAD_DIM = 128
IDX_HEADS = 8
IDX_DIM = 64
IDX_SCALE = IDX_HEADS ** -0.5 * IDX_DIM ** -0.5
DSA_TOPK = 256
Q_BLOCK = 128
ROPE_THETA = 500000.0
ROPE_FRACTION = 4
D_FF = 5632
FFN_CONV = 3
NORM_EPS = 1e-6

kernel_name = "hybrid_gdn_dsa_convffn_decode_step"

def _in_sizes():
    return (2 * GDN_QK_W + GDN_V_W, GDN_V_W, GDN_HEADS, GDN_HEADS,
            DSA_HEADS * DSA_HEAD_DIM, DSA_KV_HEADS * DSA_HEAD_DIM, DSA_KV_HEADS * DSA_HEAD_DIM,
            IDX_HEADS * IDX_DIM, IDX_DIM, IDX_HEADS, D_MODEL, D_MODEL)

def _split_cols(y):
    cuts, acc = [], 0
    for s in _in_sizes()[:-1]:
        acc += s
        cuts.append(acc)
    return jnp.split(y, cuts, axis=-1)

def _rmsnorm(x, g):
    xf = x.astype(jnp.float32)
    y = xf * lax.rsqrt(jnp.mean(xf * xf, axis=-1, keepdims=True) + NORM_EPS)
    return (y * g.astype(jnp.float32)).astype(x.dtype)

def _l2norm(x):
    xf = x.astype(jnp.float32)
    return xf * lax.rsqrt(jnp.sum(xf * xf, axis=-1, keepdims=True) + NORM_EPS)

def _partial_rotary(x, pos):
    d = x.shape[-1]
    rot = d // ROPE_FRACTION
    half = rot // 2
    inv_freq = ROPE_THETA ** (-jnp.arange(half, dtype=jnp.float32) * (2.0 / rot))
    ang = pos.astype(jnp.float32)[:, None] * inv_freq[None, :]
    cos = jnp.cos(ang)[:, None, :]
    sin = jnp.sin(ang)[:, None, :]
    xf = x.astype(jnp.float32)
    x1, x2 = xf[..., :half], xf[..., half:rot]
    out = jnp.concatenate([x1 * cos - x2 * sin, x2 * cos + x1 * sin, xf[..., rot:]], axis=-1)
    return out.astype(x.dtype)

def _causal_dwconv(x, buf, w):
    width = w.shape[0]
    t = x.shape[1]
    xx = jnp.concatenate([buf.astype(x.dtype), x], axis=1)
    y = xx[:, 0:t] * w[0]
    for i in range(1, width):
        y = y + xx[:, i:i + t] * w[i]
    return y, xx[:, -(width - 1):]

def _gated_delta_chunked(q, k, v, g, beta, s0):
    f32 = jnp.float32
    B, T, H, DK = q.shape
    DV = v.shape[-1]
    C = min(GDN_CHUNK, T)
    n = -(-T // C)
    pad = n * C - T

    def prep(a):
        a = a.astype(f32)
        a = jnp.pad(a, [(0, 0), (0, pad)] + [(0, 0)] * (a.ndim - 2))
        a = a.reshape((B, n, C) + a.shape[2:])
        a = jnp.moveaxis(a, 3, 2)
        return jnp.moveaxis(a, 1, 0)

    q, k, v, g, beta = prep(q), prep(k), prep(v), prep(g), prep(beta)
    gc = jnp.cumsum(g, axis=-1)
    incl = jnp.tril(jnp.ones((C, C), bool))
    strict = jnp.tril(jnp.ones((C, C), bool), -1)
    decay = jnp.exp(jnp.where(incl, gc[..., :, None] - gc[..., None, :], -jnp.inf))
    kk = jnp.einsum('nbhcd,nbhjd->nbhcj', k, k)
    a_mat = jnp.where(strict, beta[..., :, None] * kk * decay, 0.0)
    lhs = a_mat + jnp.eye(C, dtype=f32)
    rhs = jnp.concatenate([beta[..., None] * v, (beta * jnp.exp(gc))[..., None] * k], axis=-1)
    sol = lax.linalg.triangular_solve(lhs, rhs, left_side=True, lower=True, unit_diagonal=True)
    u_v, w_k = sol[..., :DV], sol[..., DV:]
    qk = jnp.einsum('nbhcd,nbhjd->nbhcj', q, k) * decay
    q_dec = q * jnp.exp(gc)[..., None]
    k_end = k * jnp.exp(gc[..., -1:] - gc)[..., None]
    g_end = jnp.exp(gc[..., -1])

    def step(S, xs):
        u_v_i, w_k_i, qk_i, q_dec_i, k_end_i, g_end_i = xs
        u = u_v_i - jnp.einsum('bhck,bhkv->bhcv', w_k_i, S)
        o = jnp.einsum('bhck,bhkv->bhcv', q_dec_i, S) + jnp.einsum('bhcj,bhjv->bhcv', qk_i, u)
        S = S * g_end_i[..., None, None] + jnp.einsum('bhck,bhcv->bhkv', k_end_i, u)
        return S, o

    s_fin, o = lax.scan(step, s0.astype(f32), (u_v, w_k, qk, q_dec, k_end, g_end))
    o = jnp.moveaxis(o, 0, 1)
    o = jnp.moveaxis(o, 2, 3).reshape(B, n * C, H, DV)[:, :T]
    return o, s_fin

def _gather_rows(x, idx):
    return jax.vmap(lambda xb, ib: xb[ib])(x, idx)

def _indexer_topk(iq, iw, ik, pos_q, pos_k, topk):
    rel = jax.nn.relu(jnp.einsum('bqhd,bkd->bqhk', iq.astype(jnp.float32), ik.astype(jnp.float32)))
    score = jnp.einsum('bqhk,bqh->bqk', rel, iw.astype(jnp.float32) * IDX_SCALE)
    causal = pos_k[None, None, :] <= pos_q[None, :, None]
    score = jnp.where(causal, score, -jnp.inf)
    _, idx = lax.top_k(score, topk)
    valid = jnp.take(pos_k, idx) <= pos_q[None, :, None]
    return idx, valid

def _attend_selected(q, k_sel, v_sel, valid):
    B, Tq, H, HD = q.shape
    KV = k_sel.shape[-2]
    qg = q.reshape(B, Tq, KV, H // KV, HD).astype(jnp.float32)
    s = jnp.einsum('bqkgd,bqjkd->bqkgj', qg, k_sel.astype(jnp.float32)) * (HD ** -0.5)
    s = jnp.where(valid[:, :, None, None, :], s, -jnp.inf)
    p = jax.nn.softmax(s, axis=-1)
    o = jnp.einsum('bqkgj,bqjkd->bqkgd', p.astype(v_sel.dtype), v_sel)
    return o.reshape(B, Tq, H * HD)

def _dsa_prompt(q, k, v, iq, ik, iw, pos):
    B, T = q.shape[:2]
    topk = min(DSA_TOPK, T // 4)

    def block(i):
        s = i * Q_BLOCK
        sl = lambda a: lax.dynamic_slice_in_dim(a, s, Q_BLOCK, axis=1)
        pos_q = lax.dynamic_slice_in_dim(pos, s, Q_BLOCK)
        idx, valid = _indexer_topk(sl(iq), sl(iw), ik, pos_q, pos, topk)
        return _attend_selected(sl(q), _gather_rows(k, idx), _gather_rows(v, idx), valid)

    o = lax.map(block, jnp.arange(T // Q_BLOCK))
    return jnp.moveaxis(o, 0, 1).reshape(B, T, -1)

def _dsa_sample(q, k, v, iq, ik, iw, pos, cache_k, cache_v, cache_idx_k, page_table):
    DB, Ts = q.shape[:2]
    page = cache_k.shape[1]
    past = page_table.shape[1] * page
    ik_past = cache_idx_k[page_table].reshape(DB, past, IDX_DIM)
    ik_all = jnp.concatenate([ik_past.astype(ik.dtype), ik], axis=1)
    L = past + Ts
    topk = min(DSA_TOPK, L // 4)
    idx, valid = _indexer_topk(iq, iw, ik_all, pos, jnp.arange(L), topk)
    in_past = (idx < past)[..., None, None]
    pidx = jnp.minimum(idx, past - 1)
    phys = jax.vmap(lambda pt, ib: pt[ib // page])(page_table, pidx)
    off = pidx % page
    nidx = jnp.clip(idx - past, 0, Ts - 1)
    k_sel = jnp.where(in_past, cache_k[phys, off].astype(k.dtype), _gather_rows(k, nidx))
    v_sel = jnp.where(in_past, cache_v[phys, off].astype(v.dtype), _gather_rows(v, nidx))
    return _attend_selected(q, k_sel, v_sel, valid)

def _layer(x, c, pos, gdn_buf, gdn_s0, ffn_buf, attend, p):
    B, T, _ = x.shape
    ada = jnp.dot(jax.nn.silu(c), p["w_ada"]) + p["b_ada"]
    sh1, sc1, gt1, sh2, sc2, gt2 = jnp.split(ada[:, None, :], 6, axis=-1)
    h = _rmsnorm(x, p["g_norm1"]) * (1.0 + sc1) + sh1
    (qkv_raw, z, a_raw, b_raw, dq, dk, dv, iq, ik, iw, gate_gdn, gate_dsa) = _split_cols(jnp.dot(h, p["w_in"]))

    qkv, gdn_buf_new = _causal_dwconv(qkv_raw, gdn_buf, p["w_gdn_conv"])
    qkv = jax.nn.silu(qkv)
    gq, gk, gv = jnp.split(qkv, [GDN_QK_W, 2 * GDN_QK_W], axis=-1)
    gq = _l2norm(gq.reshape(B, T, GDN_HEADS, GDN_DK)) * (GDN_DK ** -0.5)
    gk = _l2norm(gk.reshape(B, T, GDN_HEADS, GDN_DK))
    gv = gv.reshape(B, T, GDN_HEADS, GDN_DV)
    log_alpha = -jnp.exp(p["a_log"].astype(jnp.float32)) * jax.nn.softplus(
        a_raw.astype(jnp.float32) + p["dt_bias"].astype(jnp.float32))
    beta = jax.nn.sigmoid(b_raw.astype(jnp.float32))
    o_gdn, s_new = _gated_delta_chunked(gq, gk, gv, log_alpha, beta, gdn_s0)
    o_gdn = _rmsnorm(o_gdn.astype(x.dtype), p["g_gdn_norm"]) * jax.nn.silu(z.reshape(B, T, GDN_HEADS, GDN_DV))
    o_gdn = o_gdn.reshape(B, T, GDN_V_W)

    dq = _partial_rotary(dq.reshape(B, T, DSA_HEADS, DSA_HEAD_DIM), pos)
    dk = _partial_rotary(dk.reshape(B, T, DSA_KV_HEADS, DSA_HEAD_DIM), pos)
    dv = dv.reshape(B, T, DSA_KV_HEADS, DSA_HEAD_DIM)
    iq = _partial_rotary(iq.reshape(B, T, IDX_HEADS, IDX_DIM), pos)
    ik = _partial_rotary(ik[:, :, None, :], pos)[:, :, 0, :]
    o_dsa = attend(dq, dk, dv, iq, ik, iw, pos)

    mix = (jax.nn.sigmoid(gate_gdn) * jnp.dot(o_gdn, p["w_gdn_out"])
           + jax.nn.sigmoid(gate_dsa) * jnp.dot(o_dsa, p["w_dsa_out"]))
    x = x + gt1 * jnp.dot(mix, p["w_o"])

    h2 = _rmsnorm(x, p["g_norm2"]) * (1.0 + sc2) + sh2
    u, ffn_buf_new = _causal_dwconv(jnp.dot(h2, p["w_up"]), ffn_buf, p["w_ffn_conv"])
    u_gate, u_val = jnp.split(u + p["b_ffn_conv"], 2, axis=-1)
    x = x + gt2 * jnp.dot(jax.nn.silu(u_gate) * u_val, p["w_down"])
    return x, (dk, dv, ik, s_new.astype(gdn_s0.dtype), gdn_buf_new, ffn_buf_new)

def setup_inputs(seed: int = 0) -> dict:
    key = jax.random.key(seed)
    ks = jax.random.split(key, 40)
    f32 = jnp.float32
    n_pages = PAST_LEN // PAGE_SIZE
    n_used = DEC_BATCH * n_pages
    n_pool = n_used + n_used // 4
    in_cols = sum(_in_sizes())
    conv_w = 2 * GDN_QK_W + GDN_V_W
    L = DEPTH

    def nrm(k, shape, scale):
        return jax.random.normal(k, shape, f32) * scale

    page_table = jax.random.permutation(ks[0], n_pool)[:n_used].reshape(DEC_BATCH, n_pages).astype(jnp.int32)
    dt = jnp.exp(jax.random.uniform(ks[1], (L, GDN_HEADS), f32, math.log(1e-3), math.log(1e-1)))
    dt_bias = dt + jnp.log(-jnp.expm1(-dt))
    a_log = jnp.log(jax.random.uniform(ks[2], (L, GDN_HEADS), f32, 1.0, 16.0))
    return {
        "x_prompt": nrm(ks[3], (BATCH, SEQ, D_MODEL), 1.0),
        "x_sample": nrm(ks[4], (DEC_BATCH, DEC_SEQ, D_MODEL), 1.0),
        "c_prompt": nrm(ks[5], (BATCH, D_MODEL), 1.0),
        "c_sample": nrm(ks[6], (DEC_BATCH, D_MODEL), 1.0),
        "cache_k": nrm(ks[7], (L, n_pool, PAGE_SIZE, DSA_KV_HEADS, DSA_HEAD_DIM), 1.0),
        "cache_v": nrm(ks[8], (L, n_pool, PAGE_SIZE, DSA_KV_HEADS, DSA_HEAD_DIM), 1.0),
        "cache_idx_k": nrm(ks[9], (L, n_pool, PAGE_SIZE, IDX_DIM), 1.0),
        "page_table": page_table,
        "state_gdn": nrm(ks[10], (L, DEC_BATCH, GDN_HEADS, GDN_DK, GDN_DV), 0.1),
        "state_gdn_conv": nrm(ks[11], (L, DEC_BATCH, GDN_CONV - 1, conv_w), 1.0),
        "state_ffn_conv": nrm(ks[12], (L, DEC_BATCH, FFN_CONV - 1, 2 * D_FF), 1.0),
        "w_ada": nrm(ks[13], (L, D_MODEL, 6 * D_MODEL), 0.5 * D_MODEL ** -0.5),
        "b_ada": nrm(ks[14], (L, 6 * D_MODEL), 0.02),
        "g_norm1": 1.0 + nrm(ks[15], (L, D_MODEL), 0.02),
        "w_in": nrm(ks[16], (L, D_MODEL, in_cols), D_MODEL ** -0.5),
        "w_gdn_conv": nrm(ks[17], (L, GDN_CONV, conv_w), GDN_CONV ** -0.5),
        "a_log": a_log,
        "dt_bias": dt_bias,
        "g_gdn_norm": 1.0 + nrm(ks[18], (L, GDN_DV), 0.02),
        "w_gdn_out": nrm(ks[19], (L, GDN_V_W, D_MODEL), GDN_V_W ** -0.5),
        "w_dsa_out": nrm(ks[20], (L, DSA_HEADS * DSA_HEAD_DIM, D_MODEL), (DSA_HEADS * DSA_HEAD_DIM) ** -0.5),
        "w_o": nrm(ks[21], (L, D_MODEL, D_MODEL), D_MODEL ** -0.5),
        "g_norm2": 1.0 + nrm(ks[22], (L, D_MODEL), 0.02),
        "w_up": nrm(ks[23], (L, D_MODEL, 2 * D_FF), D_MODEL ** -0.5),
        "w_ffn_conv": nrm(ks[24], (L, FFN_CONV, 2 * D_FF), FFN_CONV ** -0.5),
        "b_ffn_conv": nrm(ks[25], (L, 2 * D_FF), 0.02),
        "w_down": nrm(ks[26], (L, D_FF, D_MODEL), D_FF ** -0.5),
        "g_final": 1.0 + nrm(ks[27], (D_MODEL,), 0.02),
    }

def reference(x_prompt, x_sample, c_prompt, c_sample, cache_k, cache_v, cache_idx_k, page_table,
              state_gdn, state_gdn_conv, state_ffn_conv, w_ada, b_ada, g_norm1, w_in, w_gdn_conv,
              a_log, dt_bias, g_gdn_norm, w_gdn_out, w_dsa_out, w_o, g_norm2, w_up, w_ffn_conv,
              b_ffn_conv, w_down, g_final):
    layer_params = dict(w_ada=w_ada, b_ada=b_ada, g_norm1=g_norm1, w_in=w_in, w_gdn_conv=w_gdn_conv,
                        a_log=a_log, dt_bias=dt_bias, g_gdn_norm=g_gdn_norm, w_gdn_out=w_gdn_out,
                        w_dsa_out=w_dsa_out, w_o=w_o, g_norm2=g_norm2, w_up=w_up,
                        w_ffn_conv=w_ffn_conv, b_ffn_conv=b_ffn_conv, w_down=w_down)
    B, T, _ = x_prompt.shape
    Ts = x_sample.shape[1]
    dtp = x_prompt.dtype
    past = page_table.shape[1] * cache_k.shape[2]
    pos_p = jnp.arange(T)
    pos_s = past + jnp.arange(Ts)
    conv_w = 2 * GDN_QK_W + GDN_V_W

    h_p, h_s = x_prompt, x_sample
    outs_p, outs_s = [], []
    for l in range(DEPTH):
        p = {name: arr[l] for name, arr in layer_params.items()}
        h_p, st_p = _layer(h_p, c_prompt, pos_p,
                           jnp.zeros((B, GDN_CONV - 1, conv_w), dtp),
                           jnp.zeros((B, GDN_HEADS, GDN_DK, GDN_DV), dtp),
                           jnp.zeros((B, FFN_CONV - 1, 2 * D_FF), dtp),
                           _dsa_prompt, p)
        attend_s = functools.partial(_dsa_sample, cache_k=cache_k[l], cache_v=cache_v[l],
                                     cache_idx_k=cache_idx_k[l], page_table=page_table)
        h_s, st_s = _layer(h_s, c_sample, pos_s, state_gdn_conv[l], state_gdn[l], state_ffn_conv[l],
                           attend_s, p)
        outs_p.append(st_p)
        outs_s.append(st_s)

    y_prompt = _rmsnorm(h_p, g_final)
    y_sample = _rmsnorm(h_s, g_final)
    stk = lambda outs, i: jnp.stack([o[i] for o in outs])
    return (y_prompt, y_sample,
            stk(outs_p, 0), stk(outs_p, 1), stk(outs_p, 2), stk(outs_p, 3), stk(outs_p, 4), stk(outs_p, 5),
            stk(outs_s, 0), stk(outs_s, 1), stk(outs_s, 2), stk(outs_s, 3), stk(outs_s, 4), stk(outs_s, 5))


_drawn_inputs = setup_inputs


def setup_inputs(seed=0):
    import zlib

    import numpy as np

    out = dict(_drawn_inputs(seed))
    spreads = {}
    factors = {'g_gdn_norm': 85.588,
     'g_norm2': 8.546,
     'b_ffn_conv': 8.0,
     'g_final': 22.47,
     'cache_k': 6.388,
     'cache_v': 5.04,
     'cache_idx_k': 5.765}
    for name, (base, spread) in spreads.items():
        noise = np.random.default_rng([zlib.crc32(name.encode()), seed]).standard_normal(out[name].shape)
        drawn = base * np.exp(spread * noise) if base else spread * noise
        out[name] = __import__('jax').numpy.asarray(drawn.astype(out[name].dtype))
    for name, factor in factors.items():
        out[name] = (out[name] * factor).astype(out[name].dtype)
    return out
```

```python
from contextlib import ExitStack

import numpy as np
import concourse.bass as bass
from concourse import mybir

P = 128
D_MODEL, SEQ, DB, TS = 2048, 256, 8, 4
PAGE, PAST, NPOOL = 128, 256, 20
H, DK, CONV = 8, 128, 4
QH, KV, HD = 8, 2, 128
IH, ID = 8, 64
D_FF, FCONV = 5632, 3
ROPE_THETA, EPS = 500000.0, 1e-6
NS = DB * TS
N = SEQ + NS
NC = 1 + DB
KT = D_MODEL // P
NQC = 2 * SEQ // P - 2
KS, CT = 4, 2
SLOT = KS * CT * P
RAW, RING = 4, 4
QKV_T, Z_T, DSA_T = 3 * H, H, 16
FT = D_FF // P
FC = 4
NCH = FT // FC
LV = 7
L_S = PAST + TS
TOPK_P, TOPK_S = min(256, SEQ // 4), min(256, L_S // 4)
IDX_SCALE = IH ** -0.5 * ID ** -0.5
NEG_MASK, NEG_TAKEN, BIG = -2.0e38, -3.0e38, 1.0e30
HI_S = (CONV - 1) * DB
HI_F = (FCONV - 1) * DB

V_BADA = 0
V_G1 = V_BADA + 6 * KT
V_G2 = V_G1 + KT
V_GF = V_G2 + KT
V_WC = V_GF + KT
V_WF = V_WC + CONV * QKV_T
V_BF = V_WF + FCONV * 2 * FT
V_GN = V_BF + 2 * FT
V_ALL = V_GN + 1

PHASES = [("ada1", 2 * KT // CT * (KT // KS), False), ("qkv", QKV_T // CT * (KT // KS), True),
          ("z", Z_T // CT * (KT // KS), True), ("dsa", DSA_T // CT * (KT // KS), True),
          ("small", KT // KS, True), ("ada2", 4 * KT // CT * (KT // KS), False),
          ("out", (KT // CT) * (2 * (KT // KS) + 2 * (H // KS)), True),
          ("wo", KT // CT * (KT // KS), True),
          ("ffn", NCH * (2 * FC // CT * (KT // KS) + KT // CT), True)]
BASE, SPLIT = {}, {}
_b = _s = 0
for _n, _c, _sp in PHASES:
    BASE[_n], SPLIT[_n] = _b, _s
    _b += _c
    _s += _c * _sp
NSLOTS = _b


def constants():
    f = np.float32
    c = {}
    c["ident"] = np.eye(P, dtype=f)
    c["ones"] = np.ones((P, P), f)
    j, i = np.meshgrid(np.arange(P), np.arange(P), indexing="ij")
    c["incl"] = (i >= j).astype(f)
    c["lev"] = np.stack([((i >> (l + 1)) == (j >> (l + 1))) & (((i >> l) & 1) == 1) & (((j >> l) & 1) == 0)
                         for l in range(LV)], 1).astype(f)
    js, is_ = np.meshgrid(np.arange(NS), np.arange(NS), indexing="ij")
    same = (js % DB) == (is_ % DB)
    tj, ti = js // DB, is_ // DB
    s = np.zeros((P, 4, NS), f)
    s[:NS, 0] = same & (ti >= tj)
    s[:NS, 1] = same & ((ti >> 1) == (tj >> 1)) & ((ti & 1) == 1) & ((tj & 1) == 0)
    s[:NS, 2] = same & ((ti >> 1) == 1) & ((tj >> 1) == 0)
    s[:NS, 3, :TS * DB] = (np.arange(NS)[:, None] % DB) == (np.arange(NS)[None, :] % DB)
    c["smask"] = s
    mb = (np.arange(NS)[None, :] % DB == np.arange(DB)[:, None]).astype(f)
    c["maskb"] = np.broadcast_to(mb[None], (P, DB, NS)).copy()
    c["bcol"] = np.zeros((P, DB), f)
    c["bcol"][:NS] = mb.T
    pos = np.concatenate([np.arange(SEQ), PAST + np.repeat(np.arange(TS), DB)]).astype(f)
    tab = np.zeros((P, 4, N), f)
    rot_m = np.zeros((P, 2, P), f)
    for n, d in enumerate((HD, ID)):
        rot = d // 4
        half = rot // 2
        inv = (f(ROPE_THETA) ** (-np.arange(half, dtype=f) * f(2.0 / rot))).astype(f)
        ang = (pos[None, :] * inv[:, None]).astype(f)
        cos, sin = np.cos(ang).astype(f), np.sin(ang).astype(f)
        tab[:, 2 * n] = 1.0
        for o in range(0, P, d):
            tab[o:o + half, 2 * n] = tab[o + half:o + rot, 2 * n] = cos
            tab[o:o + half, 2 * n + 1] = tab[o + half:o + rot, 2 * n + 1] = sin
            for a in range(half):
                rot_m[o + half + a, n, o + a] = -1.0
                rot_m[o + a, n, o + half + a] = 1.0
    c["rope"], c["rotm"] = tab, rot_m
    q = np.arange(P)[:, None, None] + P * np.arange(2)[None, :, None]
    c["causal"] = np.where(np.arange(SEQ)[None, None, :] <= q, -NEG_TAKEN, NEG_MASK).astype(f)
    cs = np.full((P, L_S), -NEG_TAKEN, f)
    t = np.arange(NS) // DB
    cs[:NS, PAST:] = np.where(np.arange(TS)[None, :] <= t[:, None], -NEG_TAKEN, NEG_MASK)
    c["causal_s"] = cs
    sel = np.zeros((P, H), f)
    sel[:H] = np.eye(H)
    c["sel"] = sel
    c["eps"] = np.full((P, 1), EPS, f)
    c["one"] = np.ones((P, 1), f)
    return c


CONST_SIZE = {"ident": P, "ones": P, "incl": P, "lev": LV * P, "smask": 4 * NS, "maskb": DB * NS,
              "bcol": DB, "rope": 4 * N, "rotm": 2 * P, "causal": 2 * SEQ, "causal_s": L_S,
              "sel": H, "eps": 1, "one": 1}


def decoder_step(nc, A, O):
    f32, f32r, i32 = mybir.dt.float32, mybir.dt.float32r, mybir.dt.int32
    ALU, ACT, AX = mybir.AluOpType, mybir.ActivationFunctionType, mybir.AxisListType
    ds = bass.ds
    ctx = ExitStack()
    with ctx:
        base0 = ((nc.sbuf_base + 31) // 32) * 32

        class Place:
            def __init__(self, at):
                self.at = at

            def take(self, name, shape, dt=f32):
                size = 4 * int(np.prod(shape[1:]))
                t = nc.alloc_sbuf_tensor_at(name, shape, dt, offset=self.at)
                self.at += (size + 31) // 32 * 32
                return t

        fixed = Place(base0)
        const_at = fixed.at
        consts = fixed.take("consts", [P, sum(CONST_SIZE.values())])
        cv, off = {}, 0
        for name, size in CONST_SIZE.items():
            cv[name] = consts[:, off:off + size]
            off += size
        ident, ones = cv["ident"], cv["ones"]
        lev = cv["lev"].rearrange("p (l i) -> p l i", l=LV)
        smask = cv["smask"].rearrange("p (m i) -> p m i", m=4)
        maskb = cv["maskb"].rearrange("p (b i) -> p b i", b=DB)
        rope = cv["rope"].rearrange("p (m n) -> p m n", m=4)
        rotm = cv["rotm"].rearrange("p (m n) -> p m n", m=2)
        causal = cv["causal"].rearrange("p (c k) -> p c k", c=2)
        causal_s, sel, eps_c, one_c = cv["causal_s"], cv["sel"], cv["eps"], cv["one"]
        vec = fixed.take("vec", [P, V_ALL])
        ada = fixed.take("ada", [P, 6 * KT, NC])
        cact = fixed.take("cact", [P, KT, NC])
        ptab = fixed.take("ptab", [1, DB * (PAST // PAGE)], i32)
        heads_v = fixed.take("heads_v", [H, 2])
        rsb = fixed.take("rsb", [P, N])
        h_hi = fixed.take("h_hi", [P, KT, N], f32r)
        h_lo = fixed.take("h_lo", [P, KT, N], f32r)
        raw = fixed.take("raw", [P, RAW, KS, CT * P])
        ring_at = fixed.at
        w_hi = fixed.take("w_hi", [P, RING, KS, CT * P], f32r)
        w_lo = fixed.take("w_lo", [P, RING, KS, CT * P], f32r)
        rest_at = fixed.at

        pl = Place(rest_at)
        x = pl.take("x", [P, KT, N])
        og_p = Place(rest_at)
        og_hi = og_p.take("og_hi", [P, H, N], f32r)
        og_lo = og_p.take("og_lo", [P, H, N], f32r)
        qkv_at = pl.at
        qkv = pl.take("qkv", [P, QKV_T, N])
        z = pl.take("z", [P, Z_T, N])
        dsa_at = pl.at
        dsa = pl.take("dsa", [P, DSA_T, N])
        ikk = pl.take("ikk", [P, N])
        sm_iw = pl.take("sm_iw", [H, N])
        rows = pl.take("rows", [H, 4, N])
        tail_at = pl.at
        ip = Place(rest_at)
        cst = ip.take("cst", [P, QKV_T, HI_S + NS])
        cpt = ip.take("cpt", [P, QKV_T, CONV - 1])
        cin = ip.take("cin", [P, CT, CONV - 1 + SEQ])
        cy = ip.take("cy", [P, CT, N])
        sm_a = ip.take("sm_a", [H, N])
        sm_b = ip.take("sm_b", [H, N])
        sm_t = ip.take("sm_t", [H, 2, N])
        assert ip.at <= qkv_at
        np_ = Place(qkv_at)
        sq = np_.take("sq", [P, 2, N])
        ht = np_.take("ht", [P, 2, N])
        hf = np_.take("hf", [P, 2, N])
        amul = np_.take("amul", [P, KT, NC])
        gp = Place(ring_at)
        gc_t = gp.take("gc_t", [P, 3, H])
        ke_t = gp.take("ke_t", [P, 3, H])
        sqb = gp.take("sqb", [P, 2, N])
        nrm = gp.take("nrm", [P, 2, N])
        qk = gp.take("qk", [P, 2, N])
        rows_m = gp.take("rows_m", [H, 3, N])
        br = gp.take("br", [P, 3, N])
        e_p = gp.take("e_p", [P, 2, P])
        e_s = gp.take("e_s", [NS, NS])
        qkd_p = gp.take("qkd_p", [P, 2, P])
        qkd_s = gp.take("qkd_s", [NS, NS])
        at_p = gp.take("at_p", [P, 2, P])
        at_s = gp.take("at_s", [NS, NS])
        bt_p = gp.take("bt_p", [P, LV - 1, 2, P])
        bt_s = gp.take("bt_s", [NS, NS])
        tt = gp.take("tt", [P, 4, P])
        tt_s = gp.take("tt_s", [NS, 2, NS])
        x_p = gp.take("x_p", [P, 2, P])
        x_s = gp.take("x_s", [NS, NS])
        gq = Place(tail_at)
        r_t = gq.take("r_t", [P, P])
        r_ts = gq.take("r_ts", [P, NS])
        r_p = gq.take("r_p", [P, P])
        r_s = gq.take("r_s", [NS, P])
        u_p = gq.take("u_p", [P, P])
        u_s = gq.take("u_s", [NS, P])
        kend = gq.take("kend", [P, 2, P])
        kend_s = gq.take("kend_s", [NS, P])
        kmask = gq.take("kmask", [NS, DB, P])
        qdec = gq.take("qdec", [P, P])
        st_p = gq.take("st_p", [P, P])
        st_in = gp.take("st_in", [P, DB, P])
        st_out = gq.take("st_out", [P, DB, P])
        o_add = gq.take("o_add", [P, NS])
        o_b = gq.take("o_b", [P, N])
        assert gp.at <= rest_at
        dp = Place(ring_at)
        v_c = dp.take("v_c", [P, DB, PAST // PAGE, KV * HD])
        dq_ = Place(qkv_at)
        do_hi = dq_.take("do_hi", [P, QH, N], f32r)
        do_lo = dq_.take("do_lo", [P, QH, N], f32r)
        kt_c = dq_.take("kt_c", [P, DB, KV, L_S])
        assert dq_.at <= dsa_at
        dr = Place(ring_at + 4 * DB * (PAST // PAGE) * KV * HD)
        ik_c = dr.take("ik_c", [P, DB, L_S])
        sc_p = dr.take("sc_p", [P, 2, SEQ])
        wk_p = dr.take("wk_p", [P, 2, SEQ])
        sc_s = dr.take("sc_s", [NS, L_S])
        wk_s = dr.take("wk_s", [NS, L_S])
        iw_t = dr.take("iw_t", [P, 2, IH])
        iw_s = dr.take("iw_s", [NS, IH])
        top8 = dr.take("top8", [P, 3, 8])
        vtok_s = dr.take("vtok_s", [P, KV * HD])
        assert dr.at <= rest_at, (dr.at, rest_at)
        dt_ = Place(tail_at)
        iqm = dt_.take("iqm", [P, 4, DB, NS])
        rel = dt_.take("rel", [P, 2, L_S])
        vtok = dt_.take("vtok", [P, 2, KV * HD])
        bias_p = dt_.take("bias_p", [P, P + SEQ])
        bias_s = dt_.take("bias_s", [NS, L_S])
        du = Place(dsa_at + 12 * N * 4)
        dt2 = Place(tail_at)
        rtmp = dt2.take("rtmp", [P, N])
        q_m = dt2.take("q_m", [P, DB, NS])
        p_tm = dt2.take("p_tm", [P, 2, DB, NS])
        assert dt2.at <= tail_at + 4 * 4 * DB * NS + 4 * 2 * L_S
        q_r = du.take("q_r", [P, N])
        s_p = du.take("s_p", [P, P + SEQ])
        s_s = du.take("s_s", [NS, L_S])
        stat = du.take("stat", [P, 4, 3])
        assert du.at <= dsa_at + DSA_T * N * 4
        p_t = dt_.take("p_t", [P, 3, P])
        pn = dt_.take("pn", [NS, NS])
        pn_t = dt_.take("pn_t", [P, NS])
        o_n = dt_.take("o_n", [P, 2, P])
        o_ns = dt_.take("o_ns", [NS, P])
        rot_t = dt_.take("rot_t", [P, N])
        mp = Place(qkv_at + 2 * 4 * QH * N)
        mix = mp.take("mix_hi", [P, KT, N], f32r)
        mix_lo = mp.take("mix_lo", [P, KT, N], f32r)
        sg = mp.take("sg", [P, 2, CT, N])
        mt = mp.take("mt", [P, CT, N])
        fp = Place(np_.at)
        act_f = fp.take("act_f", [P, CT, N])
        act_hi = fp.take("act_hi", [P, 2, FC, N], f32r)
        act_lo = fp.take("act_lo", [P, 2, FC, N], f32r)
        fst = fp.take("fst", [P, 2 * FT, HI_F + NS])
        fpt = fp.take("fpt", [P, 2 * FT, FCONV - 1])
        fin = fp.take("fin", [P, CT, FCONV - 1 + SEQ])
        fy = fp.take("fy", [P, CT, N])
        fsil = fp.take("fsil", [P, CT, N])
        dtmp = fp.take("dtmp", [P, NS])
        for q_ in (pl, gq, dt_, mp, fp):
            assert q_.at <= nc.sbuf_usable_end, (q_.at, nc.sbuf_usable_end)

        bank = [ctx.enter_context(nc.psum_tensor(f"bank{i}", [P, 512], f32)) for i in range(8)]

        def sem(name):
            return ctx.enter_context(nc.semaphore(name))

        raw_in = [sem(f"raw_in{i}") for i in range(RAW)]
        raw_free = [sem(f"raw_free{i}") for i in range(RAW)]
        hi_ready, lo_ready = sem("hi_ready"), sem("lo_ready")
        ring_free = sem("ring_free")
        grp_ready = [sem(f"grp_ready{i}") for i in range(4)]
        grp_free = [sem(f"grp_free{i}") for i in range(4)]
        const_in, x_in, x_back, out_done = sem("const_in"), sem("x_in"), sem("x_back"), sem("out_done")
        c_ready = sem("c_ready")
        sq_ready, sq_used, ssq_ready, rs_ready = sem("sq_ready"), sem("sq_used"), sem("ssq_ready"), sem("rs_ready")
        h_t, h_hi_ready, h_lo_ready = sem("h_t"), sem("h_hi_ready"), sem("h_lo_ready")
        conv_y, conv_used = sem("conv_y"), sem("conv_used")
        small_done = sem("small_done")
        row_dve, row_act, row_tr, row_end = sem("row_dve"), sem("row_act"), sem("row_tr"), sem("row_end")
        G = {n: sem("gdn_" + n) for n in (
            "sq ssq rowm bc nrm br qk gram kt e d t1 t1t x xs dt t kss ra rt rs u us kend qkd sa S1 ks rb sb o osq "
            "oss on sin spout ssout dve act").split()}
        X = {n: sem("dsa_" + n) for n in (
            "load rot rotd vt vtd iqm idx rel acc newk topk q rotq s m p pn pt ptm pts o on ot end outd ikn").split()}
        g_sig, mix_done = sem("g_sig"), sem("mix_done")
        x_done = sem("x_done")
        sil_done, act_ready, down_done = sem("sil_done"), sem("act_ready"), sem("down_done")
        y_ready = sem("y_ready")

        used = [0] * 4
        gbase = {}
        for name, groups, sets in (("ada1", 2 * KT // CT, 2), ("qkv", QKV_T // CT, 2), ("z", Z_T // CT, 2),
                                   ("dsa", DSA_T // CT, 2), ("small", 1, 1), ("ada2", 4 * KT // CT, 1),
                                   ("out", 4 * (KT // CT), 4), ("wo", KT // CT, 4),
                                   ("ffn", NCH * (2 * FC // CT + KT // CT), 4)):
            gbase[name] = list(used)
            for s_ in range(sets):
                used[s_] += groups // sets

        def grp(name, sets, g, i=0, per=0):
            return g % sets, gbase[name][g % sets] + g // sets + i * (per // sets)

        def raw_at(name, j, i=0, per=0):
            s_ = BASE[name] + j
            return s_ % RAW, s_ // RAW + i * (per // RAW)

        def split_at(name, j, i=0, per=0):
            s_ = SPLIT[name] + j
            return s_ % RING, s_ + i * per

        block = ctx.enter_context(nc.Block())

        @block.sync
        def _(sp):
            per = RAW
            whole = NSLOTS // per
            assert NSLOTS % per == 0

            def load(r, use, slot):
                sp.wait_ge(raw_free[r], use + 1)
                sp.dma_start(raw[:, r, :, :].rearrange("p k c -> p (k c)"),
                             A["stream"][ds(slot, 1), :, :].rearrange("s p n -> (s p) n")).then_inc(raw_in[r], 16)

            with sp.Fori(0, whole) as i:
                for r in range(per):
                    load(r, i, i * per + r)
            sp.wait_ge(y_ready, KT // 2)
            sp.dma_start(O["y"], x[:, :, :].rearrange("p k n -> p (k n)")).then_inc(out_done, 16)
            sp.wait_ge(out_done, 16 * 8)
            sp.wait_ge(G["spout"], 16 * H)
            sp.wait_ge(G["ssout"], 16 * H)

        @block.gpsimd
        def _(pool):
            for r in range(RAW):
                pool.sem_inc(raw_free[r], 1)
            pool.sem_inc(ring_free, RING)
            pool.sem_inc(sq_used, 2)
            pool.sem_inc(h_lo_ready, 2)

            def lo(name, j, i=0, per=0):
                r, use = raw_at(name, j, i, per)
                q, cnt = split_at(name, j, i, per)
                pool.wait_ge(hi_ready, cnt + 1)
                nc.gpsimd.tensor_tensor(w_lo[:, q, :, :], raw[:, r, :, :], w_hi[:, q, :, :].bitcast(f32),
                                        ALU.subtract).then_inc(lo_ready, 1)
                pool.wait_ge(lo_ready, cnt + 1)
                pool.sem_inc(raw_free[r], 1)

            def h_rest(base):
                with pool.Fori(0, KT // 2) as i:
                    for s_ in range(2):
                        pool.wait_ge(h_hi_ready, i * 2 + base + s_ + 1)
                        k = i * 2 + s_
                        nc.gpsimd.tensor_tensor(h_lo[:, ds(k, 1), :].rearrange("p k n -> p (k n)"), hf[:, s_, :],
                                                h_hi[:, ds(k, 1), :].rearrange("p k n -> p (k n)").bitcast(f32),
                                                ALU.subtract).then_inc(h_lo_ready, 1)

            def run(name, first, count, per):
                with pool.Fori(0, count // per) as i:
                    for j in range(per):
                        lo(name, first + j, i, per)

            h_rest(0)
            run("qkv", 0, 48 + 16 + 32, 8)
            for j in range(KT // KS):
                lo("small", j)
            run("out", 0, 96 + 32, 8)
            h_rest(KT)
            run("ffn", 0, PHASES[-1][1], 8)

        @block.scalar
        def _(act):
            A_ = nc.scalar.activation
            act.sem_inc(conv_used, 2)
            for g_ in range(4):
                act.sem_inc(grp_free[g_], 1)
            act.dma_start(x[:, :, :].rearrange("p k n -> p (k n)"), A["x"]).then_inc(x_in, 16)
            act.dma_start(cact[:, :, :].rearrange("p k n -> p (k n)"), A["c"]).then_inc(x_in, 16)
            act.dma_start(consts[:, :], A["consts"]).then_inc(const_in, 16)
            act.dma_start(vec[:, :], A["vec"]).then_inc(const_in, 16)
            act.dma_start(heads_v[:, :], A["heads_v"]).then_inc(const_in, 16)
            act.dma_start(ptab[:, :], A["ptab"]).then_inc(X["load"], 16)

            def hi(name, j, i=0, per=0):
                r, use = raw_at(name, j, i, per)
                q, cnt = split_at(name, j, i, per)
                act.wait_ge(raw_in[r], use * 16 + 16)
                act.wait_ge(ring_free, cnt + 1)
                A_(w_hi[:, q, :, :], raw[:, r, :, :], ACT.Copy).then_inc(hi_ready, 1)

            act.wait_ge(x_in, 32)
            A_(cact[:, :, :], cact[:, :, :], ACT.Silu).then_inc(c_ready, 1)

            def norm_stats(n):
                with act.Fori(0, KT // 2) as i:
                    for s_ in range(2):
                        act.wait_ge(sq_used, i * 2 + n * KT + s_ + 1)
                        A_(sq[:, s_, :], x[:, ds(i * 2 + s_, 1), :].rearrange("p k n -> p (k n)"),
                           ACT.Square).then_inc(sq_ready, 1)
                act.wait_ge(ssq_ready, n + 1)
                A_(rsb[:, :], bank[7][:, 0:N], ACT.Ln, bias=eps_c, scale=1.0 / D_MODEL)
                act.drain()
                A_(rsb[:, :], rsb[:, :], ACT.Exp, scale=-0.5).then_inc(rs_ready, 1)

            def h_round(base):
                with act.Fori(0, KT // 2) as i:
                    for s_ in range(2):
                        act.wait_ge(h_t, i * 2 + base + s_ + 1)
                        A_(h_hi[:, ds(i * 2 + s_, 1), :].rearrange("p k n -> p (k n)"), hf[:, s_, :],
                           ACT.Copy).then_inc(h_hi_ready, 1)

            act.wait_ge(const_in, 48)
            norm_stats(0)
            h_round(0)
            act.wait_ge(h_t, KT)
            act.dma_start(cst[:, :, 0:HI_S], A["gdn_hist"].rearrange("p (t n) -> p t n", t=QKV_T)).then_inc(const_in, 16)

            LA = 2

            def silu_tiles(g, i=0, per=0):
                for c in range(CT):
                    n = g * CT + c
                    t = i * (per * CT) + n
                    act.wait_ge(conv_y, t + 1)
                    A_(qkv[:, ds(t, 1), :].rearrange("p k n -> p (k n)"), cy[:, c, :],
                       ACT.Silu).then_inc(conv_used, 1)

            for j in range(LA):
                hi("qkv", j)
            with act.Fori(0, 5) as i:
                for j in range(4):
                    hi("qkv", LA + j, i, 8)
                silu_tiles(0, i, 2)
                for j in range(4):
                    hi("qkv", LA + 4 + j, i, 8)
                silu_tiles(1, i, 2)
            for j in range(4):
                hi("qkv", 40 + LA + j)
            silu_tiles(10)
            for j in range(4):
                hi("qkv", 44 + LA + j)
            silu_tiles(11)

            def z_tiles(g, i=0, per=0):
                bs, cnt = grp("z", 2, g, i, per)
                act.wait_ge(grp_ready[bs], cnt + 1)
                for c in range(CT):
                    t = i * (per * CT) + g * CT + c
                    A_(z[:, ds(t, 1), :].rearrange("p k n -> p (k n)"), bank[2 * bs + c][:, 0:N], ACT.Silu)
                act.drain()
                act.sem_inc(grp_free[bs], 1)

            for g in range(4):
                for j in range(4):
                    hi("z", LA + 4 * g + j)
                z_tiles(g)
            with act.Fori(0, 3) as i:
                for j in range(8):
                    hi("dsa", LA + j, i, 8)
            for j in range(24 + LA, 32 + 4):
                hi("dsa", j)

            act.wait_ge(small_done, 1)
            A_(sm_t[:, 0, :], sm_a[:, :], ACT.Identity, bias=heads_v[:, 1:2])
            A_(sm_b[:, :], sm_b[:, :], ACT.Exp, scale=-1.0)
            A_(heads_v[:, 0:1], heads_v[:, 0:1], ACT.Exp)
            act.drain()
            A_(sm_a[:, :], sm_t[:, 0, :], ACT.Abs)
            act.drain()
            A_(sm_a[:, :], sm_a[:, :], ACT.Exp, scale=-1.0)
            act.drain()
            A_(sm_a[:, :], sm_a[:, :], ACT.Ln, bias=one_c[0:H, :]).then_inc(row_act, 1)
            act.wait_ge(row_dve, 1)
            A_(rows[:, 2, :], rows[:, 0, :], ACT.Exp)
            A_(rows[:, 3, :], rows[:, 3, :], ACT.Exp, scale=-1.0).then_inc(row_act, 1)

            act.wait_ge(small_done, 1)
            act.dma_start(O["gdn_tail_s"].rearrange("p (t n) -> p t n", t=QKV_T), cst[:, :, HI_S + NS - HI_S:]).then_inc(out_done, 16)
            act.dma_start(O["gdn_tail_p"], cpt[:, :, :].rearrange("p t n -> p (t n)")).then_inc(out_done, 16)

            def g_load(h):
                act.dma_start(st_in[:, :, :].rearrange("p b n -> p (b n)"),
                              A["state"][ds(h, 1), :, :].rearrange("h p n -> (h p) n")).then_inc(G["sin"], 16)

            g_load(0)
            act.wait_ge(out_done, 32)
            with act.Fori(0, H) as h:
                A_(sqb[:, 0, :], qkv[:, ds(h, 1), :].rearrange("p k n -> p (k n)"), ACT.Square)
                A_(sqb[:, 1, :], qkv[:, ds(h + H, 1), :].rearrange("p k n -> p (k n)"), ACT.Square).then_inc(G["sq"], 1)
                act.wait_ge(G["ssq"], h + 1)
                A_(nrm[:, 0, :], bank[2][:, 0:N], ACT.Ln, bias=eps_c)
                A_(nrm[:, 1, :], bank[3][:, 0:N], ACT.Ln, bias=eps_c)
                act.drain()
                A_(nrm[:, :, :], nrm[:, :, :], ACT.Exp, scale=-0.5).then_inc(G["nrm"], 1)
                act.wait_ge(G["bc"], h + 1)
                for m in range(3):
                    last = A_(br[:, m, :], bank[4 + m][:, 0:N], ACT.Copy)
                last.then_inc(G["br"], 1)
                act.wait_ge(G["e"], h + 1)
                A_(e_s[:, :], e_s[:, :], ACT.Exp)
                A_(e_p[:, :, :], e_p[:, :, :], ACT.Exp).then_inc(G["d"], 1)
                for l in range(1, LV):
                    act.wait_ge(G["x"], h * (LV - 1) + l)
                    if l == 1:
                        A_(x_s[:, :], bank[4][0:NS, 2 * P:2 * P + NS], ACT.Copy)
                    A_(x_p[:, :, :].rearrange("p c n -> p (c n)"), bank[4][:, 0:2 * P], ACT.Copy).then_inc(G["xs"], 1)
                for c in range(2):
                    act.wait_ge(G["rt"], h * 2 + c + 1)
                    if c == 0:
                        A_(r_s[:, :], bank[6][0:NS, P:2 * P], ACT.Copy)
                    A_(r_p[:, :], bank[6][:, 0:P], ACT.Copy).then_inc(G["rs"], 1)
                    act.wait_ge(G["u"], h * 2 + c + 1)
                    if c == 0:
                        A_(u_s[:, :], bank[6][0:NS, P:2 * P], ACT.Copy)
                    A_(u_p[:, :], bank[6][:, 0:P], ACT.Copy).then_inc(G["us"], 1)
                act.wait_ge(G["o"], h + 1)
                act.dma_start(O["state_p"][ds(h, 1), :, :].rearrange("h p n -> (h p) n"), st_p[:, :]).then_inc(G["spout"], 16)
                act.dma_start(O["state_s"][ds(h, 1), :, :].rearrange("h p n -> (h p) n"),
                              st_out[:, :, :].rearrange("p b n -> p (b n)")).then_inc(G["ssout"], 16)
                hn = (h + 1) & (H - 1)
                g_load(hn)
                A_(sqb[:, 0, :], o_b[:, :], ACT.Square).then_inc(G["osq"], 1)
                act.wait_ge(G["oss"], h + 1)
                A_(nrm[:, 0, :], bank[7][:, 0:N], ACT.Ln, bias=eps_c, scale=1.0 / DK)
                act.drain()
                A_(nrm[:, 0, :], nrm[:, 0, :], ACT.Exp, scale=-0.5).then_inc(G["on"], 1)
                act.wait_ge(G["dve"], h + 1)
            act.wait_ge(G["sin"], 16 * (H + 1))

            with ExitStack() as rs_:
                act.wait_ge(X["load"], 16)
                for b in range(DB):
                    for g in range(PAST // PAGE):
                        pid = act.value_load(ptab[0:1, 2 * b + g:2 * b + g + 1], min_val=0, max_val=NPOOL - 1)
                        act.dma_start(kt_c[:, b, :, PAGE * g:PAGE * (g + 1)],
                                      A["ck"][ds(pid, 1), :, :].rearrange("s p (k n) -> (s p) k n", k=KV)).then_inc(X["load"], 16)
                        act.dma_start(ik_c[:, b, PAGE * g:PAGE * (g + 1)],
                                      A["cik"][ds(pid, 1), :, :].rearrange("s p n -> (s p) n")).then_inc(X["load"], 16)
                        act.dma_start(v_c[:, b, g, :],
                                      A["cv"][ds(pid, 1), :, :].rearrange("s p n -> (s p) n")).then_inc(X["load"], 16)
            act.wait_ge(X["rotd"], 7)
            act.dma_start(O["k"], dsa[:, QH:QH + KV, :].rearrange("p k n -> p (k n)")).then_inc(out_done, 16)
            act.dma_start(O["v"], dsa[:, QH + KV:QH + 2 * KV, :].rearrange("p k n -> p (k n)")).then_inc(out_done, 16)
            act.dma_start(O["ik"], ikk[0:ID, :]).then_inc(out_done, 16)
            act.wait_ge(X["newk"], 1)
            act.wait_ge(X["vt"], 1)
            A_(vtok[:, :, :].rearrange("p c n -> p (c n)"), bank[4][:, :], ACT.Copy)
            A_(vtok_s[0:NS, :], bank[5][0:NS, 0:KV * HD], ACT.Copy)
            A_(iw_t[:, :, :].rearrange("p c n -> p (c n)"), bank[6][:, 0:2 * IH], ACT.Copy, scale=IDX_SCALE)
            A_(iw_s[:, :], bank[6][0:NS, 2 * IH:3 * IH], ACT.Copy, scale=IDX_SCALE).then_inc(X["vtd"], 1)
            for n in range(3 * IH):
                act.wait_ge(X["idx"], n + 1)
                if n >= 2:
                    act.wait_ge(X["acc"], n - 1)
                if n < 2 * IH:
                    A_(rel[:, n % 2, 0:SEQ], bank[2 + n % 2][:, 0:SEQ], ACT.Relu).then_inc(X["rel"], 1)
                else:
                    A_(rel[0:NS, n % 2, :], bank[2 + n % 2][0:NS, 0:L_S], ACT.Relu).then_inc(X["rel"], 1)
            act.wait_ge(X["load"], 16 * (1 + 3 * DB * (PAST // PAGE)))
            sc_ = HD ** -0.5
            with act.Fori(0, QH) as h:
                act.wait_ge(X["m"], h + 1)
                A_(s_p[:, 0:P], s_p[:, 0:P], ACT.Exp, bias=stat[:, 0, 0:1], scale=sc_, accum_out=stat[:, 1, 0:1])
                A_(s_p[:, P:], s_p[:, P:], ACT.Exp, bias=stat[:, 0, 1:2], scale=sc_, accum_out=stat[:, 1, 1:2])
                A_(s_s[:, :], s_s[:, :], ACT.Exp, bias=stat[0:NS, 0, 2:3], scale=sc_,
                   accum_out=stat[0:NS, 1, 2:3]).then_inc(X["p"], 1)
                act.wait_ge(X["pt"], h + 1)
                A_(p_t[:, :, :].rearrange("p c n -> p (c n)"), bank[5][:, 0:3 * P], ACT.Copy).then_inc(X["pts"], 1)

            def gate_tiles(which, i, g0):
                bs, cnt = grp("out", 4, 4 * g0 + which, i, 8)
                act.wait_ge(grp_ready[bs], cnt + 1)
                act.wait_ge(mix_done, i * 2 + g0 + 1)
                for c in range(CT):
                    last = A_(sg[:, which, c, :], bank[2 * bs + c][:, 0:N], ACT.Sigmoid)
                last.then_inc(g_sig, 1)
                act.wait_ge(g_sig, (i * 2 + g0) * 2 + which + 1)
                act.sem_inc(grp_free[bs], 1)

            act.wait_ge(out_done, 16 * 5)
            act.wait_ge(X["end"], QH)
            for j in range(LA):
                hi("out", j)

            def out_body(i, hold=0):
                for g0 in range(2):
                    for j in range(4):
                        hi("out", LA + 12 * g0 + j, i, 24)
                    gate_tiles(0, i, g0)
                    for j in range(4, 8):
                        hi("out", LA + 12 * g0 + j, i, 24)
                    gate_tiles(1, i, g0)
                    for j in range(8, 12):
                        hi("out", LA + 12 * g0 + j, i, 24)

            with act.Fori(0, 4) as i:
                out_body(i)
            bs, cnt = grp("out", 4, 4 * (KT // CT) - 1)
            act.wait_ge(grp_ready[bs], cnt + 1)
            act.dma_start(x[:, :, :].rearrange("p k n -> p (k n)"), A["x"]).then_inc(x_back, 16)
            with act.Fori(0, 3) as i:
                for j in range(8):
                    hi("wo", LA + j, i, 8)
            for j in range(24 + LA, 32):
                hi("wo", j)
            act.wait_ge(x_done, KT)
            norm_stats(1)
            act.dma_start(fst[:, :, 0:HI_F], A["ffn_hist"].rearrange("p (t n) -> p t n", t=2 * FT)).then_inc(const_in, 16)
            h_round(KT)

            def ffn_silu(c0, q0, i):
                for c in range(CT):
                    t = i * FC + c0 + c
                    act.wait_ge(conv_y, QKV_T + i * FC + c0 + c + 1)
                    A_(fsil[:, c, :], fy[:, c, :], ACT.Silu,
                       bias=vec[:, ds(t + V_BF, 1)]).then_inc(sil_done, 1)

            for j in range(LA):
                hi("ffn", j)
            for j in range(4):
                hi("ffn", LA + j)
            ffn_silu(0, 0, 0)
            for j in range(4, 12):
                hi("ffn", LA + j)
            ffn_silu(2, 0, 0)
            for j in range(12, 16):
                hi("ffn", LA + j)
            with act.Fori(0, NCH - 1) as i:
                for j in range(4):
                    hi("ffn", 16 + LA + j, i, 24)
                ffn_silu(0, 0, i + 1)
                for j in range(4, 20):
                    hi("ffn", 16 + LA + j, i, 24)
                ffn_silu(2, 0, i + 1)
                for j in range(20, 24):
                    hi("ffn", 16 + LA + j, i, 24)
            for j in range(16 + LA + 24 * (NCH - 1), PHASES[-1][1]):
                hi("ffn", j)
            act.wait_ge(down_done, NCH * KT)
            act.dma_start(O["ffn_tail_s"].rearrange("p (t n) -> p t n", t=2 * FT), fst[:, :, NS:]).then_inc(out_done, 16)
            act.dma_start(O["ffn_tail_p"], fpt[:, :, :].rearrange("p t n -> p (t n)")).then_inc(out_done, 16)
            norm_stats(2)

        @block.vector
        def _(dve):
            V = nc.vector
            T_, S_, STT, CP = V.tensor_tensor, V.tensor_scalar, V.scalar_tensor_tensor, V.tensor_copy
            row = lambda a: a.rearrange("p k n -> p (k n)")

            def cond(base, tiles):
                for c in range(CT):
                    last = S_(row(ada[:, ds(tiles + c, 1), :]), bank[base + c][:, 0:NC], vec[:, ds(tiles + c + V_BADA, 1)], None, ALU.add)
                return last

            dve.sem_inc(mix_done, 1)
            dve.wait_ge(x_in, 32)
            dve.wait_ge(const_in, 48)
            with dve.Fori(0, KT // CT) as i:
                for g in range(2):
                    bs, cnt = grp("ada1", 2, g, i, 2)
                    dve.wait_ge(grp_ready[bs], cnt + 1)
                    cond(2 * bs, (i * 2 + g) * CT).then_inc(grp_free[bs], 1)
            dve.drain()

            def scale_shift(n, sub):
                gcol = V_G1 if n == 0 else V_G2
                g_b = vec[:, gcol:gcol + KT].unsqueeze(2).to_broadcast([P, KT, NC])
                STT(amul[:, :, :], ada[:, (3 * sub + 1) * KT:(3 * sub + 2) * KT, :], 1.0, g_b, ALU.add, ALU.mult)
                dve.drain()
                dve.wait_ge(rs_ready, n + 1)
                with dve.Fori(0, KT // 2) as i:
                    for s_ in range(2):
                        k = i * 2 + s_
                        T_(ht[:, s_, :], row(x[:, ds(k, 1), :]), rsb[:, :], ALU.mult)
                    dve.drain()
                    for s_ in range(2):
                        k = i * 2 + s_
                        dve.wait_ge(h_lo_ready, i * 2 + n * KT + s_ + 1)
                        am, sh = row(amul[:, ds(k, 1), :]), row(ada[:, ds(k + 3 * sub * KT, 1), :])
                        S_(hf[:, s_, 0:SEQ], ht[:, s_, 0:SEQ], am[:, 0:1], sh[:, 0:1], ALU.mult, ALU.add)
                        T_(ht[:, s_, SEQ:].rearrange("p (t b) -> p t b", b=DB), ht[:, s_, SEQ:].rearrange("p (t b) -> p t b", b=DB),
                           am[:, 1:NC].unsqueeze(1).to_broadcast([P, TS, DB]), ALU.mult)
                    dve.drain()
                    for s_ in range(2):
                        k = i * 2 + s_
                        sh = row(ada[:, ds(k + 3 * sub * KT, 1), :])
                        T_(hf[:, s_, SEQ:].rearrange("p (t b) -> p t b", b=DB), ht[:, s_, SEQ:].rearrange("p (t b) -> p t b", b=DB),
                           sh[:, 1:NC].unsqueeze(1).to_broadcast([P, TS, DB]), ALU.add).then_inc(h_t, 1)
                    dve.drain()

            scale_shift(0, 0)
            dve.drain()
            V.memset(cin[:, :, 0:CONV - 1], 0.0)
            dve.wait_ge(const_in, 64)

            def conv(psum, c, src, y, st, tile, tap0, taps, hist, ntile, keep):
                CP(src[:, c, taps - 1:taps - 1 + SEQ], psum[:, 0:SEQ])
                CP(row(st[:, ds(tile, 1), hist:hist + NS]), psum[:, SEQ:N])
                dve.drain()
                for w_ in range(taps):
                    wc = vec[:, ds(tile + (tap0 + w_ * ntile), 1)]
                    sp_ = src[:, c, w_:w_ + SEQ]
                    ss_ = row(st[:, ds(tile, 1), DB * w_:DB * w_ + NS])
                    if w_ == 0:
                        S_(y[:, c, 0:SEQ], sp_, wc, None, ALU.mult)
                        S_(y[:, c, SEQ:], ss_, wc, None, ALU.mult)
                        CP(row(keep[:, ds(tile, 1), :]), src[:, c, SEQ:SEQ + taps - 1])
                    else:
                        STT(y[:, c, 0:SEQ], sp_, wc, y[:, c, 0:SEQ], ALU.mult, ALU.add)
                        last = STT(y[:, c, SEQ:], ss_, wc, y[:, c, SEQ:], ALU.mult, ALU.add)
                    if w_ < taps - 1:
                        dve.drain()
                return last

            with dve.Fori(0, 6) as i:
                for g in range(2):
                    bs, cnt = grp("qkv", 2, g, i, 2)
                    dve.wait_ge(grp_ready[bs], cnt + 1)
                    for c in range(CT):
                        t = i * 4 + 2 * g + c
                        dve.wait_ge(conv_used, t + 1)
                        conv(bank[2 * bs + c], c, cin, cy, cst, t, V_WC, CONV, HI_S, QKV_T, cpt).then_inc(conv_y, 1)
                    dve.drain()
                    dve.sem_inc(grp_free[bs], 1)
            with dve.Fori(0, 4) as i:
                for g in range(2):
                    bs, cnt = grp("dsa", 2, g, i, 2)
                    dve.wait_ge(grp_ready[bs], cnt + 1)
                    for c in range(CT):
                        last = CP(row(dsa[:, ds(i * 4 + 2 * g + c, 1), :]), bank[2 * bs + c][:, 0:N])
                    dve.drain()
                    dve.sem_inc(grp_free[bs], 1)
            bs, cnt = grp("small", 1, 0)
            dve.wait_ge(grp_ready[bs], cnt + 1)
            CP(ikk[:, :], bank[0][:, 0:N])
            CP(sm_a[:, :], bank[1][0:H, 0:N])
            CP(sm_b[:, :], bank[1][32:32 + H, 0:N])
            CP(sm_iw[:, :], bank[1][64:64 + H, 0:N])
            dve.drain()
            dve.sem_inc(grp_free[bs], 1)
            dve.sem_inc(small_done, 1)

            dve.wait_ge(row_act, 1)
            STT(sm_t[:, 1, :], sm_t[:, 0, :], 0.0, sm_a[:, :], ALU.max, ALU.add)
            S_(sm_b[:, :], sm_b[:, :], 1.0, None, ALU.add)
            dve.drain()
            V.memset(sm_t[:, 0, :], 1.0)
            S_(sm_t[:, 1, :], sm_t[:, 1, :], heads_v[:, 0:1], -1.0, ALU.mult, ALU.mult)
            V.reciprocal(rows[:, 1, :], sm_b[:, :])
            dve.drain()
            for c in range(2):
                V.tensor_tensor_scan(rows[:, 0, c * P:(c + 1) * P], sm_t[:, 0, 0:P], sm_t[:, 1, c * P:(c + 1) * P], 0.0,
                                     ALU.mult, ALU.add)
            CP(rows[:, 0, SEQ:SEQ + DB], sm_t[:, 1, SEQ:SEQ + DB])
            for t in range(1, TS):
                dve.drain()
                o_ = SEQ + t * DB
                T_(rows[:, 0, o_:o_ + DB], rows[:, 0, o_ - DB:o_], sm_t[:, 1, o_:o_ + DB], ALU.add)
            dve.drain()
            for c in range(2):
                S_(rows[:, 3, c * P:(c + 1) * P], rows[:, 0, c * P:(c + 1) * P], rows[:, 0, (c + 1) * P - 1:(c + 1) * P], None, ALU.subtract)
            T_(rows[:, 3, SEQ:].rearrange("p (t b) -> p t b", b=DB), rows[:, 0, SEQ:].rearrange("p (t b) -> p t b", b=DB),
               rows[:, 0, N - DB:N].unsqueeze(1).to_broadcast([H, TS, DB]), ALU.subtract).then_inc(row_dve, 1)
            dve.wait_ge(row_tr, 1)
            for t_, bk in ((gc_t, 2), (ke_t, 3)):
                CP(t_[:, 0:2, :].rearrange("p c h -> p (c h)"), bank[bk][:, 0:2 * H])
                CP(t_[0:NS, 2, :], bank[bk][0:NS, 2 * H:3 * H])
            dve.drain()

            def ada2(n, it):
                bs, cnt = grp("ada2", 1, n, it, 2)
                dve.wait_ge(grp_ready[bs], cnt + 1)
                cond(0, 2 * KT + (it * 2 + n) * CT).then_inc(grp_free[bs], 1)

            with dve.Fori(0, H) as h:
                q_h, k_h, v_h = (row(qkv[:, ds(h + m * H, 1), :]) for m in range(3))
                S_(rows_m[:, :, :], rows[:, 0:3, :], sel[0:H, ds(h, 1)], None, ALU.mult).then_inc(G["rowm"], 1)
                dve.wait_ge(G["nrm"], h + 1)
                STT(qk[:, 0, :], q_h, DK ** -0.5, nrm[:, 0, :], ALU.mult, ALU.mult)
                T_(qk[:, 1, :], k_h, nrm[:, 1, :], ALU.mult).then_inc(G["qk"], 1)
                dve.wait_ge(G["br"], h + 1)
                for c in range(2):
                    S_(e_p[:, c, :], br[:, 0, c * P:(c + 1) * P], gc_t[:, c, ds(h, 1)], 0.0, ALU.subtract, ALU.min)
                S_(e_s[:, :], br[0:NS, 0, SEQ:], gc_t[0:NS, 2, ds(h, 1)], 0.0, ALU.subtract, ALU.min)
                T_(r_t[:, :], v_h[:, 0:P], br[:, 1, 0:P], ALU.mult)
                dve.drain()
                dve.sem_inc(G["e"], 1)
                T_(qdec[:, :], qk[:, 0, P:2 * P], br[:, 2, P:2 * P], ALU.mult)
                dve.wait_ge(G["kss"], h + 1)
                T_(o_add[:, :], bank[6][:, 0:NS], br[:, 2, SEQ:], ALU.mult)
                T_(r_ts[:, :], bank[6][:, NS:2 * NS], br[:, 2, SEQ:], ALU.mult)
                dve.drain()
                T_(r_ts[:, :], v_h[:, SEQ:], r_ts[:, :], ALU.subtract)
                dve.drain()
                T_(r_ts[:, :], r_ts[:, :], br[:, 1, SEQ:], ALU.mult)
                dve.drain()
                dve.sem_inc(G["ra"], 1)
                dve.wait_ge(G["kt"], h + 1)
                for c in range(2):
                    S_(kend[:, c, :], bank[7][:, c * P:(c + 1) * P], ke_t[:, c, ds(h, 1)], None, ALU.mult)
                S_(kend_s[:, :], bank[7][0:NS, 2 * P:3 * P], ke_t[0:NS, 2, ds(h, 1)], None, ALU.mult)
                dve.drain()
                T_(kmask[:, :, :], kend_s[:, :].unsqueeze(1).to_broadcast([NS, DB, P]),
                   cv["bcol"][0:NS, :].unsqueeze(2).to_broadcast([NS, DB, P]), ALU.mult)
                dve.drain()
                dve.sem_inc(G["kend"], 1)
                dve.wait_ge(G["d"], h + 1)
                T_(e_p[:, :, :], e_p[:, :, :], cv["incl"].unsqueeze(1).to_broadcast([P, 2, P]), ALU.mult)
                T_(e_s[:, :], e_s[:, :], smask[0:NS, 0, :], ALU.mult)
                dve.drain()
                dve.wait_ge(G["gram"], h + 1)
                g_p = bank[2][:, :].rearrange("p (c m n) -> p c m n", c=2, m=2)
                T_(qkd_p[:, :, :], g_p[:, :, 0, :], e_p[:, :, :], ALU.mult)
                T_(at_p[:, :, :], g_p[:, :, 1, :], e_p[:, :, :], ALU.mult)
                T_(qkd_s[:, :], bank[3][0:NS, 0:NS], e_s[:, :], ALU.mult)
                T_(at_s[:, :], bank[3][0:NS, NS:2 * NS], e_s[:, :], ALU.mult)
                dve.drain()
                T_(at_p[:, :, :], at_p[:, :, :], br[:, 1, 0:SEQ].rearrange("p (c n) -> p c n", c=2), ALU.mult)
                T_(at_s[:, :], at_s[:, :], br[0:NS, 1, SEQ:], ALU.mult)
                dve.drain()
                T_(tt[:, 0:2, :], at_p[:, :, :], lev[:, 0, :].unsqueeze(1).to_broadcast([P, 2, P]), ALU.mult)
                T_(tt_s[:, 0, :], at_s[:, :], smask[0:NS, 1, :], ALU.mult)
                dve.drain()
                T_(tt[:, 0:2, :], ident.unsqueeze(1).to_broadcast([P, 2, P]), tt[:, 0:2, :], ALU.subtract)
                T_(tt_s[:, 0, :], ident[0:NS, 0:NS], tt_s[:, 0, :], ALU.subtract)
                dve.drain()
                dve.sem_inc(G["t1"], 1)
                for c in range(2):
                    T_(bt_p[:, :, c, :], at_p[:, c, :].unsqueeze(1).to_broadcast([P, LV - 1, P]), lev[:, 1:LV, :], ALU.mult)
                T_(bt_s[:, :], at_s[:, :], smask[0:NS, 2, :], ALU.mult)
                dve.wait_ge(G["t1t"], h + 1)
                CP(tt[:, 2:4, :].rearrange("p c n -> p (c n)"), bank[3][:, 0:2 * P])
                CP(tt_s[:, 1, :], bank[3][0:NS, 2 * P:2 * P + NS])
                dve.drain()
                dve.sem_inc(G["t"], 1)
                for l in range(1, LV):
                    if l == 3:
                        ada2(0, h)
                    dve.wait_ge(G["dt"], h * (LV - 1) + l)
                    w_ = 4 if l < LV - 1 else 2
                    tv = tt[:, 0:w_, :].rearrange("p c n -> p (c n)")
                    T_(tv, tv, bank[5][:, 0:w_ * P], ALU.subtract)
                    if l == 1:
                        T_(tt_s[:, 0, :], tt_s[:, 0, :], bank[6][0:NS, 0:NS], ALU.subtract)
                    dve.drain()
                    dve.sem_inc(G["t"], 1)
                dve.wait_ge(G["sa"], h + 1)
                CP(st_p[:, :], bank[3][:, 0:P])
                dve.drain()
                dve.sem_inc(G["S1"], 1)
                T_(st_out[:, :, :], st_in[:, :, :], br[:, 2, N - DB:N].unsqueeze(2).to_broadcast([P, DB, P]), ALU.mult)
                dve.wait_ge(G["ks"], h + 1)
                T_(r_t[:, :], bank[4][:, 0:P], br[:, 2, P:2 * P], ALU.mult)
                dve.drain()
                T_(r_t[:, :], v_h[:, P:2 * P], r_t[:, :], ALU.subtract)
                dve.drain()
                T_(r_t[:, :], r_t[:, :], br[:, 1, P:2 * P], ALU.mult)
                dve.drain()
                dve.sem_inc(G["rb"], 1)
                for m, bk in enumerate((5, 7)):
                    so = st_out[:, 4 * m:4 * m + 4, :].rearrange("p b n -> p (b n)")
                    T_(so, so, bank[bk][:, :], ALU.add)
                ada2(1, h)
                dve.wait_ge(G["sb"], h + 1)
                STT(st_p[:, :], st_p[:, :], br[:, 2, SEQ - 1:SEQ], bank[3][:, 0:P], ALU.mult, ALU.add)
                CP(o_b[:, 0:SEQ], bank[2][:, 0:SEQ])
                T_(o_b[:, SEQ:], bank[2][:, SEQ:N], o_add[:, :], ALU.add)
                dve.drain()
                dve.sem_inc(G["o"], 1)
                dve.wait_ge(G["on"], h + 1)
                STT(o_b[:, :], o_b[:, :], vec[:, V_GN:V_GN + 1], nrm[:, 0, :], ALU.mult, ALU.mult)
                dve.drain()
                T_(o_b[:, :], o_b[:, :], row(z[:, ds(h, 1), :]), ALU.mult)
                dve.drain()
                CP(row(og_hi[:, ds(h, 1), :]), o_b[:, :])
                dve.drain()
                T_(row(og_lo[:, ds(h, 1), :]), o_b[:, :], row(og_hi[:, ds(h, 1), :]).bitcast(f32), ALU.subtract)
                dve.drain()
                dve.wait_ge(G["spout"], h * 16 + 16)
                dve.wait_ge(G["ssout"], h * 16 + 16)
                dve.sem_inc(G["dve"], 1)

            turned = [(dsa[:, QH + m, :], 0) for m in range(KV)] + [(dsa[:, 12 + m, :], 1) for m in range(4)] + [(ikk[:, :], 1)]
            for n, (t_, kind) in enumerate(turned):
                dve.wait_ge(X["rot"], n + 1)
                T_(rot_t[:, :], bank[2 + n % 2][:, 0:N], rope[:, 2 * kind + 1, :], ALU.mult)
                T_(t_, t_, rope[:, 2 * kind, :], ALU.mult)
                dve.drain()
                T_(t_, t_, rot_t[:, :], ALU.add)
                dve.drain()
                dve.sem_inc(X["rotd"], 1)
            dve.wait_ge(G["sin"], 16 * (H + 1))
            V.memset(vtok_s[:, :], 0.0)
            V.memset(pn_t[:, :], 0.0)
            for m in range(4):
                T_(iqm[:, m, :, :], dsa[:, 12 + m, SEQ:].unsqueeze(1).to_broadcast([P, DB, NS]), maskb, ALU.mult)
            dve.wait_ge(X["load"], 16 * (1 + 3 * DB * (PAST // PAGE)))
            CP(ik_c[:, :, PAST:L_S], ikk[:, SEQ:].rearrange("p (t b) -> p b t", b=DB))
            for m in range(KV):
                CP(kt_c[:, :, m, PAST:L_S], dsa[:, QH + m, SEQ:].rearrange("p (t b) -> p b t", b=DB))
            dve.drain()
            dve.sem_inc(X["newk"], 1)
            dve.wait_ge(X["vtd"], 1)
            for n in range(3 * IH):
                dve.wait_ge(X["rel"], n + 1)
                h_ = n % IH
                if n < 2 * IH:
                    out_, in_, w_ = sc_p[:, n // IH, :], rel[:, n % 2, 0:SEQ], iw_t[:, n // IH, h_:h_ + 1]
                else:
                    out_, in_, w_ = sc_s[:, :], rel[0:NS, n % 2, :], iw_s[:, h_:h_ + 1]
                if h_ == 0:
                    S_(out_, in_, w_, None, ALU.mult)
                else:
                    STT(out_, in_, w_, out_, ALU.mult, ALU.add)
                dve.drain()
                dve.sem_inc(X["acc"], 1)
            T_(sc_p[:, :, :], sc_p[:, :, :], causal, ALU.min)
            T_(sc_s[:, :], sc_s[:, :], causal_s[0:NS, :], ALU.min)
            dve.drain()
            sets = [(sc_p[:, 0, :], wk_p[:, 0, :], top8[:, 0, :]), (sc_p[:, 1, :], wk_p[:, 1, :], top8[:, 1, :]),
                    (sc_s[:, :], wk_s[:, :], top8[0:NS, 2, :])]
            for r in range(TOPK_P // 8):
                for s_, w_, t8 in sets:
                    V.max(out=t8, in_=w_ if r else s_)
                dve.drain()
                for s_, w_, t8 in sets:
                    V.match_replace(out=w_, in_to_replace=t8, in_values=w_ if r else s_, imm_value=NEG_TAKEN)
                dve.drain()
            s_, w_, t8 = sets[2]
            V.max(out=t8, in_=w_)
            dve.drain()
            V.memset(t8[:, TOPK_S - TOPK_P:], -NEG_TAKEN)
            dve.drain()
            V.match_replace(out=w_, in_to_replace=t8, in_values=w_, imm_value=NEG_TAKEN)
            dve.drain()
            T_(wk_p[:, :, :], wk_p[:, :, :], sc_p[:, :, :], ALU.not_equal)
            T_(wk_s[:, :], wk_s[:, :], sc_s[:, :], ALU.not_equal)
            dve.drain()
            S_(sc_p[:, :, :], causal, 0.0, None, ALU.is_gt)
            S_(sc_s[:, :], causal_s[0:NS, :], 0.0, None, ALU.is_gt)
            dve.drain()
            T_(wk_p[:, :, :], wk_p[:, :, :], sc_p[:, :, :], ALU.mult)
            T_(wk_s[:, :], wk_s[:, :], sc_s[:, :], ALU.mult)
            dve.drain()
            S_(bias_p[:, 0:P], wk_p[:, 0, 0:P], BIG, -BIG, ALU.mult, ALU.add)
            S_(bias_p[:, P:], wk_p[:, 1, :], BIG, -BIG, ALU.mult, ALU.add)
            S_(bias_s[:, :], wk_s[:, :], BIG, -BIG, ALU.mult, ALU.add)
            dve.drain()

            with dve.Fori(0, QH) as h:
                q_h = row(dsa[:, ds(h, 1), :])
                dve.wait_ge(X["rotq"], h + 1)
                T_(rtmp[:, :], bank[2][:, 0:N], rope[:, 1, :], ALU.mult)
                T_(q_r[:, :], q_h, rope[:, 0, :], ALU.mult)
                dve.drain()
                T_(q_r[:, :], q_r[:, :], rtmp[:, :], ALU.add)
                dve.drain()
                T_(q_m[:, :, :], q_r[:, SEQ:].unsqueeze(1).to_broadcast([P, DB, NS]), maskb, ALU.mult)
                dve.drain()
                dve.sem_inc(X["q"], 1)
                dve.wait_ge(X["s"], h + 1)
                T_(s_p[:, :], bank[3][:, 0:P + SEQ], bias_p[:, :], ALU.add)
                T_(s_s[:, :], bank[4][0:NS, 0:L_S], bias_s[:, :], ALU.add)
                dve.drain()
                V.tensor_reduce(stat[:, 2, 0:1], s_p[:, 0:P], AX.X, ALU.max)
                V.tensor_reduce(stat[:, 2, 1:2], s_p[:, P:], AX.X, ALU.max)
                V.tensor_reduce(stat[0:NS, 2, 2:3], s_s[:, :], AX.X, ALU.max)
                dve.drain()
                S_(stat[:, 0, 0:2], stat[:, 2, 0:2], -(HD ** -0.5), None, ALU.mult)
                S_(stat[0:NS, 0, 2:3], stat[0:NS, 2, 2:3], -(HD ** -0.5), None, ALU.mult)
                dve.drain()
                dve.sem_inc(X["m"], 1)
                ada2(0, h + H)
                dve.wait_ge(X["p"], h + 1)
                T_(pn[:, :].rearrange("p (t b) -> p t b", b=DB), s_s[:, PAST:].unsqueeze(2).to_broadcast([NS, TS, DB]),
                   smask[0:NS, 3, :].rearrange("p (t b) -> p t b", b=DB), ALU.mult)
                V.reciprocal(stat[:, 3, 0:2], stat[:, 1, 0:2])
                V.reciprocal(stat[0:NS, 3, 2:3], stat[0:NS, 1, 2:3])
                dve.drain()
                dve.sem_inc(X["pn"], 1)
                dve.wait_ge(X["pt"], h + 1)
                for g in range(2):
                    T_(p_tm[:, g, :, :], bank[6][:, g * NS:(g + 1) * NS].unsqueeze(1).to_broadcast([P, DB, NS]), maskb, ALU.mult)
                CP(pn_t[0:NS, :], bank[6][0:NS, 2 * NS:3 * NS])
                dve.drain()
                dve.sem_inc(X["ptm"], 1)
                dve.wait_ge(X["o"], h + 1)
                for c in range(2):
                    S_(o_n[:, c, :], bank[7][:, c * P:(c + 1) * P], stat[:, 3, c:c + 1], None, ALU.mult)
                S_(o_ns[:, :], bank[2][0:NS, 0:P], stat[0:NS, 3, 2:3], None, ALU.mult)
                dve.drain()
                dve.sem_inc(X["on"], 1)
                ada2(1, h + H)
                dve.wait_ge(X["ot"], h + 1)
                CP(row(do_hi[:, ds(h, 1), :]), bank[3][:, 0:N])
                dve.drain()
                T_(row(do_lo[:, ds(h, 1), :]), bank[3][:, 0:N], row(do_hi[:, ds(h, 1), :]).bitcast(f32), ALU.subtract)
                dve.drain()
                dve.sem_inc(X["end"], 1)

            dve.wait_ge(out_done, 16 * 5)
            with dve.Fori(0, 4) as i:
                for g0 in range(2):
                    for which in range(2):
                        bs, cnt = grp("out", 4, 4 * g0 + 2 + which, i, 8)
                        dve.wait_ge(g_sig, (i * 2 + g0) * 2 + which + 1)
                        dve.wait_ge(grp_ready[bs], cnt + 1)
                        for c in range(CT):
                            T_(mt[:, c, :] if which == 0 else sg[:, 1, c, :], bank[2 * bs + c][:, 0:N], sg[:, which, c, :], ALU.mult)
                        dve.drain()
                        dve.sem_inc(grp_free[bs], 1)
                    for c in range(CT):
                        T_(mt[:, c, :], mt[:, c, :], sg[:, 1, c, :], ALU.add)
                    dve.drain()
                    for c in range(CT):
                        CP(row(mix[:, ds(i * 4 + 2 * g0 + c, 1), :]), mt[:, c, :])
                    dve.drain()
                    for c in range(CT):
                        k = i * 4 + 2 * g0 + c
                        T_(row(mix_lo[:, ds(k, 1), :]), mt[:, c, :], row(mix[:, ds(k, 1), :]).bitcast(f32), ALU.subtract)
                    dve.drain()
                    dve.sem_inc(mix_done, 1)

            def residual(psum, t, gate_tile, tmp):
                xt, gt = row(x[:, ds(t, 1), :]), row(ada[:, ds(gate_tile, 1), :])
                STT(xt[:, 0:SEQ], psum[:, 0:SEQ], gt[:, 0:1], xt[:, 0:SEQ], ALU.mult, ALU.add)
                T_(tmp.rearrange("p (t b) -> p t b", b=DB), psum[:, SEQ:N].rearrange("p (t b) -> p t b", b=DB),
                   gt[:, 1:NC].unsqueeze(1).to_broadcast([P, TS, DB]), ALU.mult)
                dve.drain()
                return T_(xt[:, SEQ:], xt[:, SEQ:], tmp, ALU.add)

            dve.wait_ge(x_back, 16)
            with dve.Fori(0, 2) as i:
                for g in range(4):
                    bs, cnt = grp("wo", 4, g, i, 4)
                    dve.wait_ge(grp_ready[bs], cnt + 1)
                    for c in range(CT):
                        t = i * 8 + 2 * g + c
                        residual(bank[2 * bs + c], t, t + 2 * KT, mt[:, c, 0:NS]).then_inc(x_done, 1)
                    dve.drain()
                    dve.sem_inc(grp_free[bs], 1)
            scale_shift(1, 1)
            dve.drain()
            V.memset(fin[:, :, 0:FCONV - 1], 0.0)
            dve.wait_ge(const_in, 80)

            def ffn_gate(g, idx, half, i, per):
                bs, cnt = grp("ffn", 4, g, idx, per)
                dve.wait_ge(grp_ready[bs], cnt + 1)
                for c in range(CT):
                    t = i * FC + 2 * half + c
                    conv(bank[2 * bs + c], c, fin, fy, fst, t, V_WF, FCONV, HI_F, 2 * FT, fpt)
                    dve.drain()
                    dve.sem_inc(conv_y, 1)
                dve.sem_inc(grp_free[bs], 1)

            def ffn_val(g, idx, half, i, per):
                bs, cnt = grp("ffn", 4, g, idx, per)
                dve.wait_ge(grp_ready[bs], cnt + 1)
                for c in range(CT):
                    t = i * FC + 2 * half + c
                    dve.wait_ge(sil_done, t + 1)
                    conv(bank[2 * bs + c], c, fin, fy, fst, t + FT, V_WF, FCONV, HI_F, 2 * FT, fpt)
                    dve.drain()
                    STT(act_f[:, c, :], fy[:, c, :], vec[:, ds(t + FT + V_BF, 1)], fsil[:, c, :], ALU.add, ALU.mult)
                dve.drain()
                dve.sem_inc(grp_free[bs], 1)
                dst = (i & 1) * FC + 2 * half
                ah = act_hi[:, :, :, :].rearrange("p a c n -> p (a c) n")[:, ds(dst, CT), :]
                al = act_lo[:, :, :, :].rearrange("p a c n -> p (a c) n")[:, ds(dst, CT), :]
                CP(ah, act_f[:, :, :])
                dve.drain()
                T_(al, act_f[:, :, :], ah.bitcast(f32), ALU.subtract)
                dve.drain()
                dve.sem_inc(act_ready, 1)

            def ffn_down(g, idx, per):
                for m in range(KT // CT):
                    bs, cnt = grp("ffn", 4, g + m, idx, per)
                    dve.wait_ge(grp_ready[bs], cnt + 1)
                    for c in range(CT):
                        residual(bank[2 * bs + c], 2 * m + c, 2 * m + c + 5 * KT, dtmp[:, :])
                        dve.drain()
                        dve.sem_inc(down_done, 1)
                    dve.sem_inc(grp_free[bs], 1)

            ffn_gate(0, 0, 0, 0, 0)
            ffn_val(1, 0, 0, 0, 0)
            ffn_gate(2, 0, 1, 0, 0)
            ffn_val(3, 0, 1, 0, 0)
            with dve.Fori(0, NCH - 1) as i:
                ffn_gate(4, i, 0, i + 1, 12)
                ffn_val(5, i, 0, i + 1, 12)
                ffn_down(6, i, 12)
                ffn_gate(14, i, 1, i + 1, 12)
                ffn_val(15, i, 1, i + 1, 12)
            ffn_down(4 + 12 * (NCH - 1), 0, 0)

            dve.wait_ge(rs_ready, 3)
            with dve.Fori(0, KT // 2) as i:
                for s_ in range(2):
                    k = i * 2 + s_
                    xt = row(x[:, ds(k, 1), :])
                    last = STT(xt, xt, vec[:, ds(k + V_GF, 1)], rsb[:, :], ALU.mult, ALU.mult)
                dve.drain()
                dve.sem_inc(y_ready, 1)

        @block.tensor
        def _(pe):
            MM = nc.tensor.matmul
            row = lambda a: a.rearrange("p k n -> p (k n)")

            def tr(out, in_, n):
                return nc.tensor.transpose(out, in_, ident[0:n, 0:n])

            def cond(name, g, j0, sets, i=0, per_g=0, per_j=0, only=None):
                bs, cnt = grp(name, sets, g, i, per_g)
                if only is None or only == 0:
                    pe.wait_ge(grp_free[bs], cnt + 1)
                for s_ in range(KT // KS) if only is None else (only,):
                    r, use = raw_at(name, j0 + s_, i, per_j)
                    pe.wait_ge(raw_in[r], use * 16 + 16)
                    for k in range(KS):
                        for c in range(CT):
                            kk = s_ * KS + k
                            last = MM(bank[2 * bs + c][:, 0:NC], raw[:, r, k, c * P:(c + 1) * P], cact[:, kk, :],
                                      start=(kk == 0), stop=(kk == KT - 1))
                    last.then_inc(raw_free[r], 1)
                    if s_ == KT // KS - 1:
                        pe.wait_ge(raw_free[r], use + 2)
                        pe.sem_inc(grp_ready[bs], 1)

            def slot(name, j, hi_of, lo_of, banks, first, last_, i=0, per=0, done=None):
                q, cnt = split_at(name, j, i, per)
                pe.wait_ge(hi_ready, cnt + 1)
                for k in range(KS):
                    for c in range(CT):
                        w_ = w_hi[:, q, k, c * P:(c + 1) * P]
                        MM(banks[c][:, 0:N], w_, hi_of(k), start=(first and k == 0), stop=False)
                        MM(banks[c][:, 0:N], w_, lo_of(k), start=False, stop=False)
                pe.wait_ge(lo_ready, cnt + 1)
                for k in range(KS):
                    for c in range(CT):
                        ins = MM(banks[c][:, 0:N], w_lo[:, q, k, c * P:(c + 1) * P], hi_of(k),
                                 start=False, stop=(last_ and k == KS - 1))
                if done is not None:
                    ins.then_inc(done, 1)
                return ins

            def group(name, sets, g, j0, nslots, hi_t, lo_t, i=0, per_g=0, per_j=0, k0=0):
                bs, cnt = grp(name, sets, g, i, per_g)
                banks = (bank[2 * bs], bank[2 * bs + 1])
                pe.wait_ge(grp_free[bs], cnt + 1)
                for s_ in range(nslots):
                    ins = slot(name, j0 + s_, lambda k: hi_t(s_ * KS + k), lambda k: lo_t(s_ * KS + k), banks,
                               s_ == 0, s_ == nslots - 1, i, per_j, ring_free)
                q, c_ = split_at(name, j0 + nslots - 1, i, per_j)
                pe.wait_ge(ring_free, c_ + 1 + RING)
                pe.sem_inc(grp_ready[bs], 1)

            hh, hl = (lambda k: h_hi[:, k, :]), (lambda k: h_lo[:, k, :])

            def norm_sum_all(n):
                for s_ in range(KT):
                    pe.wait_ge(sq_ready, n * KT + s_ + 1)
                    ins = MM(bank[7][:, 0:N], ones, sq[:, s_ % 2, :], start=(s_ == 0), stop=(s_ == KT - 1))
                    ins.then_inc(sq_used, 1)
                pe.wait_ge(sq_used, (n + 1) * KT + 2)
                pe.sem_inc(ssq_ready, 1)

            pe.wait_ge(const_in, 48)
            norm_sum_all(0)
            pe.wait_ge(c_ready, 1)
            with pe.Fori(0, KT // CT) as i:
                for g in range(2):
                    cond("ada1", g, 4 * g, 2, i, 2, 8)
            pe.wait_ge(h_lo_ready, KT + 2)
            pe.wait_ge(h_hi_ready, KT)
            with pe.Fori(0, 6) as i:
                for g in range(2):
                    group("qkv", 2, g, 4 * g, 4, hh, hl, i, 2, 8)
            with pe.Fori(0, 2) as i:
                for g in range(2):
                    group("z", 2, g, 4 * g, 4, hh, hl, i, 2, 8)
            with pe.Fori(0, 4) as i:
                for g in range(2):
                    group("dsa", 2, g, 4 * g, 4, hh, hl, i, 2, 8)
            group("small", 1, 0, 0, 4, hh, hl)

            pe.wait_ge(row_act, 2)
            for m, bk in ((0, 2), (3, 3)):
                for c in range(3):
                    w_ = P if c < 2 else NS
                    ins = tr(bank[bk][0:w_, c * H:(c + 1) * H], rows[:, m, c * P:c * P + w_], H)
            ins.then_inc(row_tr, 1)

            with pe.Fori(0, H) as h:
                def fill(n):
                    cond("ada2", n // 4, 4 * (n // 4), 1, h, 2, 8, only=n % 4)
                pe.wait_ge(G["rowm"], h + 1)
                pe.wait_ge(G["sq"], h + 1)
                MM(bank[2][:, 0:N], ones, sqb[:, 0, :], start=True, stop=True)
                MM(bank[3][:, 0:N], ones, sqb[:, 1, :], start=True, stop=True).then_inc(G["ssq"], 1)
                for m in range(3):
                    ins = MM(bank[4 + m][:, 0:N], ones[0:H, :], rows_m[:, m, :], start=True, stop=True)
                ins.then_inc(G["bc"], 1)
                fill(0)
                pe.wait_ge(G["qk"], h + 1)
                for c in range(2):
                    MM(bank[2][:, c * 2 * P:(c + 1) * 2 * P].rearrange("p (m n) -> p m n", m=2), qk[:, 1, c * P:(c + 1) * P],
                       qk[:, :, c * P:(c + 1) * P], start=True, stop=True)
                MM(bank[3][0:NS, 0:2 * NS].rearrange("p (m n) -> p m n", m=2), qk[:, 1, SEQ:], qk[:, :, SEQ:],
                   start=True, stop=True).then_inc(G["gram"], 1)
                for c in range(2):
                    tr(bank[7][:, c * P:(c + 1) * P], qk[:, 1, c * P:(c + 1) * P], P)
                tr(bank[7][0:NS, 2 * P:3 * P], qk[:, 1, SEQ:], P).then_inc(G["kt"], 1)
                pe.wait_ge(G["sin"], h * 16 + 16)
                pe.wait_ge(G["br"], h + 1)
                for b in range(DB):
                    v2 = lambda a: a.rearrange("p m (t b) -> p m t b", b=DB)[:, :, :, b]
                    ins = MM(v2(bank[6][:, 0:2 * NS].rearrange("p (m n) -> p m n", m=2)), st_in[:, b, :], v2(qk[:, :, SEQ:]),
                             start=True, stop=True)
                ins.then_inc(G["kss"], 1)
                fill(1)
                pe.wait_ge(G["t1"], h + 1)
                for c in range(2):
                    tr(bank[3][:, c * P:(c + 1) * P], tt[:, c, :], P)
                tr(bank[3][0:NS, 2 * P:2 * P + NS], tt_s[:, 0, :], NS).then_inc(G["t1t"], 1)
                pe.wait_ge(G["ra"], h + 1)
                for l in range(1, LV):
                    pe.wait_ge(G["t"], h * LV + l)
                    for c in range(2):
                        if l == 1 and c == 1:
                            MM(bank[4][0:NS, 2 * P:2 * P + NS], bt_s[:, :], tt_s[:, 1, :], start=True, stop=True)
                        ins = MM(bank[4][:, c * P:(c + 1) * P], bt_p[:, l - 1, c, :], tt[:, 2 + c, :], start=True, stop=True)
                    ins.then_inc(G["x"], 1)
                    fill(l + 1)
                    pe.wait_ge(G["xs"], h * (LV - 1) + l)
                    for c in range(2):
                        if l == 1 and c == 1:
                            MM(bank[6][0:NS, 0:NS], x_s[:, :], tt_s[:, 0, :], start=True, stop=True)
                        ins = MM(bank[5][:, c * P:(c + 1) * P], x_p[:, c, :], tt[:, c, :], start=True, stop=True)
                    if l < LV - 1:
                        for c in range(2):
                            ins = MM(bank[5][:, (2 + c) * P:(3 + c) * P], tt[:, c, :], x_p[:, c, :], start=True, stop=True)
                    ins.then_inc(G["dt"], 1)
                pe.wait_ge(G["t"], h * LV + LV)
                tr(bank[6][0:NS, P:2 * P], r_ts[:, :], P)
                tr(bank[6][:, 0:P], r_t[:, :], P).then_inc(G["rt"], 1)
                pe.wait_ge(G["rs"], h * 2 + 1)
                MM(bank[6][:, 0:P], tt[:, 0, :], r_p[:, :], start=True, stop=True)
                MM(bank[6][0:NS, P:2 * P], tt_s[:, 0, :], r_s[:, :], start=True, stop=True).then_inc(G["u"], 1)
                pe.wait_ge(G["kend"], h + 1)
                pe.wait_ge(G["us"], h * 2 + 1)
                MM(bank[3][:, 0:P], kend[:, 0, :], u_p[:, :], start=True, stop=True)
                MM(bank[2][:, 0:P], u_p[:, :], qkd_p[:, 0, :], start=True, stop=True)
                MM(bank[2][:, SEQ:N], u_s[:, :], qkd_s[:, :], start=True, stop=True)
                for b in range(DB):
                    ins = MM(bank[5 if b < 4 else 7][:, (b % 4) * P:(b % 4 + 1) * P], kmask[:, b, :], u_s[:, :], start=True, stop=True)
                ins.then_inc(G["sa"], 1)
                pe.wait_ge(G["S1"], h + 1)
                MM(bank[4][:, 0:P], st_p[:, :], qk[:, 1, P:2 * P], start=True, stop=True).then_inc(G["ks"], 1)
                pe.wait_ge(G["rb"], h + 1)
                tr(bank[6][:, 0:P], r_t[:, :], P).then_inc(G["rt"], 1)
                pe.wait_ge(G["rs"], h * 2 + 2)
                MM(bank[6][:, 0:P], tt[:, 1, :], r_p[:, :], start=True, stop=True).then_inc(G["u"], 1)
                pe.wait_ge(G["us"], h * 2 + 2)
                MM(bank[2][:, P:2 * P], st_p[:, :], qdec[:, :], start=True, stop=False)
                MM(bank[2][:, P:2 * P], u_p[:, :], qkd_p[:, 1, :], start=False, stop=True)
                MM(bank[3][:, 0:P], kend[:, 1, :], u_p[:, :], start=True, stop=True).then_inc(G["sb"], 1)
                pe.wait_ge(G["osq"], h + 1)
                MM(bank[7][:, 0:N], ones, sqb[:, 0, :], start=True, stop=True).then_inc(G["oss"], 1)
                pe.wait_ge(G["dve"], h + 1)

            turned = [(dsa[:, QH + m, :], 0) for m in range(KV)] + [(dsa[:, 12 + m, :], 1) for m in range(4)] + [(ikk[:, :], 1)]
            for n, (t_, kind) in enumerate(turned):
                if n >= 2:
                    pe.wait_ge(X["rotd"], n - 1)
                MM(bank[2 + n % 2][:, 0:N], rotm[:, kind, :], t_, start=True, stop=True).then_inc(X["rot"], 1)
            for c in range(2):
                for m in range(KV):
                    tr(bank[4][:, (c * KV + m) * P:(c * KV + m + 1) * P], dsa[:, QH + KV + m, c * P:(c + 1) * P], P)
            for m in range(KV):
                tr(bank[5][0:NS, m * P:(m + 1) * P], dsa[:, QH + KV + m, SEQ:], P)
            for c in range(3):
                w_ = P if c < 2 else NS
                ins = tr(bank[6][0:w_, c * IH:(c + 1) * IH], sm_iw[:, c * P:c * P + w_], IH)
            ins.then_inc(X["vt"], 1)
            pe.wait_ge(X["rotd"], len(turned))
            for n in range(3 * IH):
                if n >= 2:
                    pe.wait_ge(X["rel"], n - 1)
                h_ = n % IH
                pr = slice(ID * (h_ % 2), ID * (h_ % 2) + ID)
                if n < 2 * IH:
                    c = n // IH
                    ins = MM(bank[2 + n % 2][:, 0:SEQ], dsa[pr, 12 + h_ // 2, c * P:(c + 1) * P], ikk[pr, 0:SEQ], start=True, stop=True)
                else:
                    if n == 2 * IH:
                        pe.wait_ge(X["newk"], 1)
                    for b in range(DB):
                        ins = MM(bank[2 + n % 2][0:NS, 0:L_S], iqm[pr, h_ // 2, b, :], ik_c[pr, b, :], start=(b == 0), stop=(b == DB - 1))
                ins.then_inc(X["idx"], 1)
            pe.wait_ge(X["rel"], 3 * IH)
            with pe.Fori(0, QH) as h:
                def fill(n):
                    cond("ada2", 2 * H + n // 4, 8 * H + 4 * (n // 4), 1, h, 2, 8, only=n % 4)
                kv = (h >> 2).with_bounds(min_val=0, max_val=KV - 1)
                MM(bank[2][:, 0:N], rotm[:, 0, :], row(dsa[:, ds(h, 1), :]), start=True, stop=True).then_inc(X["rotq"], 1)
                fill(0)
                fill(1)
                pe.wait_ge(X["q"], h + 1)
                kt_h = row(dsa[:, ds(kv + QH, 1), :])
                MM(bank[3][:, 0:P], q_r[:, 0:P], kt_h[:, 0:P], start=True, stop=True)
                MM(bank[3][:, P:P + SEQ], q_r[:, P:2 * P], kt_h[:, 0:SEQ], start=True, stop=True)
                for b in range(DB):
                    ins = MM(bank[4][0:NS, 0:L_S], q_m[:, b, :], row(kt_c[:, b, ds(kv, 1), :]), start=(b == 0), stop=(b == DB - 1))
                ins.then_inc(X["s"], 1)
                fill(2)
                fill(3)
                fill(4)
                pe.wait_ge(X["p"], h + 1)
                pe.wait_ge(X["pn"], h + 1)
                tr(bank[5][:, 0:P], s_p[:, 0:P], P)
                tr(bank[5][:, P:2 * P], s_p[:, P:2 * P], P)
                tr(bank[5][:, 2 * P:3 * P], s_p[:, 2 * P:3 * P], P)
                for g in range(2):
                    tr(bank[6][:, g * NS:(g + 1) * NS], s_s[:, g * PAGE:(g + 1) * PAGE], NS)
                tr(bank[6][0:NS, 2 * NS:3 * NS], pn[:, :], NS).then_inc(X["pt"], 1)
                fill(5)
                pe.wait_ge(X["pts"], h + 1)
                pe.wait_ge(X["ptm"], h + 1)
                vt = lambda c: vtok[:, c, ds(kv * HD, HD)]
                MM(bank[7][:, 0:P], p_t[:, 0, :], vt(0), start=True, stop=True)
                MM(bank[7][:, P:2 * P], p_t[:, 1, :], vt(0), start=True, stop=False)
                MM(bank[7][:, P:2 * P], p_t[:, 2, :], vt(1), start=False, stop=True)
                for g in range(2):
                    for b in range(DB):
                        MM(bank[2][0:NS, 0:P], p_tm[:, g, b, :], v_c[:, b, g, ds(kv * HD, HD)], start=(g == 0 and b == 0), stop=False)
                MM(bank[2][0:NS, 0:P], pn_t[:, :], vtok_s[:, ds(kv * HD, HD)], start=False, stop=True).then_inc(X["o"], 1)
                fill(6)
                fill(7)
                pe.wait_ge(X["on"], h + 1)
                for c in range(2):
                    tr(bank[3][:, c * P:(c + 1) * P], o_n[:, c, :], P)
                tr(bank[3][:, SEQ:N], o_ns[:, :], NS).then_inc(X["ot"], 1)
                pe.wait_ge(X["end"], h + 1)

            oh, ol = (lambda k: og_hi[:, k, :]), (lambda k: og_lo[:, k, :])
            dh, dl = (lambda k: do_hi[:, k, :]), (lambda k: do_lo[:, k, :])
            with pe.Fori(0, 4) as i:
                for g0 in range(2):
                    j = 12 * g0
                    group("out", 4, 4 * g0, j, 4, hh, hl, i, 8, 24)
                    group("out", 4, 4 * g0 + 1, j + 4, 4, hh, hl, i, 8, 24)
                    group("out", 4, 4 * g0 + 2, j + 8, 2, oh, ol, i, 8, 24)
                    group("out", 4, 4 * g0 + 3, j + 10, 2, dh, dl, i, 8, 24)
            pe.wait_ge(mix_done, KT // CT + 1)
            mh, ml = (lambda k: mix[:, k, :]), (lambda k: mix_lo[:, k, :])
            with pe.Fori(0, 2) as i:
                for g in range(4):
                    group("wo", 4, g, 4 * g, 4, mh, ml, i, 4, 16)
            norm_sum_all(1)
            pe.wait_ge(h_lo_ready, 2 * KT + 2)
            pe.wait_ge(h_hi_ready, 2 * KT)

            def down(g, j, chunk, i, per_g, per_j):
                pe.wait_ge(act_ready, chunk * 2 + 2)
                par = (chunk & 1) * FC
                ah = act_hi[:, :, :, :].rearrange("p a c n -> p (a c) n")
                al = act_lo[:, :, :, :].rearrange("p a c n -> p (a c) n")
                for m in range(KT // CT):
                    group("ffn", 4, g + m, j + m, 1, lambda k: row(ah[:, ds(par + k, 1), :]), lambda k: row(al[:, ds(par + k, 1), :]),
                          i, per_g, per_j)

            for g in range(4):
                group("ffn", 4, g, 4 * g, 4, hh, hl)
            with pe.Fori(0, NCH - 1) as i:
                group("ffn", 4, 4, 16, 4, hh, hl, i, 12, 24)
                group("ffn", 4, 5, 20, 4, hh, hl, i, 12, 24)
                down(6, 24, i, i, 12, 24)
                group("ffn", 4, 14, 32, 4, hh, hl, i, 12, 24)
                group("ffn", 4, 15, 36, 4, hh, hl, i, 12, 24)
            down(4 + 12 * (NCH - 1), 16 + 24 * (NCH - 1), NCH - 1, 0, 0, 0)
            norm_sum_all(2)


def slots_of(w, tiles):
    k, c = w.shape
    a = w.reshape(k // (KS * P), KS, P, c // (CT * P), CT * P)
    return a.transpose(3, 0, 2, 1, 4).reshape(c // (CT * P), k // (KS * P), P, SLOT)


def feature_major(a):
    t, f = a.shape
    return np.ascontiguousarray(a.reshape(t, f // P, P).transpose(2, 1, 0))


def columns(v):
    return v.reshape(-1, P).T


def kernel(**inputs):
    import concourse.bacc as bacc
    from concourse.bass_utils import run_bass_kernel_spmd

    I = {k: np.asarray(v) for k, v in inputs.items()}
    w_in = I["w_in"][0]
    cuts = np.cumsum([QKV_T * P, Z_T * P, H, H, QH * HD, KV * HD, KV * HD, IH * ID, ID, IH, D_MODEL, D_MODEL])
    qkv_w, z_w, a_w, b_w, dq_w, dk_w, dv_w, iq_w, ik_w, iw_w, gg_w, gd_w = np.split(w_in, cuts[:-1], axis=1)
    pad = lambda w, n: np.concatenate([w, np.zeros((D_MODEL, n - w.shape[1]), w.dtype)], 1)
    small = np.concatenate([ik_w, ik_w, pad(a_w, 32), pad(b_w, 32), pad(iw_w, 64)], 1)
    parts = {}
    flat = lambda a: a.reshape(-1, P, SLOT)
    ada_s = slots_of(I["w_ada"][0], None)
    half = 2 * KT // CT
    parts["ada1"], parts["ada2"] = flat(ada_s[:half]), flat(ada_s[half:])
    parts["qkv"], parts["z"] = flat(slots_of(qkv_w, None)), flat(slots_of(z_w, None))
    parts["dsa"] = flat(slots_of(np.concatenate([dq_w, dk_w, dv_w, iq_w], 1), None))
    parts["small"] = flat(slots_of(small, None))
    parts["out"] = flat(np.concatenate([slots_of(gg_w, None), slots_of(gd_w, None),
                                        slots_of(I["w_gdn_out"][0], None), slots_of(I["w_dsa_out"][0], None)], 1))
    parts["wo"] = flat(slots_of(I["w_o"][0], None))
    up, dn = slots_of(I["w_up"][0], None), slots_of(I["w_down"][0], None)
    seq = []
    for i in range(NCH):
        g0, v0 = up[2 * i], up[FT // 2 + 2 * i]
        g1, v1 = up[2 * i + 1], up[FT // 2 + 2 * i + 1]
        seq += [g0, v0] + ([dn[:, i - 1]] if i else []) + [g1, v1]
    seq.append(dn[:, NCH - 1])
    parts["ffn"] = np.concatenate(seq)
    stream = np.concatenate([parts[n] for n, _, _ in PHASES])
    assert stream.shape == (NSLOTS, P, SLOT)

    time_major = lambda a: a.transpose(1, 0, 2).reshape(-1, a.shape[-1])
    c = constants()
    A = {
        "stream": stream,
        "x": feature_major(np.concatenate([I["x_prompt"][0], time_major(I["x_sample"])])).reshape(P, -1),
        "c": feature_major(np.concatenate([I["c_prompt"], I["c_sample"]])).reshape(P, -1),
        "consts": np.concatenate([c[n].reshape(P, -1) for n in CONST_SIZE], 1),
        "vec": np.concatenate([columns(I["b_ada"][0]), columns(I["g_norm1"][0]), columns(I["g_norm2"][0]), columns(I["g_final"]),
                               columns(I["w_gdn_conv"][0]), columns(I["w_ffn_conv"][0]), columns(I["b_ffn_conv"][0]),
                               columns(I["g_gdn_norm"][0])], 1),
        "heads_v": np.stack([I["a_log"][0], I["dt_bias"][0]], 1),
        "ptab": I["page_table"].reshape(1, -1),
        "gdn_hist": feature_major(time_major(I["state_gdn_conv"][0])).reshape(P, -1),
        "ffn_hist": feature_major(time_major(I["state_ffn_conv"][0])).reshape(P, -1),
        "state": I["state_gdn"][0].transpose(1, 2, 0, 3).reshape(H, DK, DB * P),
        "ck": I["cache_k"][0].transpose(0, 3, 2, 1).reshape(NPOOL, HD, KV * PAGE),
        "cv": I["cache_v"][0].reshape(NPOOL, PAGE, KV * HD),
        "cik": np.concatenate([I["cache_idx_k"][0].transpose(0, 2, 1)] * 2, 1),
    }
    outs = {"y": (P, KT * N), "k": (P, KV * N), "v": (P, KV * N), "ik": (ID, N), "state_p": (H, DK, P),
            "state_s": (H, DK, DB * P), "gdn_tail_p": (P, QKV_T * (CONV - 1)), "gdn_tail_s": (P, QKV_T * HI_S),
            "ffn_tail_p": (P, 2 * FT * (FCONV - 1)), "ffn_tail_s": (P, 2 * FT * HI_F)}
    nc = bacc.Bacc("TRN2", target_bir_lowering=False, num_devices=1)
    arrays, aps, oaps = {}, {}, {}
    for name, a in A.items():
        a = np.ascontiguousarray(a)
        arrays[f"in_{name}"] = a
        aps[name] = nc.dram_tensor(f"in_{name}", a.shape, mybir.dt.from_np(a.dtype), kind="ExternalInput").ap()
    for name, shape in outs.items():
        oaps[name] = nc.dram_tensor(f"out_{name}", shape, mybir.dt.float32, kind="ExternalOutput").ap()
    decoder_step(nc, aps, oaps)
    r = run_bass_kernel_spmd(nc, [arrays], core_ids=[0])
    o = {name: r.results[0][f"out_{name}"] for name in outs}

    def tokens(a, tiles):
        return a.reshape(-1, tiles, N).transpose(2, 1, 0).reshape(N, -1)

    def split(a):
        return a[:SEQ], a[SEQ:].reshape(TS, DB, -1).transpose(1, 0, 2)

    def tails(a, n_cols):
        t = a.reshape(P, -1, n_cols)
        return t.transpose(2, 1, 0).reshape(n_cols, -1)

    yp, ys = split(tokens(o["y"], KT))
    kp, ks = split(tokens(o["k"], KV))
    vp, vs = split(tokens(o["v"], KV))
    ip, isa = split(tokens(o["ik"], 1))
    gs = tails(o["gdn_tail_s"], HI_S).reshape(CONV - 1, DB, -1).transpose(1, 0, 2)
    fs = tails(o["ffn_tail_s"], HI_F).reshape(FCONV - 1, DB, -1).transpose(1, 0, 2)
    ss = o["state_s"].reshape(H, DK, DB, P).transpose(2, 0, 1, 3)
    c_ = np.ascontiguousarray
    return (c_(yp[None]), c_(ys),
            c_(kp.reshape(1, 1, SEQ, KV, HD)), c_(vp.reshape(1, 1, SEQ, KV, HD)), c_(ip[None, None]),
            c_(o["state_p"][None, None]), c_(tails(o["gdn_tail_p"], CONV - 1)[None, None]),
            c_(tails(o["ffn_tail_p"], FCONV - 1)[None, None]),
            c_(ks.reshape(1, DB, TS, KV, HD)), c_(vs.reshape(1, DB, TS, KV, HD)), c_(isa[None]),
            c_(ss[None]), c_(gs[None]), c_(fs[None]))
```

```python
from contextlib import ExitStack

import numpy as np
import concourse.bass as bass
from concourse import mybir

P = 128
D_MODEL, SEQ, DB, TS = 2048, 256, 8, 4
PAGE, PAST, NPOOL = 128, 256, 20
H, DK, CONV = 8, 128, 4
QH, KV, HD = 8, 2, 128
IH, ID = 8, 64
D_FF, FCONV = 5632, 3
ROPE_THETA, EPS = 500000.0, 1e-6
NS = DB * TS
N = SEQ + NS
NC = 1 + DB
NCP = NC + NC % 2
KT = D_MODEL // P
KS, CT = 4, 2
SLOT = KS * CT * P
RAW, RAW_A = 8, 4
RING, RING_A = 4, 2
QKV_T, Z_T, DSA_T = 3 * H, H, 16
FT = D_FF // P
FC = 4
NCH = FT // FC
LV = 7
L_S = PAST + TS
TOPK_P, TOPK_S = min(256, SEQ // 4), min(256, L_S // 4)
IDX_SCALE = IH ** -0.5 * ID ** -0.5
NEG_MASK, NEG_TAKEN, BIG = -2.0e38, -3.0e38, 1.0e30
HI_S = (CONV - 1) * DB
HI_F = (FCONV - 1) * DB

V_BADA = 0
V_G1 = V_BADA + 6 * KT
V_G2 = V_G1 + KT
V_GF = V_G2 + KT
V_WC = V_GF + KT
V_WF = V_WC + CONV * QKV_T
V_BF = V_WF + FCONV * 2 * FT
V_GN = V_BF + 2 * FT
V_ALL = V_GN + 1

PHASES = [("ada1", 2 * KT // CT * (KT // KS)), ("qkv", QKV_T // CT * (KT // KS)), ("z", Z_T // CT * (KT // KS)),
          ("dsa", DSA_T // CT * (KT // KS)), ("small", KT // KS), ("ada2", 4 * KT // CT * (KT // KS)),
          ("out", (KT // CT) * (2 * (KT // KS) + 2 * (H // KS))), ("wo", KT // CT * (KT // KS)),
          ("ffn", NCH * (2 * FC // CT * (KT // KS) + KT // CT))]
BASE = {}
_b = 0
for _n, _c in PHASES:
    BASE[_n] = _b
    _b += _c
NSLOTS = _b


def constants():
    f = np.float32
    c = {}
    c["ident"] = np.eye(P, dtype=f)
    c["ones"] = np.ones((P, P), f)
    j, i = np.meshgrid(np.arange(P), np.arange(P), indexing="ij")
    c["incl"] = (i >= j).astype(f)
    c["lev"] = np.stack([((i >> (l + 1)) == (j >> (l + 1))) & (((i >> l) & 1) == 1) & (((j >> l) & 1) == 0)
                         for l in range(LV)], 1).astype(f)
    js, is_ = np.meshgrid(np.arange(NS), np.arange(NS), indexing="ij")
    same = (js % DB) == (is_ % DB)
    tj, ti = js // DB, is_ // DB
    s = np.zeros((P, 4, NS), f)
    s[:NS, 0] = same & (ti >= tj)
    s[:NS, 1] = same & ((ti >> 1) == (tj >> 1)) & ((ti & 1) == 1) & ((tj & 1) == 0)
    s[:NS, 2] = same & ((ti >> 1) == 1) & ((tj >> 1) == 0)
    s[:NS, 3, :TS * DB] = (np.arange(NS)[:, None] % DB) == (np.arange(NS)[None, :] % DB)
    c["smask"] = s
    mb = (np.arange(NS)[None, :] % DB == np.arange(DB)[:, None]).astype(f)
    c["maskb"] = np.broadcast_to(mb[None], (P, DB, NS)).copy()
    c["bcol"] = np.zeros((P, DB), f)
    c["bcol"][:NS] = mb.T
    pos = np.concatenate([np.arange(SEQ), PAST + np.repeat(np.arange(TS), DB)]).astype(f)
    tab = np.zeros((P, 4, N), f)
    rot_m = np.zeros((P, 2, P), f)
    for n, d in enumerate((HD, ID)):
        rot = d // 4
        half = rot // 2
        inv = (f(ROPE_THETA) ** (-np.arange(half, dtype=f) * f(2.0 / rot))).astype(f)
        ang = (pos[None, :] * inv[:, None]).astype(f)
        cos, sin = np.cos(ang).astype(f), np.sin(ang).astype(f)
        tab[:, 2 * n] = 1.0
        for o in range(0, P, d):
            tab[o:o + half, 2 * n] = tab[o + half:o + rot, 2 * n] = cos
            tab[o:o + half, 2 * n + 1] = tab[o + half:o + rot, 2 * n + 1] = sin
            for a in range(half):
                rot_m[o + half + a, n, o + a] = -1.0
                rot_m[o + a, n, o + half + a] = 1.0
    c["rope"], c["rotm"] = tab, rot_m
    q = np.arange(P)[:, None, None] + P * np.arange(2)[None, :, None]
    c["causal"] = np.where(np.arange(SEQ)[None, None, :] <= q, -NEG_TAKEN, NEG_MASK).astype(f)
    cs = np.full((P, L_S), -NEG_TAKEN, f)
    t = np.arange(NS) // DB
    cs[:NS, PAST:] = np.where(np.arange(TS)[None, :] <= t[:, None], -NEG_TAKEN, NEG_MASK)
    c["causal_s"] = cs
    sel = np.zeros((P, H), f)
    sel[:H] = np.eye(H)
    c["sel"] = sel
    c["fold"] = np.zeros((P, NCP), f)
    c["fold"][:2 * NCP] = np.concatenate([np.eye(NCP)] * 2)
    c["eps"] = np.full((P, 1), EPS, f)
    c["one"] = np.ones((P, 1), f)
    return c


CONST_SIZE = {"ident": P, "ones": P, "incl": P, "lev": LV * P, "smask": 4 * NS, "maskb": DB * NS,
              "bcol": DB, "rope": 4 * N, "rotm": 2 * P, "causal": 2 * SEQ, "causal_s": L_S,
              "sel": H, "fold": NCP, "eps": 1, "one": 1}


def decoder_step(nc, A, O):
    f32, f32r, i32 = mybir.dt.float32, mybir.dt.float32r, mybir.dt.int32
    ALU, ACT, AX = mybir.AluOpType, mybir.ActivationFunctionType, mybir.AxisListType
    ds = bass.ds
    ctx = ExitStack()
    with ctx:
        base0 = ((nc.sbuf_base + 31) // 32) * 32

        class Place:
            def __init__(self, at):
                self.at = at

            def take(self, name, shape, dt=f32):
                size = 4 * int(np.prod(shape[1:]))
                t = nc.alloc_sbuf_tensor_at(name, shape, dt, offset=self.at)
                self.at += (size + 31) // 32 * 32
                return t

        fixed = Place(base0)
        consts = fixed.take("consts", [P, sum(CONST_SIZE.values())])
        cv, off = {}, 0
        for name, size in CONST_SIZE.items():
            cv[name] = consts[:, off:off + size]
            off += size
        ident, ones = cv["ident"], cv["ones"]
        lev = cv["lev"].rearrange("p (l i) -> p l i", l=LV)
        smask = cv["smask"].rearrange("p (m i) -> p m i", m=4)
        maskb = cv["maskb"].rearrange("p (b i) -> p b i", b=DB)
        rope = cv["rope"].rearrange("p (m n) -> p m n", m=4)
        rotm = cv["rotm"].rearrange("p (m n) -> p m n", m=2)
        causal = cv["causal"].rearrange("p (c k) -> p c k", c=2)
        causal_s, sel, eps_c, one_c = cv["causal_s"], cv["sel"], cv["eps"], cv["one"]
        vec = fixed.take("vec", [P, V_ALL])
        ada = fixed.take("ada", [P, 6 * KT, NC])
        cact = fixed.take("cact", [P, KT, 2, NCP], f32r)
        ptab = fixed.take("ptab", [1, DB * (PAST // PAGE)], i32)
        heads_v = fixed.take("heads_v", [H, 2])
        cond_t = Place(fixed.at).take("cond_t", [2 * NCP, CT * P])
        rsb = fixed.take("rsb", [P, N])
        h_hi = fixed.take("h_hi", [P, KT, N], f32r)
        h_lo = fixed.take("h_lo", [P, KT, N], f32r)
        rest_a = Place(fixed.at).take("rest_a", [P, RAW_A, KS, CT * P], f32r)
        raw_a = fixed.take("raw_a", [P, RAW_A, KS, CT * P])
        hi_a = fixed.take("hi_a", [P, RING_A, KS, CT * P], f32r)
        ring_at = fixed.at
        hi_b = fixed.take("hi_b", [P, RING - RING_A, KS, CT * P], f32r)
        rest_b = Place(fixed.at).take("rest_b", [P, RAW - RAW_A, KS, CT * P], f32r)
        raw_b = fixed.take("raw_b", [P, RAW - RAW_A, KS, CT * P])
        raw = [raw_a[:, r, :, :] for r in range(RAW_A)] + [raw_b[:, r, :, :] for r in range(RAW - RAW_A)]
        rest = [rest_a[:, r, :, :] for r in range(RAW_A)] + [rest_b[:, r, :, :] for r in range(RAW - RAW_A)]
        w_hi = [hi_a[:, q, :, :] for q in range(RING_A)] + [hi_b[:, q, :, :] for q in range(RING - RING_A)]
        rest_at = fixed.at

        pl = Place(rest_at)
        x = pl.take("x", [P, KT, N])
        og_p = Place(rest_at)
        og_hi = og_p.take("og_hi", [P, H, N], f32r)
        og_lo = og_p.take("og_lo", [P, H, N], f32r)
        qkv_at = pl.at
        qkv = pl.take("qkv", [P, QKV_T, N])
        z = pl.take("z", [P, Z_T, N])
        dsa_at = pl.at
        dsa = pl.take("dsa", [P, DSA_T, N])
        ikk = pl.take("ikk", [P, N])
        sm_iw = pl.take("sm_iw", [H, N])
        rows_at = pl.at
        rows = pl.take("rows", [H, 4, N])
        tail_at = pl.at
        ip = Place(rest_at)
        cst = ip.take("cst", [P, QKV_T, HI_S + NS])
        cpt = ip.take("cpt", [P, QKV_T, CONV - 1])
        cin = ip.take("cin", [P, CT, CONV - 1 + SEQ])
        cy = ip.take("cy", [P, CT, N])
        sm_a = ip.take("sm_a", [H, N])
        sm_b = ip.take("sm_b", [H, N])
        sm_t = ip.take("sm_t", [H, 2, N])
        assert ip.at <= qkv_at
        np_ = Place(qkv_at)
        sq = np_.take("sq", [P, 2, N])
        ht = np_.take("ht", [P, 2, N])
        hf = np_.take("hf", [P, 2, N])
        amul = np_.take("amul", [P, KT, NC])
        c_f = np_.take("c_f", [P, KT, NCP])
        gp = Place(ring_at)
        gc_t = gp.take("gc_t", [P, 3, H])
        ke_t = gp.take("ke_t", [P, 3, H])
        sqb = gp.take("sqb", [P, 3, N])
        nrm = gp.take("nrm", [P, 3, N])
        qk = gp.take("qk", [P, 2, N])
        rows_m = gp.take("rows_m", [H, 3, N])
        br = gp.take("br", [P, 3, N])
        e_s = gp.take("e_s", [NS, NS])
        qkd_s = gp.take("qkd_s", [NS, NS])
        at_s = gp.take("at_s", [NS, NS])
        bt_s = gp.take("bt_s", [NS, NS])
        tt = gp.take("tt", [P, 4, P])
        tt_s = gp.take("tt_s", [NS, 2, NS])
        x_s = gp.take("x_s", [NS, NS])
        gq = Place(tail_at)
        at_p = gq.take("at_p", [P, 2, P])
        e_p = gq.take("e_p", [P, 2, P])
        qkd_p = gq.take("qkd_p", [P, 2, P])
        x_p = gq.take("x_p", [P, 2, P])
        bt_p = gq.take("bt_p", [P, 2, 2, P])
        r_t = gq.take("r_t", [P, P])
        r_ts = gq.take("r_ts", [P, NS])
        r_p = gq.take("r_p", [P, P])
        r_s = gq.take("r_s", [NS, P])
        u_p = gq.take("u_p", [P, P])
        u_s = gq.take("u_s", [NS, P])
        kend = gq.take("kend", [P, 2, P])
        kend_s = gq.take("kend_s", [NS, P])
        kmask = gq.take("kmask", [NS, DB, P])
        qdec = gq.take("qdec", [P, P])
        st_p = gq.take("st_p", [P, P])
        st_in = gp.take("st_in", [P, DB, P])
        st_out = gq.take("st_out", [P, DB, P])
        o_add = gq.take("o_add", [P, NS])
        o_b = gq.take("o_b", [P, N])
        assert gp.at <= rest_at
        dp = Place(ring_at)
        v_c = dp.take("v_c", [P, DB, PAST // PAGE, KV * HD])
        dq_ = Place(qkv_at)
        do_hi = dq_.take("do_hi", [P, QH, N], f32r)
        do_lo = dq_.take("do_lo", [P, QH, N], f32r)
        kt_c = dq_.take("kt_c", [P, DB, KV, L_S])
        assert dq_.at <= dsa_at
        dr = Place(dp.at)
        sc_p = dr.take("sc_p", [P, 2, SEQ])
        wk_p = dr.take("wk_p", [P, 2, SEQ])
        sc_s = dr.take("sc_s", [NS, L_S])
        wk_s = dr.take("wk_s", [NS, L_S])
        iw_t = dr.take("iw_t", [P, 2, IH])
        iw_s = dr.take("iw_s", [NS, IH])
        top8 = dr.take("top8", [P, 3, 8])
        vtok_s = dr.take("vtok_s", [P, KV * HD])
        assert dr.at <= rest_at, (dr.at, rest_at)
        dt_ = Place(tail_at)
        iqm = dt_.take("iqm", [P, 4, DB, NS])
        rel = dt_.take("rel", [P, 2, L_S])
        vtok = dt_.take("vtok", [P, 2, KV * HD])
        ik_c = dt_.take("ik_c", [P, DB, L_S])
        bias_s = dt_.take("bias_s", [NS, L_S])
        dw = Place(rows_at)
        bias_p = dw.take("bias_p", [P, P + SEQ])
        assert dw.at <= tail_at
        du = Place(dsa_at + 12 * N * 4)
        dt2 = Place(tail_at)
        rtmp = dt2.take("rtmp", [P, N])
        q_m = dt2.take("q_m", [P, DB, NS])
        p_tm = dt2.take("p_tm", [P, 2, DB, NS])
        assert dt2.at <= tail_at + 4 * 4 * DB * NS + 4 * 2 * L_S
        q_r = du.take("q_r", [P, N])
        s_p = du.take("s_p", [P, P + SEQ])
        s_s = du.take("s_s", [NS, L_S])
        stat = du.take("stat", [P, 4, 3])
        assert du.at <= dsa_at + DSA_T * N * 4
        p_t = dt_.take("p_t", [P, 3, P])
        pn = dt_.take("pn", [NS, NS])
        pn_t = dt_.take("pn_t", [P, NS])
        o_n = dt_.take("o_n", [P, 2, P])
        o_ns = dt_.take("o_ns", [NS, P])
        rot_t = dt_.take("rot_t", [P, N])
        mp = Place(qkv_at + 2 * 4 * QH * N)
        mix = mp.take("mix_hi", [P, KT, N], f32r)
        mix_lo = mp.take("mix_lo", [P, KT, N], f32r)
        sg = mp.take("sg", [P, 2, CT, N])
        mt = mp.take("mt", [P, CT, N])
        fp = Place(np_.at)
        act_f = fp.take("act_f", [P, CT, N])
        act_hi = fp.take("act_hi", [P, 2, FC, N], f32r)
        act_lo = fp.take("act_lo", [P, 2, FC, N], f32r)
        fst = fp.take("fst", [P, 2 * FT, HI_F + NS])
        fpt = fp.take("fpt", [P, 2 * FT, FCONV - 1])
        fin = fp.take("fin", [P, CT, FCONV - 1 + SEQ])
        fy = fp.take("fy", [P, CT, N])
        fsil = fp.take("fsil", [P, CT, N])
        dtmp = fp.take("dtmp", [P, NS])
        for q_ in (pl, gq, dt_, mp, fp):
            assert q_.at <= nc.sbuf_usable_end, (q_.at, nc.sbuf_usable_end)

        bank = [ctx.enter_context(nc.psum_tensor(f"bank{i}", [P, 512], f32)) for i in range(8)]

        def sem(name):
            return ctx.enter_context(nc.semaphore(name))

        raw_in = [sem(f"raw_in{i}") for i in range(RAW)]
        raw_free = [sem(f"raw_free{i}") for i in range(RAW)]
        hi_ready = sem("hi_ready")
        lo_ready, lo_dve = sem("lo_ready"), sem("lo_dve")
        ring_free = sem("ring_free")
        cond_cp = sem("cond_cp")
        cond_done = sem("cond_done")
        grp_free = [sem(f"grp_free{i}") for i in range(4)]
        const_in, x_in, x_back, out_done = sem("const_in"), sem("x_in"), sem("x_back"), sem("out_done")
        c_ready = sem("c_ready")
        sq_ready, sq_used, ssq_ready, rs_ready = sem("sq_ready"), sem("sq_used"), sem("ssq_ready"), sem("rs_ready")
        h_t, h_hi_ready, h_lo_ready = sem("h_t"), sem("h_hi_ready"), sem("h_lo_ready")
        conv_y, conv_used = sem("conv_y"), sem("conv_used")
        small_done = sem("small_done")
        row_dve, row_act, row_tr = sem("row_dve"), sem("row_act"), sem("row_tr")
        G = {n: sem("gdn_" + n) for n in (
            "sq ssq rowm bc nrm br qk gram kt e d t1 t1t x xs dt t kss ra rt rs u us kend qkd sa S1 ks ssm rb sb o "
            "sin spout ssout dve").split()}
        X = {n: sem("dsa_" + n) for n in (
            "load rot rotd vt vtd iqm idx rel acc newk topk q rotq s m p pn pt ptm pts o on ot end outd ikn").split()}
        g_sig, mix_done = sem("g_sig"), sem("mix_done")
        x_done = sem("x_done")
        sil_done, act_ready, down_done = sem("sil_done"), sem("act_ready"), sem("down_done")
        y_ready = sem("y_ready")

        used = [0] * 4
        gbase = {}
        for name, groups, sets in (("ada1", 2 * KT // CT, 2), ("qkv", QKV_T // CT, 2), ("z", Z_T // CT, 2),
                                   ("dsa", DSA_T // CT, 2), ("small", 1, 1), ("ada2", 4 * KT // CT, 1),
                                   ("out", 4 * (KT // CT), 4), ("wo", KT // CT, 4),
                                   ("ffn", NCH * (2 * FC // CT + KT // CT), 4)):
            gbase[name] = list(used)
            for s_ in range(sets):
                used[s_] += groups // sets

        def grp(name, sets, g, i=0, per=0):
            return g % sets, gbase[name][g % sets] + g // sets + i * (per // sets)

        stretches, uses = [], [0] * RAW
        for first, end, size in ((0, BASE["ada2"], RAW), (BASE["ada2"], BASE["out"], RAW_A), (BASE["out"], NSLOTS, RAW)):
            stretches.append((first, end, size, list(uses)))
            for s_ in range(end - first):
                uses[s_ % size] += 1

        def raw_at(name, j, i=0, per=0):
            s_ = BASE[name] + j
            first, _, size, before = next(t for t in stretches if t[0] <= s_ < t[1])
            return (s_ - first) % size, before[(s_ - first) % size] + (s_ - first) // size + i * (per // size)

        def wait_group(eng, name, g, i=0, per=0):
            if name == "out":
                j, per_j = 12 * (g // 4) + (3, 7, 9, 11)[g % 4], 3 * per
            elif name == "ffn":
                n, m = divmod(g - 4, 12)
                j = 4 * g + 3 if g < 4 else 16 + 24 * n + (m if n == NCH - 1 else (3, 7, 8, 9, 10, 11, 12, 13, 14, 15, 19, 23)[m])
                per_j = 2 * per
            else:
                j, per_j = 4 * g + 3, 4 * per
            r, use = raw_at(name, j, i, per_j)
            eng.wait_ge(raw_free[r], use + 2)

        def split_at(name, j, i=0, per=0):
            s_ = BASE[name] + j
            return s_ % (RING_A if BASE["ada2"] <= s_ < BASE["out"] else RING), s_ + i * per

        LO_DVE = BASE["qkv"] // 2

        block = ctx.enter_context(nc.Block())

        @block.sync
        def _(sp):
            def load(r, use, slot):
                sp.wait_ge(raw_free[r], use + 1)
                sp.dma_start(raw[r].rearrange("p k c -> p (k c)"),
                             A["stream"][ds(slot, 1), :, :].rearrange("s p n -> (s p) n")).then_inc(raw_in[r], 16)

            for n, (first, end, size, before) in enumerate(stretches):
                peel = 0
                if n == 2:
                    for r in range(size):
                        if r == RAW_A:
                            sp.wait_ge(X["end"], QH)
                        load(r, before[r], first + r)
                    peel = 1
                loops = (end - first) // size
                with sp.Fori(peel, loops) as i:
                    for r in range(size):
                        load(r, i + before[r], i * size + (first + r))
                for r in range(end - first - loops * size):
                    load(r, before[r] + loops, first + loops * size + r)
            sp.wait_ge(y_ready, KT // 2)
            sp.dma_start(O["y"], x[:, :, :].rearrange("p k n -> p (k n)")).then_inc(out_done, 16)
            sp.wait_ge(out_done, 16 * 8)
            sp.wait_ge(G["spout"], 16 * (H + 1))
            sp.wait_ge(G["ssout"], 16 * (H + 1))

        @block.gpsimd
        def _(pool):
            for r in range(RAW):
                pool.sem_inc(raw_free[r], 1)
            pool.sem_inc(ring_free, RING)
            pool.sem_inc(sq_used, 2)
            pool.sem_inc(h_lo_ready, 2)

            def lo(name, j, i=0, per=0):
                r, _ = raw_at(name, j, i, per)
                q, cnt = split_at(name, j, i, per)
                pool.wait_ge(hi_ready, cnt + 1)
                nc.gpsimd.tensor_tensor(rest[r], raw[r], w_hi[q].bitcast(f32), ALU.subtract).then_inc(lo_ready, 1)

            def h_rest(base):
                with pool.Fori(0, KT // 2) as i:
                    for s_ in range(2):
                        pool.wait_ge(h_hi_ready, i * 2 + base + s_ + 1)
                        k = i * 2 + s_
                        nc.gpsimd.tensor_tensor(h_lo[:, ds(k, 1), :].rearrange("p k n -> p (k n)"), hf[:, s_, :],
                                                h_hi[:, ds(k, 1), :].rearrange("p k n -> p (k n)").bitcast(f32),
                                                ALU.subtract).then_inc(h_lo_ready, 1)

            def run(name, first, count, per):
                with pool.Fori(0, count // per) as i:
                    for j in range(per):
                        lo(name, first + j, i, per)

            pool.wait_ge(c_ready, 1)
            nc.gpsimd.tensor_tensor(cact[:, :, 1, :], c_f[:, :, :], cact[:, :, 0, :].bitcast(f32), ALU.subtract).then_inc(c_ready, 1)
            with pool.Fori(0, LO_DVE // 4) as i:
                for j in range(0, 8, 2):
                    lo("ada1", j, i, 8)
            h_rest(0)
            run("qkv", 0, 48 + 16 + 32, 8)
            for j in range(KT // KS):
                lo("small", j)
            run("ada2", 0, 128, 8)
            run("out", 0, 96 + 32, 8)
            h_rest(KT)
            run("ffn", 0, NSLOTS - BASE["ffn"], 8)

        @block.scalar
        def _(act):
            A_ = nc.scalar.activation
            act.sem_inc(conv_used, 2)
            for g_ in range(4):
                act.sem_inc(grp_free[g_], 1)
            act.dma_start(x[:, :, :].rearrange("p k n -> p (k n)"), A["x"]).then_inc(x_in, 16)
            act.dma_start(c_f[:, :, :].rearrange("p k n -> p (k n)"), A["c"]).then_inc(x_in, 16)
            act.dma_start(consts[:, :], A["consts"]).then_inc(const_in, 16)
            act.dma_start(vec[:, :], A["vec"]).then_inc(const_in, 16)
            act.dma_start(heads_v[:, :], A["heads_v"]).then_inc(const_in, 16)
            act.dma_start(ptab[:, :], A["ptab"]).then_inc(X["load"], 16)

            def hi(name, j, i=0, per=0):
                r, use = raw_at(name, j, i, per)
                q, cnt = split_at(name, j, i, per)
                act.wait_ge(raw_in[r], use * 16 + 16)
                act.wait_ge(ring_free, cnt + 1 + (RING - RING_A if name == "ada2" else 0))
                A_(w_hi[q], raw[r], ACT.Copy).then_inc(hi_ready, 1)

            act.wait_ge(x_in, 32)
            A_(c_f[:, :, :], c_f[:, :, :], ACT.Silu)
            act.drain()
            A_(cact[:, :, 0, :], c_f[:, :, :], ACT.Copy).then_inc(c_ready, 1)

            def norm_stats(n):
                with act.Fori(0, KT // 2) as i:
                    for s_ in range(2):
                        if n == 0:
                            for j in range(4):
                                hi("ada1", 4 * s_ + j, i, 8)
                        act.wait_ge(sq_used, i * 2 + n * KT + s_ + 1)
                        A_(sq[:, s_, :], x[:, ds(i * 2 + s_, 1), :].rearrange("p k n -> p (k n)"),
                           ACT.Square).then_inc(sq_ready, 1)
                act.wait_ge(ssq_ready, n + 1)
                if n == 0:
                    act.wait_ge(cond_done, KT)
                A_(rsb[:, :], bank[7][:, 0:N], ACT.Ln, bias=eps_c, scale=1.0 / D_MODEL)
                act.drain()
                A_(rsb[:, :], rsb[:, :], ACT.Exp, scale=-0.5).then_inc(rs_ready, 1)

            def h_round(base):
                with act.Fori(0, KT // 2) as i:
                    for s_ in range(2):
                        act.wait_ge(h_t, i * 2 + base + s_ + 1)
                        A_(h_hi[:, ds(i * 2 + s_, 1), :].rearrange("p k n -> p (k n)"), hf[:, s_, :],
                           ACT.Copy).then_inc(h_hi_ready, 1)

            act.wait_ge(const_in, 48)
            norm_stats(0)
            h_round(0)
            act.wait_ge(h_t, KT)
            act.dma_start(cst[:, :, 0:HI_S], A["gdn_hist"].rearrange("p (t n) -> p t n", t=QKV_T)).then_inc(const_in, 16)

            LA = 2

            def silu_tiles(g, i=0, per=0):
                for c in range(CT):
                    n = g * CT + c
                    t = i * (per * CT) + n
                    act.wait_ge(conv_y, t + 1)
                    A_(qkv[:, ds(t, 1), :].rearrange("p k n -> p (k n)"), cy[:, c, :],
                       ACT.Silu).then_inc(conv_used, 1)

            for j in range(LA):
                hi("qkv", j)
            with act.Fori(0, 5) as i:
                for j in range(4):
                    hi("qkv", LA + j, i, 8)
                silu_tiles(0, i, 2)
                for j in range(4):
                    hi("qkv", LA + 4 + j, i, 8)
                silu_tiles(1, i, 2)
            for j in range(4):
                hi("qkv", 40 + LA + j)
            silu_tiles(10)
            for j in range(4):
                hi("qkv", 44 + LA + j)
            silu_tiles(11)

            def z_tiles(g, i=0, per=0):
                bs, _ = grp("z", 2, g)
                wait_group(act, "z", g, i, per)
                for c in range(CT):
                    t = i * (per * CT) + g * CT + c
                    A_(z[:, ds(t, 1), :].rearrange("p k n -> p (k n)"), bank[2 * bs + c][:, 0:N], ACT.Silu)
                act.drain()
                act.sem_inc(grp_free[bs], 1)

            for g in range(4):
                for j in range(4):
                    hi("z", LA + 4 * g + j)
                z_tiles(g)
            with act.Fori(0, 3) as i:
                for j in range(8):
                    hi("dsa", LA + j, i, 8)
            for j in range(24 + LA, 32 + 4):
                hi("dsa", j)

            act.wait_ge(small_done, 1)
            A_(sm_t[:, 0, :], sm_a[:, :], ACT.Identity, bias=heads_v[:, 1:2])
            A_(sm_b[:, :], sm_b[:, :], ACT.Exp, scale=-1.0)
            A_(heads_v[:, 0:1], heads_v[:, 0:1], ACT.Exp)
            act.drain()
            A_(sm_a[:, :], sm_t[:, 0, :], ACT.Abs)
            act.drain()
            A_(sm_a[:, :], sm_a[:, :], ACT.Exp, scale=-1.0)
            act.drain()
            A_(sm_a[:, :], sm_a[:, :], ACT.Ln, bias=one_c[0:H, :]).then_inc(row_act, 1)
            act.wait_ge(row_dve, 1)
            A_(rows[:, 2, :], rows[:, 0, :], ACT.Exp)
            A_(rows[:, 3, :], rows[:, 3, :], ACT.Exp, scale=-1.0).then_inc(row_act, 1)

            act.wait_ge(small_done, 1)
            act.dma_start(O["gdn_tail_s"].rearrange("p (t n) -> p t n", t=QKV_T), cst[:, :, HI_S + NS - HI_S:]).then_inc(out_done, 16)
            act.dma_start(O["gdn_tail_p"], cpt[:, :, :].rearrange("p t n -> p (t n)")).then_inc(out_done, 16)

            def g_load(h):
                act.dma_start(st_in[:, :, :].rearrange("p b n -> p (b n)"),
                              A["state"][ds(h, 1), :, :].rearrange("h p n -> (h p) n")).then_inc(G["sin"], 16)

            g_load(0)
            act.wait_ge(out_done, 32)

            def squares(hr):
                A_(sqb[:, 0, :], qkv[:, ds(hr, 1), :].rearrange("p k n -> p (k n)"), ACT.Square)
                A_(sqb[:, 1, :], qkv[:, ds(hr + H, 1), :].rearrange("p k n -> p (k n)"), ACT.Square).then_inc(G["sq"], 1)

            def norms(n, m):
                act.wait_ge(G["ssq"], n)
                A_(nrm[:, 0, :], bank[2][:, 0:N], ACT.Ln, bias=eps_c)
                A_(nrm[:, 1, :], bank[3][:, 0:N], ACT.Ln, bias=eps_c)
                if m == 3:
                    A_(nrm[:, 2, :], bank[7][:, 0:N], ACT.Ln, bias=eps_c, scale=1.0 / DK)
                act.drain()
                A_(nrm[:, 0:m, :], nrm[:, 0:m, :], ACT.Exp, scale=-0.5).then_inc(G["nrm"], 1)
                act.wait_ge(G["bc"], n)
                for c in range(3):
                    last = A_(br[:, c, :], bank[4 + c][:, 0:N], ACT.Copy)
                last.then_inc(G["br"], 1)

            squares(0)
            norms(1, 2)
            with act.Fori(0, H) as h:
                act.wait_ge(G["e"], h + 1)
                A_(e_s[:, :], e_s[:, :], ACT.Exp)
                A_(e_p[:, :, :], e_p[:, :, :], ACT.Exp).then_inc(G["d"], 1)
                hi("ada2", 0, h, 8)
                for l in range(1, LV):
                    act.wait_ge(G["x"], h * (LV - 1) + l)
                    if l == 1:
                        A_(x_s[:, :], bank[4][0:NS, 2 * P:2 * P + NS], ACT.Copy)
                    A_(x_p[:, :, :].rearrange("p c n -> p (c n)"), bank[4][:, 0:2 * P], ACT.Copy).then_inc(G["xs"], 1)
                    hi("ada2", l, h, 8)
                for c in range(2):
                    act.wait_ge(G["rt"], h * 2 + c + 1)
                    if c == 0:
                        A_(r_s[:, :], bank[6][0:NS, P:2 * P], ACT.Copy)
                    A_(r_p[:, :], bank[6][:, 0:P], ACT.Copy).then_inc(G["rs"], 1)
                    act.wait_ge(G["u"], h * 2 + c + 1)
                    if c == 0:
                        A_(u_s[:, :], bank[6][0:NS, P:2 * P], ACT.Copy)
                    A_(u_p[:, :], bank[6][:, 0:P], ACT.Copy).then_inc(G["us"], 1)
                hi("ada2", 7, h, 8)
                act.wait_ge(G["o"], h + 1)
                act.dma_start(O["state_p"][ds(h, 1), :, :].rearrange("h p n -> (h p) n"), st_p[:, :]).then_inc(G["spout"], 16)
                act.dma_start(O["state_s"][ds(h, 1), :, :].rearrange("h p n -> (h p) n"),
                              st_out[:, :, :].rearrange("p b n -> p (b n)")).then_inc(G["ssout"], 16)
                hn = (h + 1) & (H - 1)
                g_load(hn)
                A_(sqb[:, 2, :], o_b[:, :], ACT.Square)
                squares(hn)
                norms(h + 2, 3)
            act.wait_ge(G["dve"], 1)
            act.wait_ge(G["br"], H + 1)
            act.wait_ge(G["sin"], 16 * (H + 1))

            with ExitStack() as rs_:
                act.wait_ge(X["load"], 16)
                for b in range(DB):
                    for g in range(PAST // PAGE):
                        pid = act.value_load(ptab[0:1, 2 * b + g:2 * b + g + 1], min_val=0, max_val=NPOOL - 1)
                        act.dma_start(kt_c[:, b, :, PAGE * g:PAGE * (g + 1)],
                                      A["ck"][ds(pid, 1), :, :].rearrange("s p (k n) -> (s p) k n", k=KV)).then_inc(X["load"], 16)
                        act.dma_start(ik_c[:, b, PAGE * g:PAGE * (g + 1)],
                                      A["cik"][ds(pid, 1), :, :].rearrange("s p n -> (s p) n")).then_inc(X["load"], 16)
                        act.dma_start(v_c[:, b, g, :],
                                      A["cv"][ds(pid, 1), :, :].rearrange("s p n -> (s p) n")).then_inc(X["load"], 16)
            act.wait_ge(X["rotd"], 7)
            act.dma_start(O["k"], dsa[:, QH:QH + KV, :].rearrange("p k n -> p (k n)")).then_inc(out_done, 16)
            act.dma_start(O["v"], dsa[:, QH + KV:QH + 2 * KV, :].rearrange("p k n -> p (k n)")).then_inc(out_done, 16)
            act.dma_start(O["ik"], ikk[0:ID, :]).then_inc(out_done, 16)
            act.wait_ge(X["newk"], 1)
            act.wait_ge(X["vt"], 1)
            A_(vtok[:, :, :].rearrange("p c n -> p (c n)"), bank[4][:, :], ACT.Copy)
            A_(vtok_s[0:NS, :], bank[5][0:NS, 0:KV * HD], ACT.Copy)
            A_(iw_t[:, :, :].rearrange("p c n -> p (c n)"), bank[6][:, 0:2 * IH], ACT.Copy, scale=IDX_SCALE)
            A_(iw_s[:, :], bank[6][0:NS, 2 * IH:3 * IH], ACT.Copy, scale=IDX_SCALE).then_inc(X["vtd"], 1)
            for n in range(3 * IH):
                act.wait_ge(X["idx"], n + 1)
                if n >= 2:
                    act.wait_ge(X["acc"], n - 1)
                if n < 2 * IH:
                    A_(rel[:, n % 2, 0:SEQ], bank[2 + n % 2][:, 0:SEQ], ACT.Relu).then_inc(X["rel"], 1)
                else:
                    A_(rel[0:NS, n % 2, :], bank[2 + n % 2][0:NS, 0:L_S], ACT.Relu).then_inc(X["rel"], 1)
            act.wait_ge(X["load"], 16 * (1 + 3 * DB * (PAST // PAGE)))
            sc_ = HD ** -0.5
            with act.Fori(0, QH) as h:
                hi("ada2", 8 * H, h, 8)
                hi("ada2", 8 * H + 1, h, 8)
                act.wait_ge(X["m"], h + 1)
                A_(s_p[:, 0:P], s_p[:, 0:P], ACT.Exp, bias=stat[:, 0, 0:1], scale=sc_, accum_out=stat[:, 1, 0:1])
                A_(s_p[:, P:], s_p[:, P:], ACT.Exp, bias=stat[:, 0, 1:2], scale=sc_, accum_out=stat[:, 1, 1:2])
                A_(s_s[:, :], s_s[:, :], ACT.Exp, bias=stat[0:NS, 0, 2:3], scale=sc_,
                   accum_out=stat[0:NS, 1, 2:3]).then_inc(X["p"], 1)
                hi("ada2", 8 * H + 2, h, 8)
                hi("ada2", 8 * H + 3, h, 8)
                act.wait_ge(X["pt"], h + 1)
                A_(p_t[:, :, :].rearrange("p c n -> p (c n)"), bank[5][:, 0:3 * P], ACT.Copy).then_inc(X["pts"], 1)
                for j in range(4, 8):
                    hi("ada2", 8 * H + j, h, 8)

            def gate_tiles(which, i, g0):
                bs, _ = grp("out", 4, 4 * g0 + which)
                wait_group(act, "out", 4 * g0 + which, i, 8)
                act.wait_ge(mix_done, i * 2 + g0 + 1)
                for c in range(CT):
                    last = A_(sg[:, which, c, :], bank[2 * bs + c][:, 0:N], ACT.Sigmoid)
                last.then_inc(g_sig, 1)
                act.wait_ge(g_sig, (i * 2 + g0) * 2 + which + 1)
                act.sem_inc(grp_free[bs], 1)

            act.wait_ge(out_done, 16 * 5)
            act.wait_ge(X["end"], QH)
            for j in range(LA):
                hi("out", j)

            def out_body(i, hold=0):
                for g0 in range(2):
                    for j in range(4):
                        hi("out", LA + 12 * g0 + j, i, 24)
                    gate_tiles(0, i, g0)
                    for j in range(4, 8):
                        hi("out", LA + 12 * g0 + j, i, 24)
                    gate_tiles(1, i, g0)
                    for j in range(8, 12):
                        hi("out", LA + 12 * g0 + j, i, 24)

            with act.Fori(0, 4) as i:
                out_body(i)
            bs, _ = grp("out", 4, 4 * (KT // CT) - 1)
            wait_group(act, "out", 4 * (KT // CT) - 1)
            act.dma_start(x[:, :, :].rearrange("p k n -> p (k n)"), A["x"]).then_inc(x_back, 16)
            with act.Fori(0, 3) as i:
                for j in range(8):
                    hi("wo", LA + j, i, 8)
            for j in range(24 + LA, 32):
                hi("wo", j)
            act.wait_ge(x_done, KT)
            norm_stats(1)
            act.dma_start(fst[:, :, 0:HI_F], A["ffn_hist"].rearrange("p (t n) -> p t n", t=2 * FT)).then_inc(const_in, 16)
            h_round(KT)

            def ffn_silu(c0, i):
                for c in range(CT):
                    t = i * FC + c0 + c
                    act.wait_ge(conv_y, QKV_T + i * FC + c0 + c + 1)
                    A_(fsil[:, c, :], fy[:, c, :], ACT.Silu,
                       bias=vec[:, ds(t + V_BF, 1)]).then_inc(sil_done, 1)

            for j in range(LA):
                hi("ffn", j)
            for j in range(4):
                hi("ffn", LA + j)
            ffn_silu(0, 0)
            for j in range(4, 12):
                hi("ffn", LA + j)
            ffn_silu(2, 0)
            for j in range(12, 16):
                hi("ffn", LA + j)
            with act.Fori(0, NCH - 1) as i:
                for j in range(4):
                    hi("ffn", 16 + LA + j, i, 24)
                ffn_silu(0, i + 1)
                for j in range(4, 20):
                    hi("ffn", 16 + LA + j, i, 24)
                ffn_silu(2, i + 1)
                for j in range(20, 24):
                    hi("ffn", 16 + LA + j, i, 24)
            for j in range(16 + LA + 24 * (NCH - 1), NSLOTS - BASE["ffn"]):
                hi("ffn", j)
            act.wait_ge(down_done, NCH * KT)
            act.dma_start(O["ffn_tail_s"].rearrange("p (t n) -> p t n", t=2 * FT), fst[:, :, NS:]).then_inc(out_done, 16)
            act.dma_start(O["ffn_tail_p"], fpt[:, :, :].rearrange("p t n -> p (t n)")).then_inc(out_done, 16)
            norm_stats(2)

        @block.vector
        def _(dve):
            V = nc.vector
            T_, S_, STT, CP = V.tensor_tensor, V.tensor_scalar, V.scalar_tensor_tensor, V.tensor_copy
            row = lambda a: a.rearrange("p k n -> p (k n)")

            def cond_copy(name, g, sets, i=0, per=0):
                wait_group(dve, name, g, i, per)
                CP(cond_t[:, :], bank[2 * (g % sets)][0:2 * NCP, 0:CT * P]).then_inc(cond_cp, 1)

            def cond_bias(name, g, sets, i=0, per=0):
                n0 = g + (2 * KT // CT if name == "ada2" else 0)
                dve.wait_ge(cond_done, i * per + (n0 + 1))
                t = i * (per * CT) + n0 * CT
                T_(ada[:, ds(t, CT), :], bank[2 * (g % sets) + 1][:, 0:CT * NCP].rearrange("p (c n) -> p c n", c=CT)[:, :, 0:NC],
                   vec[:, ds(t + V_BADA, CT)].unsqueeze(2).to_broadcast([P, CT, NC]), ALU.add).then_inc(grp_free[g % sets], 1)

            dve.sem_inc(mix_done, 1)
            dve.wait_ge(x_in, 32)
            dve.wait_ge(const_in, 48)

            def ada1_pair(first, i=0):
                for g in (first, first + 1):
                    for j in (4 * g + 1, 4 * g + 3):
                        r, _ = raw_at("ada1", j, i, 8)
                        q, n = split_at("ada1", j, i, 8)
                        dve.wait_ge(hi_ready, n + 1)
                        T_(rest[r], raw[r], w_hi[q].bitcast(f32), ALU.subtract).then_inc(lo_dve, 1)
                        if j % 4 == 1 and g > 0:
                            cond_bias("ada1", g - 1, 2, i, 2)
                    cond_copy("ada1", g, 2, i, 2)

            dve.sem_inc(cond_cp, 2)
            ada1_pair(0)
            with dve.Fori(0, KT // CT - 2) as i:
                ada1_pair(2, i)
            ada1_pair(KT - 2)
            cond_bias("ada1", KT - 1, 2)
            dve.drain()

            def scale_shift(n, sub):
                gcol = V_G1 if n == 0 else V_G2
                g_b = vec[:, gcol:gcol + KT].unsqueeze(2).to_broadcast([P, KT, NC])
                STT(amul[:, :, :], ada[:, (3 * sub + 1) * KT:(3 * sub + 2) * KT, :], 1.0, g_b, ALU.add, ALU.mult)
                dve.drain()
                dve.wait_ge(rs_ready, n + 1)
                with dve.Fori(0, KT // 2) as i:
                    for s_ in range(2):
                        k = i * 2 + s_
                        T_(ht[:, s_, :], row(x[:, ds(k, 1), :]), rsb[:, :], ALU.mult)
                    dve.drain()
                    for s_ in range(2):
                        k = i * 2 + s_
                        dve.wait_ge(h_lo_ready, i * 2 + n * KT + s_ + 1)
                        am, sh = row(amul[:, ds(k, 1), :]), row(ada[:, ds(k + 3 * sub * KT, 1), :])
                        S_(hf[:, s_, 0:SEQ], ht[:, s_, 0:SEQ], am[:, 0:1], sh[:, 0:1], ALU.mult, ALU.add)
                        T_(ht[:, s_, SEQ:].rearrange("p (t b) -> p t b", b=DB), ht[:, s_, SEQ:].rearrange("p (t b) -> p t b", b=DB),
                           am[:, 1:NC].unsqueeze(1).to_broadcast([P, TS, DB]), ALU.mult)
                    dve.drain()
                    for s_ in range(2):
                        k = i * 2 + s_
                        sh = row(ada[:, ds(k + 3 * sub * KT, 1), :])
                        T_(hf[:, s_, SEQ:].rearrange("p (t b) -> p t b", b=DB), ht[:, s_, SEQ:].rearrange("p (t b) -> p t b", b=DB),
                           sh[:, 1:NC].unsqueeze(1).to_broadcast([P, TS, DB]), ALU.add).then_inc(h_t, 1)
                    dve.drain()

            scale_shift(0, 0)
            dve.drain()
            V.memset(cin[:, :, 0:CONV - 1], 0.0)
            dve.wait_ge(const_in, 64)

            def conv(psum, c, src, y, st, tile, tap0, taps, hist, ntile, keep):
                CP(src[:, c, taps - 1:taps - 1 + SEQ], psum[:, 0:SEQ])
                CP(row(st[:, ds(tile, 1), hist:hist + NS]), psum[:, SEQ:N])
                dve.drain()
                for w_ in range(taps):
                    wc = vec[:, ds(tile + (tap0 + w_ * ntile), 1)]
                    sp_ = src[:, c, w_:w_ + SEQ]
                    ss_ = row(st[:, ds(tile, 1), DB * w_:DB * w_ + NS])
                    if w_ == 0:
                        S_(y[:, c, 0:SEQ], sp_, wc, None, ALU.mult)
                        S_(y[:, c, SEQ:], ss_, wc, None, ALU.mult)
                        CP(row(keep[:, ds(tile, 1), :]), src[:, c, SEQ:SEQ + taps - 1])
                    else:
                        STT(y[:, c, 0:SEQ], sp_, wc, y[:, c, 0:SEQ], ALU.mult, ALU.add)
                        last = STT(y[:, c, SEQ:], ss_, wc, y[:, c, SEQ:], ALU.mult, ALU.add)
                    if w_ < taps - 1:
                        dve.drain()
                return last

            with dve.Fori(0, 6) as i:
                for g in range(2):
                    bs, _ = grp("qkv", 2, g)
                    wait_group(dve, "qkv", g, i, 2)
                    for c in range(CT):
                        t = i * 4 + 2 * g + c
                        dve.wait_ge(conv_used, t + 1)
                        conv(bank[2 * bs + c], c, cin, cy, cst, t, V_WC, CONV, HI_S, QKV_T, cpt).then_inc(conv_y, 1)
                    dve.drain()
                    dve.sem_inc(grp_free[bs], 1)
            with dve.Fori(0, 4) as i:
                for g in range(2):
                    bs, _ = grp("dsa", 2, g)
                    wait_group(dve, "dsa", g, i, 2)
                    for c in range(CT):
                        last = CP(row(dsa[:, ds(i * 4 + 2 * g + c, 1), :]), bank[2 * bs + c][:, 0:N])
                    dve.drain()
                    dve.sem_inc(grp_free[bs], 1)
            bs, _ = grp("small", 1, 0)
            wait_group(dve, "small", 0)
            CP(ikk[:, :], bank[0][:, 0:N])
            CP(sm_a[:, :], bank[1][0:H, 0:N])
            CP(sm_b[:, :], bank[1][32:32 + H, 0:N])
            CP(sm_iw[:, :], bank[1][64:64 + H, 0:N])
            dve.drain()
            dve.sem_inc(grp_free[bs], 1)
            dve.sem_inc(small_done, 1)

            dve.wait_ge(row_act, 1)
            STT(sm_t[:, 1, :], sm_t[:, 0, :], 0.0, sm_a[:, :], ALU.max, ALU.add)
            S_(sm_b[:, :], sm_b[:, :], 1.0, None, ALU.add)
            dve.drain()
            V.memset(sm_t[:, 0, :], 1.0)
            S_(sm_t[:, 1, :], sm_t[:, 1, :], heads_v[:, 0:1], -1.0, ALU.mult, ALU.mult)
            V.reciprocal(rows[:, 1, :], sm_b[:, :])
            dve.drain()
            for c in range(2):
                V.tensor_tensor_scan(rows[:, 0, c * P:(c + 1) * P], sm_t[:, 0, 0:P], sm_t[:, 1, c * P:(c + 1) * P], 0.0,
                                     ALU.mult, ALU.add)
            CP(rows[:, 0, SEQ:SEQ + DB], sm_t[:, 1, SEQ:SEQ + DB])
            for t in range(1, TS):
                dve.drain()
                o_ = SEQ + t * DB
                T_(rows[:, 0, o_:o_ + DB], rows[:, 0, o_ - DB:o_], sm_t[:, 1, o_:o_ + DB], ALU.add)
            dve.drain()
            for c in range(2):
                S_(rows[:, 3, c * P:(c + 1) * P], rows[:, 0, c * P:(c + 1) * P], rows[:, 0, (c + 1) * P - 1:(c + 1) * P], None, ALU.subtract)
            T_(rows[:, 3, SEQ:].rearrange("p (t b) -> p t b", b=DB), rows[:, 0, SEQ:].rearrange("p (t b) -> p t b", b=DB),
               rows[:, 0, N - DB:N].unsqueeze(1).to_broadcast([H, TS, DB]), ALU.subtract).then_inc(row_dve, 1)
            dve.wait_ge(row_tr, 1)
            for t_, bk in ((gc_t, 2), (ke_t, 3)):
                CP(t_[:, 0:2, :].rearrange("p c h -> p (c h)"), bank[bk][:, 0:2 * H])
                CP(t_[0:NS, 2, :], bank[bk][0:NS, 2 * H:3 * H])
            dve.drain()

            def head_rows(hr):
                S_(rows_m[:, :, :], rows[:, 0:3, :], sel[0:H, ds(hr, 1)], None, ALU.mult).then_inc(G["rowm"], 1)

            def head_qk(hr, n):
                dve.wait_ge(G["nrm"], n)
                STT(qk[:, 0, :], row(qkv[:, ds(hr, 1), :]), DK ** -0.5, nrm[:, 0, :], ALU.mult, ALU.mult)
                T_(qk[:, 1, :], row(qkv[:, ds(hr + H, 1), :]), nrm[:, 1, :], ALU.mult).then_inc(G["qk"], 1)

            dve.sem_inc(G["spout"], 16)
            dve.sem_inc(G["ssout"], 16)
            head_rows(0)
            head_qk(0, 1)
            with dve.Fori(0, H) as h:
                v_h = row(qkv[:, ds(h + 2 * H, 1), :])

                def level_mask(l):
                    T_(bt_p[:, l % 2, :, :], at_p[:, :, :], lev[:, l, :].unsqueeze(1).to_broadcast([P, 2, P]), ALU.mult)

                dve.wait_ge(G["br"], h + 1)
                for c in range(2):
                    S_(e_p[:, c, :], br[:, 0, c * P:(c + 1) * P], gc_t[:, c, ds(h, 1)], 0.0, ALU.subtract, ALU.min)
                S_(e_s[:, :], br[0:NS, 0, SEQ:], gc_t[0:NS, 2, ds(h, 1)], 0.0, ALU.subtract, ALU.min)
                dve.drain()
                dve.sem_inc(G["e"], 1)
                dve.wait_ge(G["d"], h + 1)
                T_(e_p[:, :, :], e_p[:, :, :], cv["incl"].unsqueeze(1).to_broadcast([P, 2, P]), ALU.mult)
                T_(e_s[:, :], e_s[:, :], smask[0:NS, 0, :], ALU.mult)
                dve.drain()
                dve.wait_ge(G["gram"], h + 1)
                g_p = bank[2][:, :].rearrange("p (c m n) -> p c m n", c=2, m=2)
                T_(at_p[:, :, :], g_p[:, :, 1, :], e_p[:, :, :], ALU.mult)
                T_(at_s[:, :], bank[3][0:NS, NS:2 * NS], e_s[:, :], ALU.mult)
                T_(qkd_p[:, :, :], g_p[:, :, 0, :], e_p[:, :, :], ALU.mult)
                T_(qkd_s[:, :], bank[3][0:NS, 0:NS], e_s[:, :], ALU.mult)
                dve.drain()
                T_(at_p[:, :, :], at_p[:, :, :], br[:, 1, 0:SEQ].rearrange("p (c n) -> p c n", c=2), ALU.mult)
                T_(at_s[:, :], at_s[:, :], br[0:NS, 1, SEQ:], ALU.mult)
                dve.drain()
                T_(tt[:, 0:2, :], at_p[:, :, :], lev[:, 0, :].unsqueeze(1).to_broadcast([P, 2, P]), ALU.mult)
                T_(tt_s[:, 0, :], at_s[:, :], smask[0:NS, 1, :], ALU.mult)
                dve.drain()
                T_(tt[:, 0:2, :], ident.unsqueeze(1).to_broadcast([P, 2, P]), tt[:, 0:2, :], ALU.subtract)
                T_(tt_s[:, 0, :], ident[0:NS, 0:NS], tt_s[:, 0, :], ALU.subtract)
                dve.drain()
                dve.sem_inc(G["t1"], 1)
                level_mask(1)
                T_(bt_s[:, :], at_s[:, :], smask[0:NS, 2, :], ALU.mult)
                dve.wait_ge(G["t1t"], h + 1)
                CP(tt[:, 2:4, :].rearrange("p c n -> p (c n)"), bank[3][:, 0:2 * P])
                CP(tt_s[:, 1, :], bank[3][0:NS, 2 * P:2 * P + NS])
                dve.drain()
                dve.sem_inc(G["t"], 1)
                for l in range(1, LV):
                    if l < LV - 1:
                        level_mask(l + 1)
                    if l == 1:
                        dve.wait_ge(G["kss"], h + 1)
                        T_(o_add[:, :], bank[6][:, 0:NS], br[:, 2, SEQ:], ALU.mult)
                        T_(r_ts[:, :], bank[6][:, NS:2 * NS], br[:, 2, SEQ:], ALU.mult)
                        T_(r_t[:, :], v_h[:, 0:P], br[:, 1, 0:P], ALU.mult)
                        dve.drain()
                        T_(r_ts[:, :], v_h[:, SEQ:], r_ts[:, :], ALU.subtract)
                    if l == 2:
                        T_(r_ts[:, :], r_ts[:, :], br[:, 1, SEQ:], ALU.mult)
                        T_(qdec[:, :], qk[:, 0, P:2 * P], br[:, 2, P:2 * P], ALU.mult)
                        dve.wait_ge(G["kt"], h + 1)
                        for c in range(2):
                            S_(kend[:, c, :], bank[7][:, c * P:(c + 1) * P], ke_t[:, c, ds(h, 1)], None, ALU.mult)
                        S_(kend_s[:, :], bank[7][0:NS, 2 * P:3 * P], ke_t[0:NS, 2, ds(h, 1)], None, ALU.mult)
                    if l == 3:
                        T_(kmask[:, :, :], kend_s[:, :].unsqueeze(1).to_broadcast([NS, DB, P]),
                           cv["bcol"][0:NS, :].unsqueeze(2).to_broadcast([NS, DB, P]), ALU.mult)
                    if l == 4:
                        dve.sem_inc(G["kend"], 1)
                        dve.wait_ge(G["ssout"], h * 16 + 16)
                        T_(st_out[:, :, :], st_in[:, :, :], br[:, 2, N - DB:N].unsqueeze(2).to_broadcast([P, DB, P]), ALU.mult)
                    if l == 5:
                        cond_copy("ada2", 0, 1, h, 2)
                    dve.wait_ge(G["dt"], h * (LV - 1) + l)
                    w_ = 4 if l < LV - 1 else 2
                    tv = tt[:, 0:w_, :].rearrange("p c n -> p (c n)")
                    T_(tv, tv, bank[5][:, 0:w_ * P], ALU.subtract)
                    if l == 1:
                        T_(tt_s[:, 0, :], tt_s[:, 0, :], bank[3][0:NS, 0:NS], ALU.subtract)
                    dve.drain()
                    dve.sem_inc(G["t"], 1)
                cond_bias("ada2", 0, 1, h, 2)
                dve.wait_ge(G["spout"], h * 16 + 16)
                dve.wait_ge(G["sa"], h + 1)
                CP(st_p[:, :], bank[3][:, 0:P])
                dve.drain()
                dve.sem_inc(G["S1"], 1)
                dve.wait_ge(G["ks"], h + 1)
                T_(r_t[:, :], bank[4][:, 0:P], br[:, 2, P:2 * P], ALU.mult)
                dve.drain()
                T_(r_t[:, :], v_h[:, P:2 * P], r_t[:, :], ALU.subtract)
                dve.drain()
                T_(r_t[:, :], r_t[:, :], br[:, 1, P:2 * P], ALU.mult)
                dve.drain()
                dve.sem_inc(G["rb"], 1)
                for m, bk in enumerate((5, 7)):
                    dve.wait_ge(G["ssm"], h * 2 + m + 1)
                    so = st_out[:, 4 * m:4 * m + 4, :].rearrange("p b n -> p (b n)")
                    T_(so, so, bank[bk][:, :], ALU.add)
                dve.wait_ge(G["sb"], h + 1)
                CP(o_b[:, 0:SEQ], bank[2][:, 0:SEQ])
                T_(o_b[:, SEQ:], bank[2][:, SEQ:N], o_add[:, :], ALU.add)
                STT(st_p[:, :], st_p[:, :], br[:, 2, SEQ - 1:SEQ], bank[3][:, 0:P], ALU.mult, ALU.add)
                dve.drain()
                dve.sem_inc(G["o"], 1)
                hn = (h + 1) & (H - 1)
                head_rows(hn)
                cond_copy("ada2", 1, 1, h, 2)
                head_qk(hn, h + 2)
                STT(o_b[:, :], o_b[:, :], vec[:, V_GN:V_GN + 1], nrm[:, 2, :], ALU.mult, ALU.mult)
                dve.drain()
                T_(o_b[:, :], o_b[:, :], row(z[:, ds(h, 1), :]), ALU.mult)
                dve.drain()
                CP(row(og_hi[:, ds(h, 1), :]), o_b[:, :])
                dve.drain()
                T_(row(og_lo[:, ds(h, 1), :]), o_b[:, :], row(og_hi[:, ds(h, 1), :]).bitcast(f32), ALU.subtract)
                cond_bias("ada2", 1, 1, h, 2)
            dve.drain()
            dve.wait_ge(G["spout"], H * 16 + 16)
            dve.wait_ge(G["ssout"], H * 16 + 16)
            dve.wait_ge(G["br"], H + 1)
            dve.sem_inc(G["dve"], 1)

            turned = [(dsa[:, QH + m, :], 0) for m in range(KV)] + [(dsa[:, 12 + m, :], 1) for m in range(4)] + [(ikk[:, :], 1)]
            for n, (t_, kind) in enumerate(turned):
                dve.wait_ge(X["rot"], n + 1)
                T_(rot_t[:, :], bank[2 + n % 2][:, 0:N], rope[:, 2 * kind + 1, :], ALU.mult)
                T_(t_, t_, rope[:, 2 * kind, :], ALU.mult)
                dve.drain()
                T_(t_, t_, rot_t[:, :], ALU.add)
                dve.drain()
                dve.sem_inc(X["rotd"], 1)
            dve.wait_ge(G["sin"], 16 * (H + 1))
            V.memset(vtok_s[:, :], 0.0)
            V.memset(pn_t[:, :], 0.0)
            for m in range(4):
                T_(iqm[:, m, :, :], dsa[:, 12 + m, SEQ:].unsqueeze(1).to_broadcast([P, DB, NS]), maskb, ALU.mult)
            dve.wait_ge(X["load"], 16 * (1 + 3 * DB * (PAST // PAGE)))
            CP(ik_c[:, :, PAST:L_S], ikk[:, SEQ:].rearrange("p (t b) -> p b t", b=DB))
            for m in range(KV):
                CP(kt_c[:, :, m, PAST:L_S], dsa[:, QH + m, SEQ:].rearrange("p (t b) -> p b t", b=DB))
            dve.drain()
            dve.sem_inc(X["newk"], 1)
            dve.wait_ge(X["vtd"], 1)
            for n in range(3 * IH):
                dve.wait_ge(X["rel"], n + 1)
                h_ = n % IH
                if n < 2 * IH:
                    out_, in_, w_ = sc_p[:, n // IH, :], rel[:, n % 2, 0:SEQ], iw_t[:, n // IH, h_:h_ + 1]
                else:
                    out_, in_, w_ = sc_s[:, :], rel[0:NS, n % 2, :], iw_s[:, h_:h_ + 1]
                if h_ == 0:
                    S_(out_, in_, w_, None, ALU.mult)
                else:
                    STT(out_, in_, w_, out_, ALU.mult, ALU.add)
                dve.drain()
                dve.sem_inc(X["acc"], 1)
            T_(sc_p[:, :, :], sc_p[:, :, :], causal, ALU.min)
            T_(sc_s[:, :], sc_s[:, :], causal_s[0:NS, :], ALU.min)
            dve.drain()
            sets = [(sc_p[:, 0, :], wk_p[:, 0, :], top8[:, 0, :]), (sc_p[:, 1, :], wk_p[:, 1, :], top8[:, 1, :]),
                    (sc_s[:, :], wk_s[:, :], top8[0:NS, 2, :])]
            for r in range(TOPK_P // 8):
                for s_, w_, t8 in sets:
                    V.max(out=t8, in_=w_ if r else s_)
                dve.drain()
                for s_, w_, t8 in sets:
                    V.match_replace(out=w_, in_to_replace=t8, in_values=w_ if r else s_, imm_value=NEG_TAKEN)
                dve.drain()
            s_, w_, t8 = sets[2]
            V.max(out=t8, in_=w_)
            dve.drain()
            V.memset(t8[:, TOPK_S - TOPK_P:], -NEG_TAKEN)
            dve.drain()
            V.match_replace(out=w_, in_to_replace=t8, in_values=w_, imm_value=NEG_TAKEN)
            dve.drain()
            T_(wk_p[:, :, :], wk_p[:, :, :], sc_p[:, :, :], ALU.not_equal)
            T_(wk_s[:, :], wk_s[:, :], sc_s[:, :], ALU.not_equal)
            dve.drain()
            S_(sc_p[:, :, :], causal, 0.0, None, ALU.is_gt)
            S_(sc_s[:, :], causal_s[0:NS, :], 0.0, None, ALU.is_gt)
            dve.drain()
            T_(wk_p[:, :, :], wk_p[:, :, :], sc_p[:, :, :], ALU.mult)
            T_(wk_s[:, :], wk_s[:, :], sc_s[:, :], ALU.mult)
            dve.drain()
            S_(bias_p[:, 0:P], wk_p[:, 0, 0:P], BIG, -BIG, ALU.mult, ALU.add)
            S_(bias_p[:, P:], wk_p[:, 1, :], BIG, -BIG, ALU.mult, ALU.add)
            S_(bias_s[:, :], wk_s[:, :], BIG, -BIG, ALU.mult, ALU.add)
            dve.drain()

            with dve.Fori(0, QH) as h:
                q_h = row(dsa[:, ds(h, 1), :])
                dve.wait_ge(X["rotq"], h + 1)
                T_(rtmp[:, :], bank[2][:, 0:N], rope[:, 1, :], ALU.mult)
                T_(q_r[:, :], q_h, rope[:, 0, :], ALU.mult)
                dve.drain()
                T_(q_r[:, :], q_r[:, :], rtmp[:, :], ALU.add)
                dve.drain()
                T_(q_m[:, :, :], q_r[:, SEQ:].unsqueeze(1).to_broadcast([P, DB, NS]), maskb, ALU.mult)
                dve.drain()
                dve.sem_inc(X["q"], 1)
                dve.wait_ge(X["s"], h + 1)
                T_(s_p[:, :], bank[3][:, 0:P + SEQ], bias_p[:, :], ALU.add)
                T_(s_s[:, :], bank[4][0:NS, 0:L_S], bias_s[:, :], ALU.add)
                dve.drain()
                V.tensor_reduce(stat[:, 2, 0:1], s_p[:, 0:P], AX.X, ALU.max)
                V.tensor_reduce(stat[:, 2, 1:2], s_p[:, P:], AX.X, ALU.max)
                V.tensor_reduce(stat[0:NS, 2, 2:3], s_s[:, :], AX.X, ALU.max)
                dve.drain()
                S_(stat[:, 0, 0:2], stat[:, 2, 0:2], -(HD ** -0.5), None, ALU.mult)
                S_(stat[0:NS, 0, 2:3], stat[0:NS, 2, 2:3], -(HD ** -0.5), None, ALU.mult)
                dve.drain()
                dve.sem_inc(X["m"], 1)
                dve.wait_ge(X["p"], h + 1)
                T_(pn[:, :].rearrange("p (t b) -> p t b", b=DB), s_s[:, PAST:].unsqueeze(2).to_broadcast([NS, TS, DB]),
                   smask[0:NS, 3, :].rearrange("p (t b) -> p t b", b=DB), ALU.mult)
                V.reciprocal(stat[:, 3, 0:2], stat[:, 1, 0:2])
                V.reciprocal(stat[0:NS, 3, 2:3], stat[0:NS, 1, 2:3])
                dve.drain()
                dve.sem_inc(X["pn"], 1)
                dve.wait_ge(X["pt"], h + 1)
                for g in range(2):
                    T_(p_tm[:, g, :, :], bank[6][:, g * NS:(g + 1) * NS].unsqueeze(1).to_broadcast([P, DB, NS]), maskb, ALU.mult)
                CP(pn_t[0:NS, :], bank[6][0:NS, 2 * NS:3 * NS])
                dve.drain()
                dve.sem_inc(X["ptm"], 1)
                dve.wait_ge(X["o"], h + 1)
                for c in range(2):
                    S_(o_n[:, c, :], bank[7][:, c * P:(c + 1) * P], stat[:, 3, c:c + 1], None, ALU.mult)
                S_(o_ns[:, :], bank[2][0:NS, 0:P], stat[0:NS, 3, 2:3], None, ALU.mult)
                dve.drain()
                dve.sem_inc(X["on"], 1)
                cond_copy("ada2", 2 * H, 1, h, 2)
                dve.wait_ge(X["ot"], h + 1)
                CP(row(do_hi[:, ds(h, 1), :]), bank[3][:, 0:N])
                dve.drain()
                T_(row(do_lo[:, ds(h, 1), :]), bank[3][:, 0:N], row(do_hi[:, ds(h, 1), :]).bitcast(f32), ALU.subtract)
                dve.drain()
                cond_bias("ada2", 2 * H, 1, h, 2)
                cond_copy("ada2", 2 * H + 1, 1, h, 2)
                cond_bias("ada2", 2 * H + 1, 1, h, 2)
                dve.sem_inc(X["end"], 1)

            dve.wait_ge(out_done, 16 * 5)
            with dve.Fori(0, 4) as i:
                for g0 in range(2):
                    for which in range(2):
                        bs, _ = grp("out", 4, 4 * g0 + 2 + which)
                        dve.wait_ge(g_sig, (i * 2 + g0) * 2 + which + 1)
                        wait_group(dve, "out", 4 * g0 + 2 + which, i, 8)
                        for c in range(CT):
                            T_(mt[:, c, :] if which == 0 else sg[:, 1, c, :], bank[2 * bs + c][:, 0:N], sg[:, which, c, :], ALU.mult)
                        dve.drain()
                        dve.sem_inc(grp_free[bs], 1)
                    for c in range(CT):
                        T_(mt[:, c, :], mt[:, c, :], sg[:, 1, c, :], ALU.add)
                    dve.drain()
                    for c in range(CT):
                        CP(row(mix[:, ds(i * 4 + 2 * g0 + c, 1), :]), mt[:, c, :])
                    dve.drain()
                    for c in range(CT):
                        k = i * 4 + 2 * g0 + c
                        T_(row(mix_lo[:, ds(k, 1), :]), mt[:, c, :], row(mix[:, ds(k, 1), :]).bitcast(f32), ALU.subtract)
                    dve.drain()
                    dve.sem_inc(mix_done, 1)

            def residual(psum, t, gate_tile, tmp):
                xt, gt = row(x[:, ds(t, 1), :]), row(ada[:, ds(gate_tile, 1), :])
                STT(xt[:, 0:SEQ], psum[:, 0:SEQ], gt[:, 0:1], xt[:, 0:SEQ], ALU.mult, ALU.add)
                T_(tmp.rearrange("p (t b) -> p t b", b=DB), psum[:, SEQ:N].rearrange("p (t b) -> p t b", b=DB),
                   gt[:, 1:NC].unsqueeze(1).to_broadcast([P, TS, DB]), ALU.mult)
                dve.drain()
                return T_(xt[:, SEQ:], xt[:, SEQ:], tmp, ALU.add)

            dve.wait_ge(x_back, 16)
            with dve.Fori(0, 2) as i:
                for g in range(4):
                    bs, _ = grp("wo", 4, g)
                    wait_group(dve, "wo", g, i, 4)
                    for c in range(CT):
                        t = i * 8 + 2 * g + c
                        residual(bank[2 * bs + c], t, t + 2 * KT, mt[:, c, 0:NS]).then_inc(x_done, 1)
                    dve.drain()
                    dve.sem_inc(grp_free[bs], 1)
            scale_shift(1, 1)
            dve.drain()
            V.memset(fin[:, :, 0:FCONV - 1], 0.0)
            dve.wait_ge(const_in, 80)

            def ffn_gate(g, idx, half, i, per):
                bs, _ = grp("ffn", 4, g)
                wait_group(dve, "ffn", g, idx, per)
                for c in range(CT):
                    t = i * FC + 2 * half + c
                    conv(bank[2 * bs + c], c, fin, fy, fst, t, V_WF, FCONV, HI_F, 2 * FT, fpt)
                    dve.drain()
                    dve.sem_inc(conv_y, 1)
                dve.sem_inc(grp_free[bs], 1)

            def ffn_val(g, idx, half, i, per):
                bs, _ = grp("ffn", 4, g)
                wait_group(dve, "ffn", g, idx, per)
                for c in range(CT):
                    t = i * FC + 2 * half + c
                    dve.wait_ge(sil_done, t + 1)
                    conv(bank[2 * bs + c], c, fin, fy, fst, t + FT, V_WF, FCONV, HI_F, 2 * FT, fpt)
                    dve.drain()
                    STT(act_f[:, c, :], fy[:, c, :], vec[:, ds(t + FT + V_BF, 1)], fsil[:, c, :], ALU.add, ALU.mult)
                dve.drain()
                dve.sem_inc(grp_free[bs], 1)
                dst = (i & 1) * FC + 2 * half
                ah = act_hi[:, :, :, :].rearrange("p a c n -> p (a c) n")[:, ds(dst, CT), :]
                al = act_lo[:, :, :, :].rearrange("p a c n -> p (a c) n")[:, ds(dst, CT), :]
                CP(ah, act_f[:, :, :])
                dve.drain()
                T_(al, act_f[:, :, :], ah.bitcast(f32), ALU.subtract)
                dve.drain()
                dve.sem_inc(act_ready, 1)

            def ffn_down(g, idx, per):
                for m in range(KT // CT):
                    bs, _ = grp("ffn", 4, g + m)
                    wait_group(dve, "ffn", g + m, idx, per)
                    for c in range(CT):
                        residual(bank[2 * bs + c], 2 * m + c, 2 * m + c + 5 * KT, dtmp[:, :])
                        dve.drain()
                        dve.sem_inc(down_done, 1)
                    dve.sem_inc(grp_free[bs], 1)

            ffn_gate(0, 0, 0, 0, 0)
            ffn_val(1, 0, 0, 0, 0)
            ffn_gate(2, 0, 1, 0, 0)
            ffn_val(3, 0, 1, 0, 0)
            with dve.Fori(0, NCH - 1) as i:
                ffn_gate(4, i, 0, i + 1, 12)
                ffn_val(5, i, 0, i + 1, 12)
                ffn_down(6, i, 12)
                ffn_gate(14, i, 1, i + 1, 12)
                ffn_val(15, i, 1, i + 1, 12)
            ffn_down(4 + 12 * (NCH - 1), 0, 0)

            dve.wait_ge(rs_ready, 3)
            with dve.Fori(0, KT // 2) as i:
                for s_ in range(2):
                    k = i * 2 + s_
                    xt = row(x[:, ds(k, 1), :])
                    last = STT(xt, xt, vec[:, ds(k + V_GF, 1)], rsb[:, :], ALU.mult, ALU.mult)
                dve.drain()
                dve.sem_inc(y_ready, 1)

        @block.tensor
        def _(pe):
            MM = nc.tensor.matmul
            row = lambda a: a.rearrange("p k n -> p (k n)")

            def tr(out, in_, n):
                return nc.tensor.transpose(out, in_, ident[0:n, 0:n])

            def wait_rest(name, j, i, per):
                _, cnt = split_at(name, j, i, per)
                if name != "ada1":
                    pe.wait_ge(lo_ready, cnt + (1 - LO_DVE))
                elif j % 2 == 0:
                    pe.wait_ge(lo_ready, i * (per // 2) + (j // 2 + 1))
                else:
                    pe.wait_ge(lo_dve, i * (per // 2) + (j // 2 + 1))

            def cond(name, g, sets, s_, i=0, per=0):
                j = 4 * g + s_
                if s_ == 0:
                    n0 = g + (2 * KT // CT if name == "ada2" else 0)
                    pe.wait_ge(cond_cp, i * per + (n0 + 3 - sets))
                r, _ = raw_at(name, j, i, 4 * per)
                q, n = split_at(name, j, i, 4 * per)
                out = bank[2 * (g % sets)]
                pe.wait_ge(hi_ready, n + 1)
                for k in range(KS):
                    MM(out[0:2 * NCP, 0:CT * P], cact[:, s_ * KS + k, :, :].rearrange("p m n -> p (m n)"), w_hi[q][:, k, :],
                       start=(s_ == 0 and k == 0), stop=False)
                wait_rest(name, j, i, 4 * per)
                for k in range(KS):
                    last = MM(out[0:NCP, 0:CT * P], cact[:, s_ * KS + k, 0, :], rest[r][:, k, :],
                              start=False, stop=(s_ * KS + k == KT - 1))
                    if k == 0:
                        last.then_inc(ring_free, 1)
                last.then_inc(raw_free[r], 1)

            def turn(name, g, sets, i=0, per=0):
                n0 = g + (2 * KT // CT if name == "ada2" else 0)
                bs, cnt = grp(name, sets, g, i, per)
                pe.wait_ge(cond_cp, i * per + (n0 + 3))
                pe.wait_ge(grp_free[bs], cnt + 1)
                for c in range(CT):
                    last = MM(bank[2 * bs + 1][:, c * NCP:(c + 1) * NCP], cond_t[:, c * P:(c + 1) * P],
                              cv["fold"][0:2 * NCP, :], start=True, stop=True)
                last.then_inc(cond_done, 1)

            def slot(name, j, hi_of, lo_of, banks, first, last_, i=0, per=0):
                r, _ = raw_at(name, j, i, per)
                q, cnt = split_at(name, j, i, per)
                pe.wait_ge(hi_ready, cnt + 1)
                for k in range(KS):
                    for c in range(CT):
                        w_ = w_hi[q][:, k, c * P:(c + 1) * P]
                        MM(banks[c][:, 0:N], w_, hi_of(k), start=(first and k == 0), stop=False)
                        ins = MM(banks[c][:, 0:N], w_, lo_of(k), start=False, stop=False)
                wait_rest(name, j, i, per)
                for k in range(KS):
                    for c in range(CT):
                        ins = MM(banks[c][:, 0:N], rest[r][:, k, c * P:(c + 1) * P], hi_of(k),
                                 start=False, stop=(last_ and k == KS - 1))
                        if k == 0 and c == 0:
                            ins.then_inc(ring_free, 1)
                ins.then_inc(raw_free[r], 1)

            def group(name, sets, g, j0, nslots, hi_t, lo_t, i=0, per_g=0, per_j=0, k0=0):
                bs, cnt = grp(name, sets, g, i, per_g)
                banks = (bank[2 * bs], bank[2 * bs + 1])
                pe.wait_ge(grp_free[bs], cnt + 1)
                for s_ in range(nslots):
                    slot(name, j0 + s_, lambda k: hi_t(s_ * KS + k), lambda k: lo_t(s_ * KS + k), banks,
                         s_ == 0, s_ == nslots - 1, i, per_j)

            hh, hl = (lambda k: h_hi[:, k, :]), (lambda k: h_lo[:, k, :])

            def norm_part(n, s_, i=0):
                pe.wait_ge(sq_ready, 2 * i + (n * KT + s_ + 1))
                MM(bank[7][:, 0:N], ones, sq[:, s_ % 2, :], start=(s_ == 0), stop=(s_ == KT - 1)).then_inc(sq_used, 1)

            def norm_sum_all(n):
                for s_ in range(KT if n else 0):
                    norm_part(n, s_)
                pe.wait_ge(sq_used, (n + 1) * KT + 2)
                pe.sem_inc(ssq_ready, 1)

            pe.wait_ge(const_in, 48)
            pe.wait_ge(c_ready, 2)

            def ada1_pair(first, i=0):
                for g in (first, first + 1):
                    for s_ in range(KT // KS):
                        cond("ada1", g, 2, s_, i, 2)
                        if s_ == 1 and g > 0:
                            turn("ada1", g - 1, 2, i, 2)
                    norm_part(0, g, i)

            ada1_pair(0)
            with pe.Fori(0, KT // CT - 2) as i:
                ada1_pair(2, i)
            ada1_pair(KT - 2)
            turn("ada1", KT - 1, 2)
            norm_sum_all(0)
            pe.wait_ge(h_lo_ready, KT + 2)
            pe.wait_ge(h_hi_ready, KT)
            with pe.Fori(0, 6) as i:
                for g in range(2):
                    group("qkv", 2, g, 4 * g, 4, hh, hl, i, 2, 8)
            with pe.Fori(0, 2) as i:
                for g in range(2):
                    group("z", 2, g, 4 * g, 4, hh, hl, i, 2, 8)
            with pe.Fori(0, 4) as i:
                for g in range(2):
                    group("dsa", 2, g, 4 * g, 4, hh, hl, i, 2, 8)
            group("small", 1, 0, 0, 4, hh, hl)

            pe.wait_ge(row_act, 2)
            for m, bk in ((0, 2), (3, 3)):
                for c in range(3):
                    w_ = P if c < 2 else NS
                    ins = tr(bank[bk][0:w_, c * H:(c + 1) * H], rows[:, m, c * P:c * P + w_], H)
            ins.then_inc(row_tr, 1)

            def head_sums(n, last_o):
                pe.wait_ge(G["rowm"], n)
                pe.wait_ge(G["sq"], n)
                if last_o:
                    MM(bank[7][:, 0:N], ones, sqb[:, 2, :], start=True, stop=True)
                MM(bank[2][:, 0:N], ones, sqb[:, 0, :], start=True, stop=True)
                MM(bank[3][:, 0:N], ones, sqb[:, 1, :], start=True, stop=True).then_inc(G["ssq"], 1)
                for m in range(3):
                    ins = MM(bank[4 + m][:, 0:N], ones[0:H, :], rows_m[:, m, :], start=True, stop=True)
                ins.then_inc(G["bc"], 1)

            head_sums(1, False)
            with pe.Fori(0, H) as h:
                def fill(n):
                    cond("ada2", n // 4, 1, n % 4, h, 2)
                pe.wait_ge(G["qk"], h + 1)
                for c in range(2):
                    MM(bank[2][:, c * 2 * P:(c + 1) * 2 * P].rearrange("p (m n) -> p m n", m=2), qk[:, 1, c * P:(c + 1) * P],
                       qk[:, :, c * P:(c + 1) * P], start=True, stop=True)
                MM(bank[3][0:NS, 0:2 * NS].rearrange("p (m n) -> p m n", m=2), qk[:, 1, SEQ:], qk[:, :, SEQ:],
                   start=True, stop=True).then_inc(G["gram"], 1)
                for c in range(2):
                    tr(bank[7][:, c * P:(c + 1) * P], qk[:, 1, c * P:(c + 1) * P], P)
                tr(bank[7][0:NS, 2 * P:3 * P], qk[:, 1, SEQ:], P).then_inc(G["kt"], 1)
                pe.wait_ge(G["sin"], h * 16 + 16)
                pe.wait_ge(G["br"], h + 1)
                for b in range(DB):
                    v2 = lambda a: a.rearrange("p m (t b) -> p m t b", b=DB)[:, :, :, b]
                    ins = MM(v2(bank[6][:, 0:2 * NS].rearrange("p (m n) -> p m n", m=2)), st_in[:, b, :], v2(qk[:, :, SEQ:]),
                             start=True, stop=True)
                ins.then_inc(G["kss"], 1)
                pe.wait_ge(G["t1"], h + 1)
                for c in range(2):
                    tr(bank[3][:, c * P:(c + 1) * P], tt[:, c, :], P)
                tr(bank[3][0:NS, 2 * P:2 * P + NS], tt_s[:, 0, :], NS).then_inc(G["t1t"], 1)
                for l in range(1, LV):
                    pe.wait_ge(G["t"], h * LV + l)
                    for c in range(2):
                        if l == 1 and c == 1:
                            MM(bank[4][0:NS, 2 * P:2 * P + NS], bt_s[:, :], tt_s[:, 1, :], start=True, stop=True)
                        ins = MM(bank[4][:, c * P:(c + 1) * P], bt_p[:, l % 2, c, :], tt[:, 2 + c, :], start=True, stop=True)
                    ins.then_inc(G["x"], 1)
                    fill(l - 1)
                    if l == LV - 1:
                        turn("ada2", 0, 1, h, 2)
                    pe.wait_ge(G["xs"], h * (LV - 1) + l)
                    for c in range(2):
                        if l == 1 and c == 1:
                            MM(bank[3][0:NS, 0:NS], x_s[:, :], tt_s[:, 0, :], start=True, stop=True)
                        ins = MM(bank[5][:, c * P:(c + 1) * P], x_p[:, c, :], tt[:, c, :], start=True, stop=True)
                    if l < LV - 1:
                        for c in range(2):
                            ins = MM(bank[5][:, (2 + c) * P:(3 + c) * P], tt[:, c, :], x_p[:, c, :], start=True, stop=True)
                    ins.then_inc(G["dt"], 1)
                pe.wait_ge(G["t"], h * LV + LV)
                pe.wait_ge(G["kend"], h + 1)
                tr(bank[6][0:NS, P:2 * P], r_ts[:, :], P)
                tr(bank[6][:, 0:P], r_t[:, :], P).then_inc(G["rt"], 1)
                pe.wait_ge(G["rs"], h * 2 + 1)
                MM(bank[6][:, 0:P], tt[:, 0, :], r_p[:, :], start=True, stop=True)
                MM(bank[6][0:NS, P:2 * P], tt_s[:, 0, :], r_s[:, :], start=True, stop=True).then_inc(G["u"], 1)
                pe.wait_ge(G["us"], h * 2 + 1)
                MM(bank[3][:, 0:P], kend[:, 0, :], u_p[:, :], start=True, stop=True).then_inc(G["sa"], 1)
                MM(bank[2][:, 0:P], u_p[:, :], qkd_p[:, 0, :], start=True, stop=True)
                MM(bank[2][:, SEQ:N], u_s[:, :], qkd_s[:, :], start=True, stop=True)
                fill(6)
                pe.wait_ge(G["S1"], h + 1)
                MM(bank[4][:, 0:P], st_p[:, :], qk[:, 1, P:2 * P], start=True, stop=True).then_inc(G["ks"], 1)

                def sample_states(m):
                    for b in range(4):
                        ins = MM(bank[(5, 7)[m]][:, b * P:(b + 1) * P], kmask[:, 4 * m + b, :], u_s[:, :], start=True, stop=True)
                    ins.then_inc(G["ssm"], 1)

                sample_states(0)
                pe.wait_ge(G["rb"], h + 1)
                tr(bank[6][:, 0:P], r_t[:, :], P).then_inc(G["rt"], 1)
                sample_states(1)
                pe.wait_ge(G["rs"], h * 2 + 2)
                MM(bank[6][:, 0:P], tt[:, 1, :], r_p[:, :], start=True, stop=True).then_inc(G["u"], 1)
                MM(bank[2][:, P:2 * P], st_p[:, :], qdec[:, :], start=True, stop=False)
                pe.wait_ge(G["us"], h * 2 + 2)
                MM(bank[3][:, 0:P], kend[:, 1, :], u_p[:, :], start=True, stop=True)
                MM(bank[2][:, P:2 * P], u_p[:, :], qkd_p[:, 1, :], start=False, stop=True).then_inc(G["sb"], 1)
                fill(7)
                head_sums(h + 2, True)
                turn("ada2", 1, 1, h, 2)
            pe.wait_ge(G["dve"], 1)
            pe.wait_ge(G["br"], H + 1)

            turned = [(dsa[:, QH + m, :], 0) for m in range(KV)] + [(dsa[:, 12 + m, :], 1) for m in range(4)] + [(ikk[:, :], 1)]
            for n, (t_, kind) in enumerate(turned):
                if n >= 2:
                    pe.wait_ge(X["rotd"], n - 1)
                MM(bank[2 + n % 2][:, 0:N], rotm[:, kind, :], t_, start=True, stop=True).then_inc(X["rot"], 1)
            for c in range(2):
                for m in range(KV):
                    tr(bank[4][:, (c * KV + m) * P:(c * KV + m + 1) * P], dsa[:, QH + KV + m, c * P:(c + 1) * P], P)
            for m in range(KV):
                tr(bank[5][0:NS, m * P:(m + 1) * P], dsa[:, QH + KV + m, SEQ:], P)
            for c in range(3):
                w_ = P if c < 2 else NS
                ins = tr(bank[6][0:w_, c * IH:(c + 1) * IH], sm_iw[:, c * P:c * P + w_], IH)
            ins.then_inc(X["vt"], 1)
            pe.wait_ge(X["rotd"], len(turned))
            for n in range(3 * IH):
                if n >= 2:
                    pe.wait_ge(X["rel"], n - 1)
                h_ = n % IH
                pr = slice(ID * (h_ % 2), ID * (h_ % 2) + ID)
                if n < 2 * IH:
                    c = n // IH
                    ins = MM(bank[2 + n % 2][:, 0:SEQ], dsa[pr, 12 + h_ // 2, c * P:(c + 1) * P], ikk[pr, 0:SEQ], start=True, stop=True)
                else:
                    if n == 2 * IH:
                        pe.wait_ge(X["newk"], 1)
                    for b in range(DB):
                        ins = MM(bank[2 + n % 2][0:NS, 0:L_S], iqm[pr, h_ // 2, b, :], ik_c[pr, b, :], start=(b == 0), stop=(b == DB - 1))
                ins.then_inc(X["idx"], 1)
            pe.wait_ge(X["rel"], 3 * IH)
            with pe.Fori(0, QH) as h:
                def fill(n):
                    cond("ada2", 2 * H + n // 4, 1, n % 4, h, 2)
                kv = (h >> 2).with_bounds(min_val=0, max_val=KV - 1)
                MM(bank[2][:, 0:N], rotm[:, 0, :], row(dsa[:, ds(h, 1), :]), start=True, stop=True).then_inc(X["rotq"], 1)
                pe.wait_ge(X["q"], h + 1)
                kt_h = row(dsa[:, ds(kv + QH, 1), :])
                MM(bank[3][:, 0:P], q_r[:, 0:P], kt_h[:, 0:P], start=True, stop=True)
                MM(bank[3][:, P:P + SEQ], q_r[:, P:2 * P], kt_h[:, 0:SEQ], start=True, stop=True)
                for b in range(DB):
                    ins = MM(bank[4][0:NS, 0:L_S], q_m[:, b, :], row(kt_c[:, b, ds(kv, 1), :]), start=(b == 0), stop=(b == DB - 1))
                ins.then_inc(X["s"], 1)
                fill(0)
                fill(1)
                pe.wait_ge(X["p"], h + 1)
                pe.wait_ge(X["pn"], h + 1)
                tr(bank[5][:, 0:P], s_p[:, 0:P], P)
                tr(bank[5][:, P:2 * P], s_p[:, P:2 * P], P)
                tr(bank[5][:, 2 * P:3 * P], s_p[:, 2 * P:3 * P], P)
                for g in range(2):
                    tr(bank[6][:, g * NS:(g + 1) * NS], s_s[:, g * PAGE:(g + 1) * PAGE], NS)
                tr(bank[6][0:NS, 2 * NS:3 * NS], pn[:, :], NS).then_inc(X["pt"], 1)
                fill(2)
                pe.wait_ge(X["pts"], h + 1)
                pe.wait_ge(X["ptm"], h + 1)
                vt = lambda c: vtok[:, c, ds(kv * HD, HD)]
                MM(bank[7][:, 0:P], p_t[:, 0, :], vt(0), start=True, stop=True)
                MM(bank[7][:, P:2 * P], p_t[:, 1, :], vt(0), start=True, stop=False)
                MM(bank[7][:, P:2 * P], p_t[:, 2, :], vt(1), start=False, stop=True)
                for g in range(2):
                    for b in range(DB):
                        MM(bank[2][0:NS, 0:P], p_tm[:, g, b, :], v_c[:, b, g, ds(kv * HD, HD)], start=(g == 0 and b == 0), stop=False)
                MM(bank[2][0:NS, 0:P], pn_t[:, :], vtok_s[:, ds(kv * HD, HD)], start=False, stop=True).then_inc(X["o"], 1)
                fill(3)
                pe.wait_ge(X["on"], h + 1)
                for c in range(2):
                    tr(bank[3][:, c * P:(c + 1) * P], o_n[:, c, :], P)
                tr(bank[3][:, SEQ:N], o_ns[:, :], NS).then_inc(X["ot"], 1)
                fill(4)
                turn("ada2", 2 * H, 1, h, 2)
                fill(5)
                fill(6)
                fill(7)
                turn("ada2", 2 * H + 1, 1, h, 2)
                pe.wait_ge(X["end"], h + 1)

            oh, ol = (lambda k: og_hi[:, k, :]), (lambda k: og_lo[:, k, :])
            dh, dl = (lambda k: do_hi[:, k, :]), (lambda k: do_lo[:, k, :])
            with pe.Fori(0, 4) as i:
                for g0 in range(2):
                    j = 12 * g0
                    group("out", 4, 4 * g0, j, 4, hh, hl, i, 8, 24)
                    group("out", 4, 4 * g0 + 1, j + 4, 4, hh, hl, i, 8, 24)
                    group("out", 4, 4 * g0 + 2, j + 8, 2, oh, ol, i, 8, 24)
                    group("out", 4, 4 * g0 + 3, j + 10, 2, dh, dl, i, 8, 24)
            pe.wait_ge(mix_done, KT // CT + 1)
            mh, ml = (lambda k: mix[:, k, :]), (lambda k: mix_lo[:, k, :])
            with pe.Fori(0, 2) as i:
                for g in range(4):
                    group("wo", 4, g, 4 * g, 4, mh, ml, i, 4, 16)
            norm_sum_all(1)
            pe.wait_ge(h_lo_ready, 2 * KT + 2)
            pe.wait_ge(h_hi_ready, 2 * KT)

            def down(g, j, chunk, i, per_g, per_j):
                pe.wait_ge(act_ready, chunk * 2 + 2)
                par = (chunk & 1) * FC
                ah = act_hi[:, :, :, :].rearrange("p a c n -> p (a c) n")
                al = act_lo[:, :, :, :].rearrange("p a c n -> p (a c) n")
                for m in range(KT // CT):
                    group("ffn", 4, g + m, j + m, 1, lambda k: row(ah[:, ds(par + k, 1), :]), lambda k: row(al[:, ds(par + k, 1), :]),
                          i, per_g, per_j)

            for g in range(4):
                group("ffn", 4, g, 4 * g, 4, hh, hl)
            with pe.Fori(0, NCH - 1) as i:
                group("ffn", 4, 4, 16, 4, hh, hl, i, 12, 24)
                group("ffn", 4, 5, 20, 4, hh, hl, i, 12, 24)
                down(6, 24, i, i, 12, 24)
                group("ffn", 4, 14, 32, 4, hh, hl, i, 12, 24)
                group("ffn", 4, 15, 36, 4, hh, hl, i, 12, 24)
            down(4 + 12 * (NCH - 1), 16 + 24 * (NCH - 1), NCH - 1, 0, 0, 0)
            norm_sum_all(2)


def slots_of(w, tiles):
    k, c = w.shape
    a = w.reshape(k // (KS * P), KS, P, c // (CT * P), CT * P)
    return a.transpose(3, 0, 2, 1, 4).reshape(c // (CT * P), k // (KS * P), P, SLOT)


def feature_major(a):
    t, f = a.shape
    return np.ascontiguousarray(a.reshape(t, f // P, P).transpose(2, 1, 0))


def columns(v):
    return v.reshape(-1, P).T


def kernel(**inputs):
    import concourse.bacc as bacc
    from concourse.bass_utils import run_bass_kernel_spmd

    I = {k: np.asarray(v) for k, v in inputs.items()}
    w_in = I["w_in"][0]
    cuts = np.cumsum([QKV_T * P, Z_T * P, H, H, QH * HD, KV * HD, KV * HD, IH * ID, ID, IH, D_MODEL, D_MODEL])
    qkv_w, z_w, a_w, b_w, dq_w, dk_w, dv_w, iq_w, ik_w, iw_w, gg_w, gd_w = np.split(w_in, cuts[:-1], axis=1)
    pad = lambda w, n: np.concatenate([w, np.zeros((D_MODEL, n - w.shape[1]), w.dtype)], 1)
    small = np.concatenate([ik_w, ik_w, pad(a_w, 32), pad(b_w, 32), pad(iw_w, 64)], 1)
    parts = {}
    flat = lambda a: a.reshape(-1, P, SLOT)
    ada_s = slots_of(I["w_ada"][0], None)
    half = 2 * KT // CT
    parts["ada1"], parts["ada2"] = flat(ada_s[:half]), flat(ada_s[half:])
    parts["qkv"], parts["z"] = flat(slots_of(qkv_w, None)), flat(slots_of(z_w, None))
    parts["dsa"] = flat(slots_of(np.concatenate([dq_w, dk_w, dv_w, iq_w], 1), None))
    parts["small"] = flat(slots_of(small, None))
    parts["out"] = flat(np.concatenate([slots_of(gg_w, None), slots_of(gd_w, None),
                                        slots_of(I["w_gdn_out"][0], None), slots_of(I["w_dsa_out"][0], None)], 1))
    parts["wo"] = flat(slots_of(I["w_o"][0], None))
    up, dn = slots_of(I["w_up"][0], None), slots_of(I["w_down"][0], None)
    seq = []
    for i in range(NCH):
        g0, v0 = up[2 * i], up[FT // 2 + 2 * i]
        g1, v1 = up[2 * i + 1], up[FT // 2 + 2 * i + 1]
        seq += [g0, v0] + ([dn[:, i - 1]] if i else []) + [g1, v1]
    seq.append(dn[:, NCH - 1])
    parts["ffn"] = np.concatenate(seq)
    stream = np.concatenate([parts[n] for n, _ in PHASES])
    assert stream.shape == (NSLOTS, P, SLOT)

    time_major = lambda a: a.transpose(1, 0, 2).reshape(-1, a.shape[-1])
    c = constants()
    A = {
        "stream": stream,
        "x": feature_major(np.concatenate([I["x_prompt"][0], time_major(I["x_sample"])])).reshape(P, -1),
        "c": feature_major(np.concatenate([I["c_prompt"], I["c_sample"], np.zeros((NCP - NC, D_MODEL), np.float32)])).reshape(P, -1),
        "consts": np.concatenate([c[n].reshape(P, -1) for n in CONST_SIZE], 1),
        "vec": np.concatenate([columns(I["b_ada"][0]), columns(I["g_norm1"][0]), columns(I["g_norm2"][0]), columns(I["g_final"]),
                               columns(I["w_gdn_conv"][0]), columns(I["w_ffn_conv"][0]), columns(I["b_ffn_conv"][0]),
                               columns(I["g_gdn_norm"][0])], 1),
        "heads_v": np.stack([I["a_log"][0], I["dt_bias"][0]], 1),
        "ptab": I["page_table"].reshape(1, -1),
        "gdn_hist": feature_major(time_major(I["state_gdn_conv"][0])).reshape(P, -1),
        "ffn_hist": feature_major(time_major(I["state_ffn_conv"][0])).reshape(P, -1),
        "state": I["state_gdn"][0].transpose(1, 2, 0, 3).reshape(H, DK, DB * P),
        "ck": I["cache_k"][0].transpose(0, 3, 2, 1).reshape(NPOOL, HD, KV * PAGE),
        "cv": I["cache_v"][0].reshape(NPOOL, PAGE, KV * HD),
        "cik": np.concatenate([I["cache_idx_k"][0].transpose(0, 2, 1)] * 2, 1),
    }
    outs = {"y": (P, KT * N), "k": (P, KV * N), "v": (P, KV * N), "ik": (ID, N), "state_p": (H, DK, P),
            "state_s": (H, DK, DB * P), "gdn_tail_p": (P, QKV_T * (CONV - 1)), "gdn_tail_s": (P, QKV_T * HI_S),
            "ffn_tail_p": (P, 2 * FT * (FCONV - 1)), "ffn_tail_s": (P, 2 * FT * HI_F)}
    nc = bacc.Bacc("TRN2", target_bir_lowering=False, num_devices=1)
    arrays, aps, oaps = {}, {}, {}
    for name, a in A.items():
        a = np.ascontiguousarray(a)
        arrays[f"in_{name}"] = a
        aps[name] = nc.dram_tensor(f"in_{name}", a.shape, mybir.dt.from_np(a.dtype), kind="ExternalInput").ap()
    for name, shape in outs.items():
        oaps[name] = nc.dram_tensor(f"out_{name}", shape, mybir.dt.float32, kind="ExternalOutput").ap()
    decoder_step(nc, aps, oaps)
    r = run_bass_kernel_spmd(nc, [arrays], core_ids=[0])
    o = {name: r.results[0][f"out_{name}"] for name in outs}

    def tokens(a, tiles):
        return a.reshape(-1, tiles, N).transpose(2, 1, 0).reshape(N, -1)

    def split(a):
        return a[:SEQ], a[SEQ:].reshape(TS, DB, -1).transpose(1, 0, 2)

    def tails(a, n_cols):
        t = a.reshape(P, -1, n_cols)
        return t.transpose(2, 1, 0).reshape(n_cols, -1)

    yp, ys = split(tokens(o["y"], KT))
    kp, ks = split(tokens(o["k"], KV))
    vp, vs = split(tokens(o["v"], KV))
    ip, isa = split(tokens(o["ik"], 1))
    gs = tails(o["gdn_tail_s"], HI_S).reshape(CONV - 1, DB, -1).transpose(1, 0, 2)
    fs = tails(o["ffn_tail_s"], HI_F).reshape(FCONV - 1, DB, -1).transpose(1, 0, 2)
    ss = o["state_s"].reshape(H, DK, DB, P).transpose(2, 0, 1, 3)
    c_ = np.ascontiguousarray
    return (c_(yp[None]), c_(ys),
            c_(kp.reshape(1, 1, SEQ, KV, HD)), c_(vp.reshape(1, 1, SEQ, KV, HD)), c_(ip[None, None]),
            c_(o["state_p"][None, None]), c_(tails(o["gdn_tail_p"], CONV - 1)[None, None]),
            c_(tails(o["ffn_tail_p"], FCONV - 1)[None, None]),
            c_(ks.reshape(1, DB, TS, KV, HD)), c_(vs.reshape(1, DB, TS, KV, HD)), c_(isa[None]),
            c_(ss[None]), c_(gs[None]), c_(fs[None]))
```

```python
from contextlib import ExitStack

import numpy as np
import concourse.bass as bass
from concourse import mybir

P = 128
D_MODEL, SEQ, DB, TS = 2048, 256, 8, 4
PAGE, PAST, NPOOL = 128, 256, 20
H, DK, CONV = 8, 128, 4
QH, KV, HD = 8, 2, 128
IH, ID = 8, 64
D_FF, FCONV = 5632, 3
ROPE_THETA, EPS = 500000.0, 1e-6
NS = DB * TS
N = SEQ + NS
NC = 1 + DB
NCP = NC + NC % 2
KT = D_MODEL // P
KS, CT = 4, 2
SLOT = KS * CT * P
RAW, RAW_A = 8, 4
RING, RING_A = 4, 2
QKV_T, Z_T, DSA_T = 3 * H, H, 16
FT = D_FF // P
FC = 4
NCH = FT // FC
HB = 4
LV = 7
L_S = PAST + TS
TOPK_P, TOPK_S = min(256, SEQ // 4), min(256, L_S // 4)
IDX_SCALE = IH ** -0.5 * ID ** -0.5
NEG_MASK, NEG_TAKEN, BIG = -2.0e38, -3.0e38, 1.0e30
HI_S = (CONV - 1) * DB
HI_F = (FCONV - 1) * DB

V_BADA = 0
V_G1 = V_BADA + 6 * KT
V_G2 = V_G1 + KT
V_GF = V_G2 + KT
V_WC = V_GF + KT
V_WF = V_WC + CONV * QKV_T
V_BF = V_WF + FCONV * 2 * FT
V_GN = V_BF + 2 * FT
V_ALL = V_GN + 1

PHASES = [("ada1", 2 * KT // CT * (KT // KS)), ("small", KT // KS), ("qkv", QKV_T // CT * (KT // KS)), ("z", Z_T // CT * (KT // KS)),
          ("dsa", DSA_T // CT * (KT // KS)), ("ada2", 4 * KT // CT * (KT // KS)),
          ("out", (KT // CT) * (2 * (KT // KS) + 2 * (H // KS))), ("wo", KT // CT * (KT // KS)),
          ("ffn", NCH * 2 * FC // CT * (KT // KS) + (NCH - 1) * KT // CT), ("last", KT // CT)]
BASE = {}
_b = 0
for _n, _c in PHASES:
    BASE[_n] = _b
    _b += _c
NSLOTS = _b


def constants():
    f = np.float32
    c = {}
    c["ident"] = np.eye(P, dtype=f)
    c["ones"] = np.ones((P, P), f)
    j, i = np.meshgrid(np.arange(P), np.arange(P), indexing="ij")
    c["incl"] = (i >= j).astype(f)
    c["lev"] = np.stack([((i >> (l + 1)) == (j >> (l + 1))) & (((i >> l) & 1) == 1) & (((j >> l) & 1) == 0)
                         for l in range(LV)], 1).astype(f)
    js, is_ = np.meshgrid(np.arange(NS), np.arange(NS), indexing="ij")
    same = (js % DB) == (is_ % DB)
    tj, ti = js // DB, is_ // DB
    s = np.zeros((P, 4, NS), f)
    s[:NS, 0] = same & (ti >= tj)
    s[:NS, 1] = same & ((ti >> 1) == (tj >> 1)) & ((ti & 1) == 1) & ((tj & 1) == 0)
    s[:NS, 2] = same & ((ti >> 1) == 1) & ((tj >> 1) == 0)
    s[:NS, 3, :TS * DB] = (np.arange(NS)[:, None] % DB) == (np.arange(NS)[None, :] % DB)
    c["smask"] = s
    mb = (np.arange(NS)[None, :] % DB == np.arange(DB)[:, None]).astype(f)
    c["maskb"] = np.broadcast_to(mb[None], (P, DB, NS)).copy()
    c["bcol"] = np.zeros((P, DB), f)
    c["bcol"][:NS] = mb.T
    pos = np.concatenate([np.arange(SEQ), PAST + np.repeat(np.arange(TS), DB)]).astype(f)
    tab = np.zeros((P, 4, N), f)
    rot_m = np.zeros((P, 2, P), f)
    for n, d in enumerate((HD, ID)):
        rot = d // 4
        half = rot // 2
        inv = (f(ROPE_THETA) ** (-np.arange(half, dtype=f) * f(2.0 / rot))).astype(f)
        ang = (pos[None, :] * inv[:, None]).astype(f)
        cos, sin = np.cos(ang).astype(f), np.sin(ang).astype(f)
        tab[:, 2 * n] = 1.0
        for o in range(0, P, d):
            tab[o:o + half, 2 * n] = tab[o + half:o + rot, 2 * n] = cos
            tab[o:o + half, 2 * n + 1] = tab[o + half:o + rot, 2 * n + 1] = sin
            for a in range(half):
                rot_m[o + half + a, n, o + a] = -1.0
                rot_m[o + a, n, o + half + a] = 1.0
    c["rope"], c["rotm"] = tab, rot_m
    q = np.arange(P)[:, None, None] + P * np.arange(2)[None, :, None]
    c["causal"] = np.where(np.arange(SEQ)[None, None, :] <= q, -NEG_TAKEN, NEG_MASK).astype(f)
    cs = np.full((P, L_S), -NEG_TAKEN, f)
    t = np.arange(NS) // DB
    cs[:NS, PAST:] = np.where(np.arange(TS)[None, :] <= t[:, None], -NEG_TAKEN, NEG_MASK)
    c["causal_s"] = cs
    sel = np.zeros((P, H), f)
    sel[:H] = np.eye(H)
    c["sel"] = sel
    c["fold"] = np.zeros((P, NCP), f)
    c["fold"][:2 * NCP] = np.concatenate([np.eye(NCP)] * 2)
    c["eps"] = np.full((P, 1), EPS, f)
    c["one"] = np.ones((P, 1), f)
    return c


CONST_SIZE = {"ident": P, "ones": P, "incl": P, "lev": LV * P, "smask": 4 * NS, "maskb": DB * NS,
              "bcol": DB, "rope": 4 * N, "rotm": 2 * P, "causal": 2 * SEQ, "causal_s": L_S,
              "sel": H, "fold": NCP, "eps": 1, "one": 1}


def decoder_step(nc, A, O):
    f32, f32r, i32 = mybir.dt.float32, mybir.dt.float32r, mybir.dt.int32
    ALU, ACT, AX = mybir.AluOpType, mybir.ActivationFunctionType, mybir.AxisListType
    ds = bass.ds
    ctx = ExitStack()
    with ctx:
        base0 = ((nc.sbuf_base + 31) // 32) * 32

        class Place:
            def __init__(self, at):
                self.at = at

            def take(self, name, shape, dt=f32):
                size = 4 * int(np.prod(shape[1:]))
                t = nc.alloc_sbuf_tensor_at(name, shape, dt, offset=self.at)
                self.at += (size + 31) // 32 * 32
                return t

        fixed = Place(base0)
        consts = fixed.take("consts", [P, sum(CONST_SIZE.values())])
        cv, off = {}, 0
        for name, size in CONST_SIZE.items():
            cv[name] = consts[:, off:off + size]
            off += size
        ident, ones = cv["ident"], cv["ones"]
        lev = cv["lev"].rearrange("p (l i) -> p l i", l=LV)
        smask = cv["smask"].rearrange("p (m i) -> p m i", m=4)
        maskb = cv["maskb"].rearrange("p (b i) -> p b i", b=DB)
        rope = cv["rope"].rearrange("p (m n) -> p m n", m=4)
        rotm = cv["rotm"].rearrange("p (m n) -> p m n", m=2)
        causal = cv["causal"].rearrange("p (c k) -> p c k", c=2)
        causal_s, sel, eps_c, one_c = cv["causal_s"], cv["sel"], cv["eps"], cv["one"]
        vec = fixed.take("vec", [P, V_ALL])
        ada = fixed.take("ada", [P, 6 * KT, NC])
        cact = fixed.take("cact", [P, KT, 2, NCP], f32r)
        ptab = fixed.take("ptab", [1, DB * (PAST // PAGE)], i32)
        heads_v = fixed.take("heads_v", [H, 2])
        cond_t = Place(fixed.at).take("cond_t", [2 * NCP, CT * P])
        rsb = fixed.take("rsb", [P, N])
        h_hi = fixed.take("h_hi", [P, KT, N], f32r)
        h_lo = fixed.take("h_lo", [P, KT, N], f32r)
        rest_a = Place(fixed.at).take("rest_a", [P, RAW_A, KS, CT * P], f32r)
        raw_a = fixed.take("raw_a", [P, RAW_A, KS, CT * P])
        hi_a = fixed.take("hi_a", [P, RING_A, KS, CT * P], f32r)
        ring_at = fixed.at
        hi_b = fixed.take("hi_b", [P, RING - RING_A, KS, CT * P], f32r)
        rest_b = Place(fixed.at).take("rest_b", [P, RAW - RAW_A, KS, CT * P], f32r)
        raw_b = fixed.take("raw_b", [P, RAW - RAW_A, KS, CT * P])
        raw = [raw_a[:, r, :, :] for r in range(RAW_A)] + [raw_b[:, r, :, :] for r in range(RAW - RAW_A)]
        rest = [rest_a[:, r, :, :] for r in range(RAW_A)] + [rest_b[:, r, :, :] for r in range(RAW - RAW_A)]
        w_hi = [hi_a[:, q, :, :] for q in range(RING_A)] + [hi_b[:, q, :, :] for q in range(RING - RING_A)]
        rest_at = fixed.at

        pl = Place(rest_at)
        x = pl.take("x", [P, KT, N])
        og_p = Place(rest_at)
        og_hi = og_p.take("og_hi", [P, H, N], f32r)
        og_lo = og_p.take("og_lo", [P, H, N], f32r)
        qkv_at = pl.at
        qkv = pl.take("qkv", [P, QKV_T, N])
        z = pl.take("z", [P, Z_T, N])
        dsa_at = pl.at
        dsa = pl.take("dsa", [P, DSA_T, N])
        ikk = pl.take("ikk", [P, N])
        sm_iw = pl.take("sm_iw", [H, N])
        rows_at = pl.at
        rows = pl.take("rows", [H, 4, N])
        tail_at = pl.at
        ip = Place(rest_at)
        cst = ip.take("cst", [P, QKV_T, HI_S + NS])
        cpt = ip.take("cpt", [P, QKV_T, CONV - 1])
        cin = ip.take("cin", [P, CT, CONV - 1 + SEQ])
        cy = ip.take("cy", [P, CT, N])
        sm_a = ip.take("sm_a", [H, N])
        sm_b = ip.take("sm_b", [H, N])
        sm_t = ip.take("sm_t", [H, 2, N])
        assert ip.at <= qkv_at
        np_ = Place(qkv_at)
        sq = np_.take("sq", [P, 2, N])
        ht = np_.take("ht", [P, HB, N])
        hf = np_.take("hf", [P, HB, N])
        amul = np_.take("amul", [P, KT, NC])
        c_f = np_.take("c_f", [P, KT, NCP])
        gp = Place(ring_at)
        gc_t = gp.take("gc_t", [P, 3, H])
        ke_t = gp.take("ke_t", [P, 3, H])
        sqb = gp.take("sqb", [P, 3, N])
        nrm = gp.take("nrm", [P, 3, N])
        qk = gp.take("qk", [P, 2, N])
        rows_m = gp.take("rows_m", [H, 3, N])
        br = gp.take("br", [P, 3, N])
        e_s = gp.take("e_s", [NS, NS])
        qkd_s = gp.take("qkd_s", [NS, NS])
        at_s = gp.take("at_s", [NS, NS])
        bt_s = gp.take("bt_s", [NS, NS])
        tt = gp.take("tt", [P, 4, P])
        tt_s = gp.take("tt_s", [NS, 2, NS])
        x_s = gp.take("x_s", [NS, NS])
        gq = Place(tail_at)
        at_p = gq.take("at_p", [P, 2, P])
        e_p = gq.take("e_p", [P, 2, P])
        qkd_p = gq.take("qkd_p", [P, 2, P])
        x_p = gq.take("x_p", [P, 2, P])
        bt_p = gq.take("bt_p", [P, 2, 2, P])
        r_t = gq.take("r_t", [P, P])
        r_ts = gq.take("r_ts", [P, NS])
        r_p = gq.take("r_p", [P, P])
        r_s = gq.take("r_s", [NS, P])
        u_p = gq.take("u_p", [P, P])
        u_s = gq.take("u_s", [NS, P])
        kend = gq.take("kend", [P, 2, P])
        kend_s = gq.take("kend_s", [NS, P])
        kmask = gq.take("kmask", [NS, DB, P])
        qdec = gq.take("qdec", [P, P])
        st_p = gq.take("st_p", [P, P])
        st_in = gp.take("st_in", [P, DB, P])
        st_out = gq.take("st_out", [P, DB, P])
        o_add = gq.take("o_add", [P, NS])
        o_b = gq.take("o_b", [P, N])
        assert gp.at <= rest_at
        dp = Place(ring_at)
        v_c = dp.take("v_c", [P, DB, PAST // PAGE, KV * HD])
        dq_ = Place(qkv_at)
        do_hi = dq_.take("do_hi", [P, QH, N], f32r)
        do_lo = dq_.take("do_lo", [P, QH, N], f32r)
        kt_c = dq_.take("kt_c", [P, DB, KV, L_S])
        assert dq_.at <= dsa_at
        dr = Place(dp.at)
        sc_p = dr.take("sc_p", [P, 2, SEQ])
        wk_p = dr.take("wk_p", [P, 2, SEQ])
        sc_s = dr.take("sc_s", [NS, L_S])
        wk_s = dr.take("wk_s", [NS, L_S])
        iw_t = dr.take("iw_t", [P, 2, IH])
        iw_s = dr.take("iw_s", [NS, IH])
        top8 = dr.take("top8", [P, 3, 8])
        vtok_s = dr.take("vtok_s", [P, KV * HD])
        assert dr.at <= rest_at, (dr.at, rest_at)
        dt_ = Place(tail_at)
        iqm = dt_.take("iqm", [P, IH, DB // 2, NS])
        rel = dt_.take("rel", [P, 2, L_S])
        vtok = dt_.take("vtok", [P, 2, KV * HD])
        ik_c = dt_.take("ik_c", [P, DB // 2, L_S])
        iq_sw = dt_.take("iq_sw", [P, IH // 2, NS])
        bias_s = dt_.take("bias_s", [NS, L_S])
        dw = Place(rows_at)
        bias_p = dw.take("bias_p", [P, P + SEQ])
        assert dw.at <= tail_at
        du = Place(dsa_at + 12 * N * 4)
        dt2 = Place(tail_at)
        rtmp = dt2.take("rtmp", [P, N])
        q_m = dt2.take("q_m", [P, DB, NS])
        p_tm = dt2.take("p_tm", [P, 2, DB, NS])
        assert dt2.at <= tail_at + 4 * 4 * DB * NS + 4 * 2 * L_S
        q_r = du.take("q_r", [P, N])
        s_p = du.take("s_p", [P, P + SEQ])
        s_s = du.take("s_s", [NS, L_S])
        stat = du.take("stat", [P, 4, 3])
        assert du.at <= dsa_at + DSA_T * N * 4
        p_t = dt_.take("p_t", [P, 3, P])
        pn = dt_.take("pn", [NS, NS])
        pn_t = dt_.take("pn_t", [P, NS])
        o_n = dt_.take("o_n", [P, 2, P])
        o_ns = dt_.take("o_ns", [NS, P])
        rot_t = dt_.take("rot_t", [P, N])
        mp = Place(qkv_at + 2 * 4 * QH * N)
        mix = mp.take("mix_hi", [P, KT, N], f32r)
        mix_lo = mp.take("mix_lo", [P, KT, N], f32r)
        sg = mp.take("sg", [P, 2, CT, N])
        mt = mp.take("mt", [P, CT, N])
        fp = Place(np_.at)
        act_f = fp.take("act_f", [P, CT, N])
        act_hi = fp.take("act_hi", [P, 2, FC, N], f32r)
        act_lo = fp.take("act_lo", [P, 2, FC, N], f32r)
        fst = fp.take("fst", [P, 2 * FT, HI_F + NS])
        fpt = fp.take("fpt", [P, 2 * FT, FCONV - 1])
        fin = fp.take("fin", [P, CT, FCONV - 1 + SEQ])
        fy = fp.take("fy", [P, CT, N])
        fsil = fp.take("fsil", [P, CT, N])
        dtmp = fp.take("dtmp", [P, NS])
        for q_ in (pl, gq, dt_, mp, fp):
            assert q_.at <= nc.sbuf_usable_end, (q_.at, nc.sbuf_usable_end)

        bank = [ctx.enter_context(nc.psum_tensor(f"bank{i}", [P, 512], f32)) for i in range(8)]

        def sem(name):
            return ctx.enter_context(nc.semaphore(name))

        raw_in = [sem(f"raw_in{i}") for i in range(RAW)]
        raw_free = [sem(f"raw_free{i}") for i in range(RAW)]
        hi_ready = sem("hi_ready")
        lo_ready, lo_dve = sem("lo_ready"), sem("lo_dve")
        ring_free = sem("ring_free")
        cond_cp = sem("cond_cp")
        cond_done = sem("cond_done")
        grp_free = [sem(f"grp_free{i}") for i in range(4)]
        c_in = sem("c_in")
        const_in, x_in, x_back, out_done = sem("const_in"), sem("x_in"), sem("x_back"), sem("out_done")
        c_ready = sem("c_ready")
        sq_ready, sq_used, ssq_ready, rs_ready = sem("sq_ready"), sem("sq_used"), sem("ssq_ready"), sem("rs_ready")
        h_t, h_hi_ready, h_lo_ready = sem("h_t"), sem("h_hi_ready"), sem("h_lo_ready")
        conv_y, conv_used = sem("conv_y"), sem("conv_used")
        small_done = sem("small_done")
        row_dve, row_act, row_tr = sem("row_dve"), sem("row_act"), sem("row_tr")
        G = {n: sem("gdn_" + n) for n in (
            "sq ssq rowm bc nrm br qk gram kt e d t1 t1t x xs dt t kss rt rs u us kend sa S1 ks ssm rb sb o "
            "sin spout ssout dve").split()}
        X = {n: sem("dsa_" + n) for n in (
            "load rot rotd clr sw vt vtd idx rel acc newk q rotq s m p pn pt ptm pts o on ot end").split()}
        g_sig, mix_done = sem("g_sig"), sem("mix_done")
        x_done = sem("x_done")
        sil_done, act_ready, down_done = sem("sil_done"), sem("act_ready"), sem("down_done")
        y_ready = sem("y_ready")

        used = [0] * 4
        gbase = {}
        for name, groups, sets in (("ada1", 2 * KT // CT, 2), ("small", 1, 1), ("qkv", QKV_T // CT, 2), ("z", Z_T // CT, 2),
                                   ("dsa", DSA_T // CT, 2), ("ada2", 4 * KT // CT, 1),
                                   ("out", 4 * (KT // CT), 4), ("wo", KT // CT, 3),
                                   ("ffn", NCH * 2 * FC // CT + (NCH - 1) * KT // CT, 4), ("last", KT // CT, 3)):
            gbase[name] = list(used)
            for s_ in range(sets):
                used[s_] += (groups - s_ + sets - 1) // sets

        def grp(name, sets, g, i=0, per=0):
            return g % sets, gbase[name][g % sets] + g // sets + i * (per // sets)

        stretches, uses = [], [0] * RAW
        for first, end, size in ((0, BASE["ada2"], RAW), (BASE["ada2"], BASE["out"], RAW_A), (BASE["out"], NSLOTS, RAW)):
            stretches.append((first, end, size, list(uses)))
            for s_ in range(end - first):
                uses[s_ % size] += 1

        def raw_at(name, j, i=0, per=0):
            s_ = BASE[name] + j
            first, _, size, before = next(t for t in stretches if t[0] <= s_ < t[1])
            return (s_ - first) % size, before[(s_ - first) % size] + (s_ - first) // size + i * (per // size)

        def wait_group(eng, name, g, i=0, per=0):
            if name == "out":
                j, per_j = 12 * (g // 4) + (3, 7, 9, 11)[g % 4], 3 * per
            elif name == "ffn":
                n, m = divmod(g - 4, 12)
                j = 4 * g + 3 if g < 4 else 16 + 24 * n + (3, 7, 8, 9, 10, 11, 12, 13, 14, 15, 19, 23)[m]
                per_j = 2 * per
            elif name == "last":
                j, per_j = g, per
            else:
                j, per_j = 4 * g + 3, 4 * per
            r, use = raw_at(name, j, i, per_j)
            eng.wait_ge(raw_free[r], use + 2)

        GA, XA = 3, 1
        assert (GA * H + XA * QH) * CT == 4 * KT

        def split_at(name, j, i=0, per=0):
            s_ = BASE[name] + j
            return s_ % (RING_A if BASE["ada2"] <= s_ < BASE["out"] else RING), s_ + i * per

        LO_DVE = BASE["small"] // 2

        block = ctx.enter_context(nc.Block())

        @block.sync
        def _(sp):
            def load(r, use, slot):
                sp.wait_ge(raw_free[r], use + 1)
                sp.dma_start(raw[r].rearrange("p k c -> p (k c)"),
                             A["stream"][ds(slot, 1), :, :].rearrange("s p n -> (s p) n")).then_inc(raw_in[r], 16)

            for n, (first, end, size, before) in enumerate(stretches):
                peel = 0
                if n == 2:
                    for r in range(size):
                        if r == RAW_A:
                            sp.wait_ge(X["end"], QH)
                        load(r, before[r], first + r)
                    peel = 1
                loops = (end - first) // size
                with sp.Fori(peel, loops) as i:
                    for r in range(size):
                        load(r, i + before[r], i * size + (first + r))
                for r in range(end - first - loops * size):
                    load(r, before[r] + loops, first + loops * size + r)
            for part in range(4):
                k0, k1 = part * KT // 4, (part + 1) * KT // 4
                sp.wait_ge(y_ready, k1 // 2)
                sp.dma_start(O["y"][:, k0 * N:k1 * N], x[:, k0:k1, :].rearrange("p k n -> p (k n)")).then_inc(out_done, 16)
            sp.wait_ge(out_done, 16 * (7 + 4))
            sp.wait_ge(G["spout"], 16 * (H + 1))
            sp.wait_ge(G["ssout"], 16 * (H + 1))

        @block.gpsimd
        def _(pool):
            for r in range(RAW):
                pool.sem_inc(raw_free[r], 1)
            pool.sem_inc(ring_free, RING)
            pool.sem_inc(sq_used, 2)
            pool.sem_inc(h_lo_ready, HB)

            def lo(name, j, i=0, per=0):
                r, _ = raw_at(name, j, i, per)
                q, cnt = split_at(name, j, i, per)
                pool.wait_ge(hi_ready, cnt + 1)
                nc.gpsimd.tensor_tensor(rest[r], raw[r], w_hi[q].bitcast(f32), ALU.subtract).then_inc(lo_ready, 1)

            def h_rest(base):
                with pool.Fori(0, KT // HB) as i:
                    for s_ in range(HB):
                        pool.wait_ge(h_hi_ready, i * HB + base + s_ + 1)
                        k = i * HB + s_
                        nc.gpsimd.tensor_tensor(h_lo[:, ds(k, 1), :].rearrange("p k n -> p (k n)"), hf[:, s_, :],
                                                h_hi[:, ds(k, 1), :].rearrange("p k n -> p (k n)").bitcast(f32),
                                                ALU.subtract).then_inc(h_lo_ready, 1)

            def run(name, first, count, per):
                with pool.Fori(0, count // per) as i:
                    for j in range(per):
                        lo(name, first + j, i, per)

            pool.wait_ge(c_ready, 1)
            nc.gpsimd.tensor_tensor(cact[:, :, 1, :], c_f[:, :, :], cact[:, :, 0, :].bitcast(f32), ALU.subtract).then_inc(c_ready, 1)
            with pool.Fori(0, LO_DVE // 4) as i:
                for j in range(0, 8, 2):
                    lo("ada1", j, i, 8)
            for j in range(RING):
                lo("small", j)
            h_rest(0)
            run("qkv", 0, BASE["ada2"] - BASE["qkv"], 8)
            run("ada2", 0, BASE["out"] - BASE["ada2"], 8)
            run("out", 0, BASE["ffn"] - BASE["out"], 8)
            for j in range(RING):
                lo("ffn", j)
            h_rest(KT)
            for j in range(RING, 8):
                lo("ffn", j)
            run("ffn", 8, NSLOTS - BASE["ffn"] - 8, 8)

        @block.scalar
        def _(act):
            A_ = nc.scalar.activation
            act.sem_inc(conv_used, 2)
            for g_ in range(4):
                act.sem_inc(grp_free[g_], 1)
            act.dma_start(c_f[:, :, :].rearrange("p k n -> p (k n)"), A["c"]).then_inc(c_in, 16)
            act.dma_start(consts[:, :], A["consts"]).then_inc(const_in, 16)
            act.dma_start(vec[:, :], A["vec"]).then_inc(const_in, 16)
            act.dma_start(heads_v[:, :], A["heads_v"]).then_inc(const_in, 16)
            act.dma_start(x[:, :, :].rearrange("p k n -> p (k n)"), A["x"]).then_inc(x_in, 16)
            act.dma_start(ptab[:, :], A["ptab"]).then_inc(X["load"], 16)

            def hi(name, j, i=0, per=0):
                r, use = raw_at(name, j, i, per)
                q, cnt = split_at(name, j, i, per)
                act.wait_ge(raw_in[r], use * 16 + 16)
                act.wait_ge(ring_free, cnt + 1 + (RING - RING_A if name == "ada2" else 0))
                A_(w_hi[q], raw[r], ACT.Copy).then_inc(hi_ready, 1)

            act.wait_ge(c_in, 16)
            A_(c_f[:, :, :], c_f[:, :, :], ACT.Silu)
            act.drain()
            A_(cact[:, :, 0, :], c_f[:, :, :], ACT.Copy).then_inc(c_ready, 1)

            def squares_of(n, i, s_, tile_done=None, before=0):
                if tile_done is not None:
                    act.wait_ge(tile_done, i * 2 + (before + s_ + 1))
                act.wait_ge(sq_used, i * 2 + n * KT + s_ + 1)
                A_(sq[:, s_, :], x[:, ds(i * 2 + s_, 1), :].rearrange("p k n -> p (k n)"),
                   ACT.Square).then_inc(sq_ready, 1)

            def rms(n):
                act.wait_ge(ssq_ready, n + 1)
                if n == 0:
                    act.wait_ge(cond_done, KT)
                A_(rsb[:, :], bank[7][:, 0:N], ACT.Ln, bias=eps_c, scale=1.0 / D_MODEL)
                act.drain()
                A_(rsb[:, :], rsb[:, :], ACT.Exp, scale=-0.5).then_inc(rs_ready, 1)

            def h_round(base):
                with act.Fori(0, KT // HB) as i:
                    for s_ in range(HB):
                        act.wait_ge(h_t, i * HB + base + s_ + 1)
                        A_(h_hi[:, ds(i * HB + s_, 1), :].rearrange("p k n -> p (k n)"), hf[:, s_, :],
                           ACT.Copy).then_inc(h_hi_ready, 1)

            with act.Fori(0, KT // 2) as i:
                for s_ in range(2):
                    for j in range(4):
                        hi("ada1", 4 * s_ + j, i, 8)
                    act.wait_ge(x_in, 16)
                    squares_of(0, i, s_)
            act.wait_ge(const_in, 48)
            rms(0)
            for j in range(KT // KS):
                hi("small", j)
            h_round(0)
            act.wait_ge(h_t, KT)
            act.dma_start(cst[:, :, 0:HI_S], A["gdn_hist"].rearrange("p (t n) -> p t n", t=QKV_T)).then_inc(const_in, 16)

            LA = 4

            def silu_tiles(g, i=0, per=0):
                for c in range(CT):
                    n = g * CT + c
                    t = i * (per * CT) + n
                    act.wait_ge(conv_y, t + 1)
                    A_(qkv[:, ds(t, 1), :].rearrange("p k n -> p (k n)"), cy[:, c, :],
                       ACT.Silu).then_inc(conv_used, 1)

            for j in range(LA):
                hi("qkv", j)
            with act.Fori(0, 5) as i:
                for j in range(4):
                    hi("qkv", LA + j, i, 8)
                silu_tiles(0, i, 2)
                for j in range(4):
                    hi("qkv", LA + 4 + j, i, 8)
                silu_tiles(1, i, 2)
            for j in range(4):
                hi("qkv", 40 + LA + j)
            silu_tiles(10)
            for j in range(4):
                hi("qkv", 44 + LA + j)
            silu_tiles(11)

            act.wait_ge(small_done, 1)
            A_(sm_t[:, 0, :], sm_a[:, :], ACT.Identity, bias=heads_v[:, 1:2])
            A_(sm_b[:, :], sm_b[:, :], ACT.Exp, scale=-1.0)
            A_(heads_v[:, 0:1], heads_v[:, 0:1], ACT.Exp)
            act.drain()
            A_(sm_a[:, :], sm_t[:, 0, :], ACT.Abs)
            act.drain()
            A_(sm_a[:, :], sm_a[:, :], ACT.Exp, scale=-1.0)
            act.drain()
            A_(sm_a[:, :], sm_a[:, :], ACT.Ln, bias=one_c[0:H, :]).then_inc(row_act, 1)

            def z_tiles(g, i=0, per=0):
                bs, _ = grp("z", 2, g)
                wait_group(act, "z", g, i, per)
                for c in range(CT):
                    t = i * (per * CT) + g * CT + c
                    A_(z[:, ds(t, 1), :].rearrange("p k n -> p (k n)"), bank[2 * bs + c][:, 0:N], ACT.Silu)
                act.drain()
                act.sem_inc(grp_free[bs], 1)

            for g in range(4):
                for j in range(4):
                    hi("z", LA + 4 * g + j)
                z_tiles(g)
            with act.Fori(0, 3) as i:
                for j in range(8):
                    hi("dsa", LA + j, i, 8)
            for j in range(24 + LA, 32):
                hi("dsa", j)

            act.wait_ge(row_dve, 1)
            A_(rows[:, 2, :], rows[:, 0, :], ACT.Exp)
            A_(rows[:, 3, :], rows[:, 3, :], ACT.Exp, scale=-1.0).then_inc(row_act, 1)

            act.wait_ge(conv_y, QKV_T)
            act.dma_start(O["gdn_tail_s"].rearrange("p (t n) -> p t n", t=QKV_T), cst[:, :, HI_S + NS - HI_S:]).then_inc(out_done, 16)
            act.dma_start(O["gdn_tail_p"], cpt[:, :, :].rearrange("p t n -> p (t n)")).then_inc(out_done, 16)

            def g_load(h):
                act.dma_start(st_in[:, :, :].rearrange("p b n -> p (b n)"),
                              A["state"][ds(h, 1), :, :].rearrange("h p n -> (h p) n")).then_inc(G["sin"], 16)

            act.wait_ge(row_tr, 1)
            g_load(0)
            act.wait_ge(out_done, 32)

            def squares(hr):
                A_(sqb[:, 0, :], qkv[:, ds(hr, 1), :].rearrange("p k n -> p (k n)"), ACT.Square)
                A_(sqb[:, 1, :], qkv[:, ds(hr + H, 1), :].rearrange("p k n -> p (k n)"), ACT.Square).then_inc(G["sq"], 1)

            def norms(n, m):
                act.wait_ge(G["ssq"], n)
                A_(nrm[:, 0, :], bank[2][:, 0:N], ACT.Ln, bias=eps_c)
                A_(nrm[:, 1, :], bank[3][:, 0:N], ACT.Ln, bias=eps_c)
                if m == 3:
                    A_(nrm[:, 2, :], bank[7][:, 0:N], ACT.Ln, bias=eps_c, scale=1.0 / DK)
                act.drain()
                A_(nrm[:, 0:m, :], nrm[:, 0:m, :], ACT.Exp, scale=-0.5).then_inc(G["nrm"], 1)
                act.wait_ge(G["bc"], n)
                for c in range(3):
                    last = A_(br[:, c, :], bank[4 + c][:, 0:N], ACT.Copy)
                last.then_inc(G["br"], 1)

            squares(0)
            norms(1, 2)
            hi("ada2", 0)
            with act.Fori(0, H) as h:
                act.wait_ge(G["e"], h + 1)
                A_(e_s[:, :], e_s[:, :], ACT.Exp)
                A_(e_p[:, :, :], e_p[:, :, :], ACT.Exp).then_inc(G["d"], 1)
                hi("ada2", 1, h, 4 * GA)
                hi("ada2", 2, h, 4 * GA)
                for l in range(1, LV):
                    act.wait_ge(G["x"], h * (LV - 1) + l)
                    if l == 1:
                        A_(x_s[:, :], bank[4][0:NS, 2 * P:2 * P + NS], ACT.Copy)
                    A_(x_p[:, :, :].rearrange("p c n -> p (c n)"), bank[4][:, 0:2 * P], ACT.Copy).then_inc(G["xs"], 1)
                    hi("ada2", l + 2, h, 4 * GA)
                for c in range(2):
                    act.wait_ge(G["rt"], h * 2 + c + 1)
                    if c == 0:
                        A_(r_s[:, :], bank[6][0:NS, P:2 * P], ACT.Copy)
                    A_(r_p[:, :], bank[6][:, 0:P], ACT.Copy).then_inc(G["rs"], 1)
                    act.wait_ge(G["u"], h * 2 + c + 1)
                    if c == 0:
                        A_(u_s[:, :], bank[6][0:NS, P:2 * P], ACT.Copy)
                    A_(u_p[:, :], bank[6][:, 0:P], ACT.Copy).then_inc(G["us"], 1)
                    hi("ada2", LV + 2 + c, h, 4 * GA)
                act.wait_ge(G["o"], h + 1)
                act.dma_start(O["state_p"][ds(h, 1), :, :].rearrange("h p n -> (h p) n"), st_p[:, :]).then_inc(G["spout"], 16)
                act.dma_start(O["state_s"][ds(h, 1), :, :].rearrange("h p n -> (h p) n"),
                              st_out[:, :, :].rearrange("p b n -> p (b n)")).then_inc(G["ssout"], 16)
                hn = (h + 1) & (H - 1)
                g_load(hn)
                A_(sqb[:, 2, :], o_b[:, :], ACT.Square)
                squares(hn)
                hi("ada2", 4 * GA - 1, h, 4 * GA)
                norms(h + 2, 3)
                hi("ada2", 4 * GA, h, 4 * GA)
            act.wait_ge(G["dve"], 1)
            act.wait_ge(G["br"], H + 1)
            act.wait_ge(G["sin"], 16 * (H + 1))

            act.wait_ge(X["load"], 16)

            def gather(b, g):
                pid = act.value_load(ptab[0:1, 2 * b + g:2 * b + g + 1], min_val=0, max_val=NPOOL - 1)
                u = ID * (b % 2)
                act.dma_start(ik_c[u:u + ID, b // 2, PAGE * g:PAGE * (g + 1)],
                              A["cik"][ds(pid, 1), :, :].rearrange("s p n -> (s p) n")).then_inc(X["load"], 16)
                act.dma_start(kt_c[:, b, :, PAGE * g:PAGE * (g + 1)],
                              A["ck"][ds(pid, 1), :, :].rearrange("s p (k n) -> (s p) k n", k=KV)).then_inc(X["load"], 16)
                act.dma_start(v_c[:, b, g, :],
                              A["cv"][ds(pid, 1), :, :].rearrange("s p n -> (s p) n")).then_inc(X["load"], 16)

            act.wait_ge(X["rotd"], 7)
            for u in range(2):
                act.dma_start(iq_sw[ID * u:ID * (u + 1), :, :], dsa[ID * (1 - u):ID * (2 - u), 12:12 + IH // 2, SEQ:]).then_inc(X["sw"], 16)
            act.dma_start(O["k"], dsa[:, QH:QH + KV, :].rearrange("p k n -> p (k n)")).then_inc(out_done, 16)
            act.dma_start(O["v"], dsa[:, QH + KV:QH + 2 * KV, :].rearrange("p k n -> p (k n)")).then_inc(out_done, 16)
            act.dma_start(O["ik"], ikk[0:ID, :]).then_inc(out_done, 16)
            act.wait_ge(X["clr"], 1)
            act.wait_ge(X["vt"], 1)
            A_(iw_t[:, :, :].rearrange("p c n -> p (c n)"), bank[6][:, 0:2 * IH], ACT.Copy, scale=IDX_SCALE)
            A_(iw_s[:, :], bank[6][0:NS, 2 * IH:3 * IH], ACT.Copy, scale=IDX_SCALE)
            A_(vtok[:, :, :].rearrange("p c n -> p (c n)"), bank[4][:, :], ACT.Copy)
            A_(vtok_s[0:NS, :], bank[5][0:NS, 0:KV * HD], ACT.Copy).then_inc(X["vtd"], 1)
            for n in range(3 * IH):
                act.wait_ge(X["idx"], n + 1)
                if n >= 2:
                    act.wait_ge(X["acc"], n - 1)
                if n < 2 * IH:
                    A_(rel[:, n % 2, 0:SEQ], bank[2 + n % 2][:, 0:SEQ], ACT.Relu).then_inc(X["rel"], 1)
                    gather(n // 2, n % 2)
                else:
                    A_(rel[0:NS, n % 2, :], bank[2 + n % 2][0:NS, 0:L_S], ACT.Relu).then_inc(X["rel"], 1)
            act.wait_ge(X["load"], 16 * (1 + 3 * DB * (PAST // PAGE)))
            sc_ = HD ** -0.5

            def sparse_head(h, last):
                j0 = 4 * GA * H
                hi("ada2", j0 + 1, h, 4 * XA)
                act.wait_ge(X["m"], h + 1)
                A_(s_p[:, 0:P], s_p[:, 0:P], ACT.Exp, bias=stat[:, 0, 0:1], scale=sc_, accum_out=stat[:, 1, 0:1])
                A_(s_p[:, P:], s_p[:, P:], ACT.Exp, bias=stat[:, 0, 1:2], scale=sc_, accum_out=stat[:, 1, 1:2])
                A_(s_s[:, :], s_s[:, :], ACT.Exp, bias=stat[0:NS, 0, 2:3], scale=sc_,
                   accum_out=stat[0:NS, 1, 2:3]).then_inc(X["p"], 1)
                hi("ada2", j0 + 2, h, 4 * XA)
                act.wait_ge(X["pt"], h + 1)
                A_(p_t[:, :, :].rearrange("p c n -> p (c n)"), bank[5][:, 0:3 * P], ACT.Copy).then_inc(X["pts"], 1)
                hi("ada2", j0 + 3, h, 4 * XA)
                if not last:
                    hi("ada2", j0 + 4, h, 4 * XA)

            with act.Fori(0, QH - 1) as h:
                sparse_head(h, False)
            sparse_head(QH - 1, True)

            def gate_tiles(which, i, g0):
                bs, _ = grp("out", 4, 4 * g0 + which)
                wait_group(act, "out", 4 * g0 + which, i, 8)
                act.wait_ge(mix_done, i * 2 + g0 + 1)
                for c in range(CT):
                    last = A_(sg[:, which, c, :], bank[2 * bs + c][:, 0:N], ACT.Sigmoid)
                last.then_inc(g_sig, 1)
                act.wait_ge(g_sig, (i * 2 + g0) * 2 + which + 1)
                act.sem_inc(grp_free[bs], 1)

            act.wait_ge(out_done, 16 * 5)
            act.wait_ge(X["end"], QH)
            for j in range(LA):
                hi("out", j)

            def out_body(i):
                for g0 in range(2):
                    for j in range(4):
                        hi("out", LA + 12 * g0 + j, i, 24)
                    gate_tiles(0, i, g0)
                    for j in range(4, 8):
                        hi("out", LA + 12 * g0 + j, i, 24)
                    gate_tiles(1, i, g0)
                    for j in range(8, 12):
                        hi("out", LA + 12 * g0 + j, i, 24)

            with act.Fori(0, 4) as i:
                out_body(i)
            bs, _ = grp("out", 4, 4 * (KT // CT) - 1)
            wait_group(act, "out", 4 * (KT // CT) - 1)
            act.dma_start(x[:, :, :].rearrange("p k n -> p (k n)"), A["x"]).then_inc(x_back, 16)
            for j in range(LA, 32):
                hi("wo", j)
                if j >= 11 and j % 4 == 3:
                    for s_ in range(2):
                        squares_of(1, (j - 11) // 4, s_, x_done)
            for g in range(6, KT // 2):
                for s_ in range(2):
                    squares_of(1, g, s_, x_done)
            rms(1)
            for j in range(LA):
                hi("ffn", j)
            act.dma_start(fst[:, :, 0:HI_F], A["ffn_hist"].rearrange("p (t n) -> p t n", t=2 * FT)).then_inc(const_in, 16)
            h_round(KT)

            def ffn_silu(c0, i):
                for c in range(CT):
                    t = i * FC + c0 + c
                    act.wait_ge(conv_y, QKV_T + i * FC + c0 + c + 1)
                    A_(fsil[:, c, :], fy[:, c, :], ACT.Silu,
                       bias=vec[:, ds(t + V_BF, 1)]).then_inc(sil_done, 1)

            for j in range(4):
                hi("ffn", LA + j)
            ffn_silu(0, 0)
            for j in range(4, 12):
                hi("ffn", LA + j)
            ffn_silu(2, 0)
            for j in range(12, 16):
                hi("ffn", LA + j)
            with act.Fori(0, NCH - 1) as i:
                for j in range(4):
                    hi("ffn", 16 + LA + j, i, 24)
                ffn_silu(0, i + 1)
                for j in range(4, 20):
                    hi("ffn", 16 + LA + j, i, 24)
                ffn_silu(2, i + 1)
                for j in range(20, 24):
                    hi("ffn", 16 + LA + j, i, 24)
            for j in range(LA, KT // CT):
                hi("last", j)
                if j >= 5:
                    for s_ in range(2):
                        squares_of(2, j - 5, s_, down_done, (NCH - 1) * KT)
            for g in range(3, KT // 2):
                for s_ in range(2):
                    squares_of(2, g, s_, down_done, (NCH - 1) * KT)
            act.dma_start(O["ffn_tail_s"].rearrange("p (t n) -> p t n", t=2 * FT), fst[:, :, NS:]).then_inc(out_done, 16)
            act.dma_start(O["ffn_tail_p"], fpt[:, :, :].rearrange("p t n -> p (t n)")).then_inc(out_done, 16)
            rms(2)

        @block.vector
        def _(dve):
            V = nc.vector
            T_, S_, STT, CP = V.tensor_tensor, V.tensor_scalar, V.scalar_tensor_tensor, V.tensor_copy
            row = lambda a: a.rearrange("p k n -> p (k n)")

            def cond_copy(name, g, sets, i=0, per=0):
                wait_group(dve, name, g, i, per)
                CP(cond_t[:, :], bank[2 * (g % sets)][0:2 * NCP, 0:CT * P]).then_inc(cond_cp, 1)

            def cond_bias(name, g, sets, i=0, per=0):
                n0 = g + (2 * KT // CT if name == "ada2" else 0)
                dve.wait_ge(cond_done, i * per + (n0 + 1))
                t = i * (per * CT) + n0 * CT
                T_(ada[:, ds(t, CT), :], bank[2 * (g % sets) + 1][:, 0:CT * NCP].rearrange("p (c n) -> p c n", c=CT)[:, :, 0:NC],
                   vec[:, ds(t + V_BADA, CT)].unsqueeze(2).to_broadcast([P, CT, NC]), ALU.add).then_inc(grp_free[g % sets], 1)

            dve.sem_inc(mix_done, 1)
            def ada1_pair(first, i=0):
                for g in (first, first + 1):
                    for j in (4 * g + 1, 4 * g + 3):
                        r, _ = raw_at("ada1", j, i, 8)
                        q, n = split_at("ada1", j, i, 8)
                        dve.wait_ge(hi_ready, n + 1)
                        T_(rest[r], raw[r], w_hi[q].bitcast(f32), ALU.subtract).then_inc(lo_dve, 1)
                        if j % 4 == 1 and g > 0:
                            cond_bias("ada1", g - 1, 2, i, 2)
                    cond_copy("ada1", g, 2, i, 2)
                    if g == 0:
                        dve.wait_ge(const_in, 48)

            dve.sem_inc(cond_cp, 2)
            ada1_pair(0)
            with dve.Fori(0, KT // CT - 2) as i:
                ada1_pair(2, i)
            ada1_pair(KT - 2)
            cond_bias("ada1", KT - 1, 2)
            dve.wait_ge(x_in, 16)
            dve.drain()

            def scale_shift(n, sub):
                gcol = V_G1 if n == 0 else V_G2
                g_b = vec[:, gcol:gcol + KT].unsqueeze(2).to_broadcast([P, KT, NC])
                STT(amul[:, :, :], ada[:, (3 * sub + 1) * KT:(3 * sub + 2) * KT, :], 1.0, g_b, ALU.add, ALU.mult)
                dve.drain()
                dve.wait_ge(rs_ready, n + 1)
                with dve.Fori(0, KT // HB) as i:
                    for s_ in range(HB):
                        k = i * HB + s_
                        T_(ht[:, s_, :], row(x[:, ds(k, 1), :]), rsb[:, :], ALU.mult)
                    dve.drain()
                    for s_ in range(HB):
                        k = i * HB + s_
                        dve.wait_ge(h_lo_ready, i * HB + n * KT + s_ + 1)
                        am, sh = row(amul[:, ds(k, 1), :]), row(ada[:, ds(k + 3 * sub * KT, 1), :])
                        S_(hf[:, s_, 0:SEQ], ht[:, s_, 0:SEQ], am[:, 0:1], sh[:, 0:1], ALU.mult, ALU.add)
                        T_(ht[:, s_, SEQ:].rearrange("p (t b) -> p t b", b=DB), ht[:, s_, SEQ:].rearrange("p (t b) -> p t b", b=DB),
                           am[:, 1:NC].unsqueeze(1).to_broadcast([P, TS, DB]), ALU.mult)
                    dve.drain()
                    for s_ in range(HB):
                        k = i * HB + s_
                        sh = row(ada[:, ds(k + 3 * sub * KT, 1), :])
                        T_(hf[:, s_, SEQ:].rearrange("p (t b) -> p t b", b=DB), ht[:, s_, SEQ:].rearrange("p (t b) -> p t b", b=DB),
                           sh[:, 1:NC].unsqueeze(1).to_broadcast([P, TS, DB]), ALU.add).then_inc(h_t, 1)
                    dve.drain()

            scale_shift(0, 0)
            dve.drain()
            V.memset(cin[:, :, 0:CONV - 1], 0.0)
            dve.wait_ge(const_in, 64)

            def conv(psum, c, src, y, st, tile, tap0, taps, hist, ntile, keep):
                CP(src[:, c, taps - 1:taps - 1 + SEQ], psum[:, 0:SEQ])
                CP(row(st[:, ds(tile, 1), hist:hist + NS]), psum[:, SEQ:N])
                dve.drain()
                for w_ in range(taps):
                    wc = vec[:, ds(tile + (tap0 + w_ * ntile), 1)]
                    sp_ = src[:, c, w_:w_ + SEQ]
                    ss_ = row(st[:, ds(tile, 1), DB * w_:DB * w_ + NS])
                    if w_ == 0:
                        S_(y[:, c, 0:SEQ], sp_, wc, None, ALU.mult)
                        S_(y[:, c, SEQ:], ss_, wc, None, ALU.mult)
                        CP(row(keep[:, ds(tile, 1), :]), src[:, c, SEQ:SEQ + taps - 1])
                    else:
                        STT(y[:, c, 0:SEQ], sp_, wc, y[:, c, 0:SEQ], ALU.mult, ALU.add)
                        last = STT(y[:, c, SEQ:], ss_, wc, y[:, c, SEQ:], ALU.mult, ALU.add)
                    if w_ < taps - 1:
                        dve.drain()
                return last

            bs, _ = grp("small", 1, 0)
            wait_group(dve, "small", 0)
            CP(ikk[:, :], bank[0][:, 0:N])
            CP(sm_a[:, :], bank[1][0:H, 0:N])
            CP(sm_b[:, :], bank[1][32:32 + H, 0:N])
            CP(sm_iw[:, :], bank[1][64:64 + H, 0:N])
            dve.drain()
            dve.sem_inc(grp_free[bs], 1)
            dve.sem_inc(small_done, 1)

            with dve.Fori(0, 6) as i:
                for g in range(2):
                    bs, _ = grp("qkv", 2, g)
                    wait_group(dve, "qkv", g, i, 2)
                    for c in range(CT):
                        t = i * 4 + 2 * g + c
                        dve.wait_ge(conv_used, t + 1)
                        conv(bank[2 * bs + c], c, cin, cy, cst, t, V_WC, CONV, HI_S, QKV_T, cpt).then_inc(conv_y, 1)
                    dve.drain()
                    dve.sem_inc(grp_free[bs], 1)
            dve.wait_ge(row_act, 1)
            STT(sm_t[:, 1, :], sm_t[:, 0, :], 0.0, sm_a[:, :], ALU.max, ALU.add)
            S_(sm_b[:, :], sm_b[:, :], 1.0, None, ALU.add)
            dve.drain()
            V.memset(sm_t[:, 0, :], 1.0)
            S_(sm_t[:, 1, :], sm_t[:, 1, :], heads_v[:, 0:1], -1.0, ALU.mult, ALU.mult)
            V.reciprocal(rows[:, 1, :], sm_b[:, :])
            dve.drain()
            for c in range(2):
                V.tensor_tensor_scan(rows[:, 0, c * P:(c + 1) * P], sm_t[:, 0, 0:P], sm_t[:, 1, c * P:(c + 1) * P], 0.0,
                                     ALU.mult, ALU.add)
            CP(rows[:, 0, SEQ:SEQ + DB], sm_t[:, 1, SEQ:SEQ + DB])
            for t in range(1, TS):
                dve.drain()
                o_ = SEQ + t * DB
                T_(rows[:, 0, o_:o_ + DB], rows[:, 0, o_ - DB:o_], sm_t[:, 1, o_:o_ + DB], ALU.add)
            dve.drain()
            for c in range(2):
                S_(rows[:, 3, c * P:(c + 1) * P], rows[:, 0, c * P:(c + 1) * P], rows[:, 0, (c + 1) * P - 1:(c + 1) * P], None, ALU.subtract)
            T_(rows[:, 3, SEQ:].rearrange("p (t b) -> p t b", b=DB), rows[:, 0, SEQ:].rearrange("p (t b) -> p t b", b=DB),
               rows[:, 0, N - DB:N].unsqueeze(1).to_broadcast([H, TS, DB]), ALU.subtract).then_inc(row_dve, 1)
            with dve.Fori(0, 4) as i:
                for g in range(2):
                    bs, _ = grp("dsa", 2, g)
                    wait_group(dve, "dsa", g, i, 2)
                    for c in range(CT):
                        last = CP(row(dsa[:, ds(i * 4 + 2 * g + c, 1), :]), bank[2 * bs + c][:, 0:N])
                    dve.drain()
                    dve.sem_inc(grp_free[bs], 1)
            dve.wait_ge(row_tr, 1)
            for t_, bk in ((gc_t, 2), (ke_t, 3)):
                CP(t_[:, 0:2, :].rearrange("p c h -> p (c h)"), bank[bk][:, 0:2 * H])
                CP(t_[0:NS, 2, :], bank[bk][0:NS, 2 * H:3 * H])
            dve.drain()

            def head_rows(hr):
                S_(rows_m[:, :, :], rows[:, 0:3, :], sel[0:H, ds(hr, 1)], None, ALU.mult).then_inc(G["rowm"], 1)

            def head_qk(hr, n):
                dve.wait_ge(G["nrm"], n)
                STT(qk[:, 0, :], row(qkv[:, ds(hr, 1), :]), DK ** -0.5, nrm[:, 0, :], ALU.mult, ALU.mult)
                T_(qk[:, 1, :], row(qkv[:, ds(hr + H, 1), :]), nrm[:, 1, :], ALU.mult).then_inc(G["qk"], 1)

            dve.sem_inc(G["spout"], 16)
            dve.sem_inc(G["ssout"], 16)
            head_rows(0)
            head_qk(0, 1)
            with dve.Fori(0, H) as h:
                v_h = row(qkv[:, ds(h + 2 * H, 1), :])

                def level_mask(l):
                    T_(bt_p[:, l % 2, :, :], at_p[:, :, :], lev[:, l, :].unsqueeze(1).to_broadcast([P, 2, P]), ALU.mult)

                dve.wait_ge(G["br"], h + 1)
                for c in range(2):
                    S_(e_p[:, c, :], br[:, 0, c * P:(c + 1) * P], gc_t[:, c, ds(h, 1)], 0.0, ALU.subtract, ALU.min)
                S_(e_s[:, :], br[0:NS, 0, SEQ:], gc_t[0:NS, 2, ds(h, 1)], 0.0, ALU.subtract, ALU.min)
                dve.drain()
                dve.sem_inc(G["e"], 1)
                dve.wait_ge(G["d"], h + 1)
                T_(e_p[:, :, :], e_p[:, :, :], cv["incl"].unsqueeze(1).to_broadcast([P, 2, P]), ALU.mult)
                T_(e_s[:, :], e_s[:, :], smask[0:NS, 0, :], ALU.mult)
                dve.drain()
                dve.wait_ge(G["gram"], h + 1)
                g_p = bank[2][:, :].rearrange("p (c m n) -> p c m n", c=2, m=2)
                T_(at_p[:, :, :], g_p[:, :, 1, :], e_p[:, :, :], ALU.mult)
                T_(at_s[:, :], bank[3][0:NS, NS:2 * NS], e_s[:, :], ALU.mult)
                T_(qkd_p[:, :, :], g_p[:, :, 0, :], e_p[:, :, :], ALU.mult)
                T_(qkd_s[:, :], bank[3][0:NS, 0:NS], e_s[:, :], ALU.mult)
                dve.drain()
                T_(at_p[:, :, :], at_p[:, :, :], br[:, 1, 0:SEQ].rearrange("p (c n) -> p c n", c=2), ALU.mult)
                T_(at_s[:, :], at_s[:, :], br[0:NS, 1, SEQ:], ALU.mult)
                dve.drain()
                T_(tt[:, 0:2, :], at_p[:, :, :], lev[:, 0, :].unsqueeze(1).to_broadcast([P, 2, P]), ALU.mult)
                T_(tt_s[:, 0, :], at_s[:, :], smask[0:NS, 1, :], ALU.mult)
                dve.drain()
                T_(tt[:, 0:2, :], ident.unsqueeze(1).to_broadcast([P, 2, P]), tt[:, 0:2, :], ALU.subtract)
                T_(tt_s[:, 0, :], ident[0:NS, 0:NS], tt_s[:, 0, :], ALU.subtract)
                dve.drain()
                dve.sem_inc(G["t1"], 1)
                level_mask(1)
                T_(bt_s[:, :], at_s[:, :], smask[0:NS, 2, :], ALU.mult)
                dve.wait_ge(G["t1t"], h + 1)
                CP(tt[:, 2:4, :].rearrange("p c n -> p (c n)"), bank[3][:, 0:2 * P])
                CP(tt_s[:, 1, :], bank[3][0:NS, 2 * P:2 * P + NS])
                dve.drain()
                dve.sem_inc(G["t"], 1)
                for l in range(1, LV):
                    if l < LV - 1:
                        level_mask(l + 1)
                    if l == 1:
                        dve.wait_ge(G["kss"], h + 1)
                        T_(o_add[:, :], bank[6][:, 0:NS], br[:, 2, SEQ:], ALU.mult)
                        T_(r_ts[:, :], bank[6][:, NS:2 * NS], br[:, 2, SEQ:], ALU.mult)
                        T_(r_t[:, :], v_h[:, 0:P], br[:, 1, 0:P], ALU.mult)
                        dve.drain()
                        T_(r_ts[:, :], v_h[:, SEQ:], r_ts[:, :], ALU.subtract)
                    if l == 2:
                        T_(r_ts[:, :], r_ts[:, :], br[:, 1, SEQ:], ALU.mult)
                        T_(qdec[:, :], qk[:, 0, P:2 * P], br[:, 2, P:2 * P], ALU.mult)
                        dve.wait_ge(G["kt"], h + 1)
                        for c in range(2):
                            S_(kend[:, c, :], bank[7][:, c * P:(c + 1) * P], ke_t[:, c, ds(h, 1)], None, ALU.mult)
                        S_(kend_s[:, :], bank[7][0:NS, 2 * P:3 * P], ke_t[0:NS, 2, ds(h, 1)], None, ALU.mult)
                    if l == 3:
                        T_(kmask[:, :, :], kend_s[:, :].unsqueeze(1).to_broadcast([NS, DB, P]),
                           cv["bcol"][0:NS, :].unsqueeze(2).to_broadcast([NS, DB, P]), ALU.mult)
                    if l == 4:
                        dve.sem_inc(G["kend"], 1)
                        dve.wait_ge(G["ssout"], h * 16 + 16)
                        T_(st_out[:, :, :], st_in[:, :, :], br[:, 2, N - DB:N].unsqueeze(2).to_broadcast([P, DB, P]), ALU.mult)
                    if l == 3:
                        cond_copy("ada2", 0, 1, h, GA)
                    if l == 5:
                        cond_bias("ada2", 0, 1, h, GA)
                    dve.wait_ge(G["dt"], h * (LV - 1) + l)
                    w_ = 4 if l < LV - 1 else 2
                    tv = tt[:, 0:w_, :].rearrange("p c n -> p (c n)")
                    T_(tv, tv, bank[5][:, 0:w_ * P], ALU.subtract)
                    if l == 1:
                        T_(tt_s[:, 0, :], tt_s[:, 0, :], bank[3][0:NS, 0:NS], ALU.subtract)
                    dve.drain()
                    dve.sem_inc(G["t"], 1)
                cond_copy("ada2", 1, 1, h, GA)
                dve.wait_ge(G["spout"], h * 16 + 16)
                dve.wait_ge(G["sa"], h + 1)
                CP(st_p[:, :], bank[3][:, 0:P])
                dve.drain()
                dve.sem_inc(G["S1"], 1)
                dve.wait_ge(G["ks"], h + 1)
                T_(r_t[:, :], bank[4][:, 0:P], br[:, 2, P:2 * P], ALU.mult)
                dve.drain()
                T_(r_t[:, :], v_h[:, P:2 * P], r_t[:, :], ALU.subtract)
                dve.drain()
                T_(r_t[:, :], r_t[:, :], br[:, 1, P:2 * P], ALU.mult)
                dve.drain()
                dve.sem_inc(G["rb"], 1)
                for m, bk in enumerate((5, 7)):
                    dve.wait_ge(G["ssm"], h * 2 + m + 1)
                    so = st_out[:, 4 * m:4 * m + 4, :].rearrange("p b n -> p (b n)")
                    T_(so, so, bank[bk][:, :], ALU.add)
                cond_bias("ada2", 1, 1, h, GA)
                dve.wait_ge(G["sb"], h + 1)
                CP(o_b[:, 0:SEQ], bank[2][:, 0:SEQ])
                T_(o_b[:, SEQ:], bank[2][:, SEQ:N], o_add[:, :], ALU.add)
                STT(st_p[:, :], st_p[:, :], br[:, 2, SEQ - 1:SEQ], bank[3][:, 0:P], ALU.mult, ALU.add)
                dve.drain()
                dve.sem_inc(G["o"], 1)
                hn = (h + 1) & (H - 1)
                head_rows(hn)
                head_qk(hn, h + 2)
                cond_copy("ada2", 2, 1, h, GA)
                STT(o_b[:, :], o_b[:, :], vec[:, V_GN:V_GN + 1], nrm[:, 2, :], ALU.mult, ALU.mult)
                dve.drain()
                T_(o_b[:, :], o_b[:, :], row(z[:, ds(h, 1), :]), ALU.mult)
                dve.drain()
                CP(row(og_hi[:, ds(h, 1), :]), o_b[:, :])
                dve.drain()
                T_(row(og_lo[:, ds(h, 1), :]), o_b[:, :], row(og_hi[:, ds(h, 1), :]).bitcast(f32), ALU.subtract)
                cond_bias("ada2", 2, 1, h, GA)
            dve.drain()
            dve.wait_ge(G["spout"], H * 16 + 16)
            dve.wait_ge(G["ssout"], H * 16 + 16)
            dve.wait_ge(G["br"], H + 1)
            dve.sem_inc(G["dve"], 1)

            turned = [(dsa[:, QH + m, :], 0) for m in range(KV)] + [(dsa[:, 12 + m, :], 1) for m in range(4)] + [(ikk[:, :], 1)]
            for n, (t_, kind) in enumerate(turned):
                dve.wait_ge(X["rot"], n + 1)
                T_(rot_t[:, :], bank[2 + n % 2][:, 0:N], rope[:, 2 * kind + 1, :], ALU.mult)
                T_(t_, t_, rope[:, 2 * kind, :], ALU.mult)
                dve.drain()
                T_(t_, t_, rot_t[:, :], ALU.add)
                dve.drain()
                dve.sem_inc(X["rotd"], 1)
            dve.wait_ge(G["sin"], 16 * (H + 1))
            V.memset(vtok_s[:, :], 0.0)
            V.memset(pn_t[:, :], 0.0)
            dve.drain()
            dve.sem_inc(X["clr"], 1)
            dve.wait_ge(X["sw"], 32)
            for h_ in range(IH):
                for u in range(2):
                    pr = slice(ID * u, ID * (u + 1))
                    src = dsa[pr, 12 + h_ // 2, SEQ:] if h_ % 2 == u else iq_sw[pr, h_ // 2, :]
                    T_(iqm[pr, h_, :, :], src.unsqueeze(1).to_broadcast([ID, DB // 2, NS]),
                       maskb[pr, :, :].rearrange("p (q u) n -> p q u n", u=2)[:, :, u, :], ALU.mult)

            def accumulate(n):
                dve.wait_ge(X["rel"], n + 1)
                h_ = n % IH
                if n < 2 * IH:
                    out_, in_, w_ = sc_p[:, n // IH, :], rel[:, n % 2, 0:SEQ], iw_t[:, n // IH, h_:h_ + 1]
                else:
                    out_, in_, w_ = sc_s[:, :], rel[0:NS, n % 2, :], iw_s[:, h_:h_ + 1]
                if h_ == 0:
                    S_(out_, in_, w_, None, ALU.mult)
                else:
                    STT(out_, in_, w_, out_, ALU.mult, ALU.add)
                dve.drain()
                dve.sem_inc(X["acc"], 1)

            sets = [(sc_p[:, 0, :], wk_p[:, 0, :], top8[:, 0, :]), (sc_p[:, 1, :], wk_p[:, 1, :], top8[:, 1, :]),
                    (sc_s[:, :], wk_s[:, :], top8[0:NS, 2, :])]

            def take_eight(r, which):
                for s_, w_, t8 in which:
                    V.max(out=t8, in_=w_ if r else s_)
                dve.drain()
                for s_, w_, t8 in which:
                    V.match_replace(out=w_, in_to_replace=t8, in_values=w_ if r else s_, imm_value=NEG_TAKEN)
                dve.drain()

            dve.wait_ge(X["vtd"], 1)
            for n in range(2 * IH):
                accumulate(n)
            dve.wait_ge(X["load"], 16 * (1 + 3 * DB * (PAST // PAGE)))
            for u in range(2):
                pr = slice(ID * u, ID * (u + 1))
                CP(ik_c[pr, :, PAST:L_S], ikk[pr, SEQ:].rearrange("p (t q u) -> p q u t", q=DB // 2, u=2)[:, :, u, :])
            for m in range(KV):
                CP(kt_c[:, :, m, PAST:L_S], dsa[:, QH + m, SEQ:].rearrange("p (t b) -> p b t", b=DB))
            T_(sc_p[:, :, :], sc_p[:, :, :], causal, ALU.min)
            dve.drain()
            dve.sem_inc(X["newk"], 1)
            for r in range(max(IH, TOPK_P // 8)):
                if r < TOPK_P // 8:
                    take_eight(r, sets[0:2])
                if r < IH:
                    accumulate(2 * IH + r)
            T_(sc_s[:, :], sc_s[:, :], causal_s[0:NS, :], ALU.min)
            dve.drain()
            for r in range(TOPK_P // 8):
                take_eight(r, sets[2:3])
            s_, w_, t8 = sets[2]
            V.max(out=t8, in_=w_)
            dve.drain()
            V.memset(t8[:, TOPK_S - TOPK_P:], -NEG_TAKEN)
            dve.drain()
            V.match_replace(out=w_, in_to_replace=t8, in_values=w_, imm_value=NEG_TAKEN)
            dve.drain()
            T_(wk_p[:, :, :], wk_p[:, :, :], sc_p[:, :, :], ALU.not_equal)
            T_(wk_s[:, :], wk_s[:, :], sc_s[:, :], ALU.not_equal)
            dve.drain()
            S_(sc_p[:, :, :], causal, 0.0, None, ALU.is_gt)
            S_(sc_s[:, :], causal_s[0:NS, :], 0.0, None, ALU.is_gt)
            dve.drain()
            T_(wk_p[:, :, :], wk_p[:, :, :], sc_p[:, :, :], ALU.mult)
            T_(wk_s[:, :], wk_s[:, :], sc_s[:, :], ALU.mult)
            dve.drain()
            S_(bias_p[:, 0:P], wk_p[:, 0, 0:P], BIG, -BIG, ALU.mult, ALU.add)
            S_(bias_p[:, P:], wk_p[:, 1, :], BIG, -BIG, ALU.mult, ALU.add)
            S_(bias_s[:, :], wk_s[:, :], BIG, -BIG, ALU.mult, ALU.add)
            dve.drain()

            def turn_q(hr, n):
                dve.wait_ge(X["rotq"], n)
                T_(rtmp[:, :], bank[2][:, 0:N], rope[:, 1, :], ALU.mult)
                T_(q_r[:, :], row(dsa[:, ds(hr, 1), :]), rope[:, 0, :], ALU.mult)
                dve.drain()
                T_(q_r[:, :], q_r[:, :], rtmp[:, :], ALU.add)
                dve.drain()
                T_(q_m[:, :, :], q_r[:, SEQ:].unsqueeze(1).to_broadcast([P, DB, NS]), maskb, ALU.mult)
                dve.drain()
                dve.sem_inc(X["q"], 1)

            turn_q(0, 1)
            with dve.Fori(0, QH) as h:
                dve.wait_ge(X["s"], h + 1)
                T_(s_p[:, :], bank[3][:, 0:P + SEQ], bias_p[:, :], ALU.add)
                T_(s_s[:, :], bank[4][0:NS, 0:L_S], bias_s[:, :], ALU.add)
                dve.drain()
                V.tensor_reduce(stat[:, 2, 0:1], s_p[:, 0:P], AX.X, ALU.max)
                V.tensor_reduce(stat[:, 2, 1:2], s_p[:, P:], AX.X, ALU.max)
                V.tensor_reduce(stat[0:NS, 2, 2:3], s_s[:, :], AX.X, ALU.max)
                dve.drain()
                S_(stat[:, 0, 0:2], stat[:, 2, 0:2], -(HD ** -0.5), None, ALU.mult)
                S_(stat[0:NS, 0, 2:3], stat[0:NS, 2, 2:3], -(HD ** -0.5), None, ALU.mult)
                dve.drain()
                dve.sem_inc(X["m"], 1)
                dve.wait_ge(X["p"], h + 1)
                T_(pn[:, :].rearrange("p (t b) -> p t b", b=DB), s_s[:, PAST:].unsqueeze(2).to_broadcast([NS, TS, DB]),
                   smask[0:NS, 3, :].rearrange("p (t b) -> p t b", b=DB), ALU.mult)
                V.reciprocal(stat[:, 3, 0:2], stat[:, 1, 0:2])
                V.reciprocal(stat[0:NS, 3, 2:3], stat[0:NS, 1, 2:3])
                dve.drain()
                dve.sem_inc(X["pn"], 1)
                dve.wait_ge(X["pt"], h + 1)
                for g in range(2):
                    T_(p_tm[:, g, :, :], bank[6][:, g * NS:(g + 1) * NS].unsqueeze(1).to_broadcast([P, DB, NS]), maskb, ALU.mult)
                CP(pn_t[0:NS, :], bank[6][0:NS, 2 * NS:3 * NS])
                dve.drain()
                dve.sem_inc(X["ptm"], 1)
                turn_q((h + 1) & (QH - 1), h + 2)
                dve.wait_ge(X["o"], h + 1)
                for c in range(2):
                    S_(o_n[:, c, :], bank[7][:, c * P:(c + 1) * P], stat[:, 3, c:c + 1], None, ALU.mult)
                S_(o_ns[:, :], bank[2][0:NS, 0:P], stat[0:NS, 3, 2:3], None, ALU.mult)
                dve.drain()
                dve.sem_inc(X["on"], 1)
                cond_copy("ada2", GA * H, 1, h, XA)
                dve.wait_ge(X["ot"], h + 1)
                CP(row(do_hi[:, ds(h, 1), :]), bank[5][:, 0:N])
                dve.drain()
                T_(row(do_lo[:, ds(h, 1), :]), bank[5][:, 0:N], row(do_hi[:, ds(h, 1), :]).bitcast(f32), ALU.subtract)
                dve.drain()
                cond_bias("ada2", GA * H, 1, h, XA)
                dve.sem_inc(X["end"], 1)

            dve.wait_ge(out_done, 16 * 5)
            with dve.Fori(0, 4) as i:
                for g0 in range(2):
                    for which in range(2):
                        bs, _ = grp("out", 4, 4 * g0 + 2 + which)
                        dve.wait_ge(g_sig, (i * 2 + g0) * 2 + which + 1)
                        wait_group(dve, "out", 4 * g0 + 2 + which, i, 8)
                        for c in range(CT):
                            T_(mt[:, c, :] if which == 0 else sg[:, 1, c, :], bank[2 * bs + c][:, 0:N], sg[:, which, c, :], ALU.mult)
                        dve.drain()
                        dve.sem_inc(grp_free[bs], 1)
                    for c in range(CT):
                        T_(mt[:, c, :], mt[:, c, :], sg[:, 1, c, :], ALU.add)
                    dve.drain()
                    for c in range(CT):
                        CP(row(mix[:, ds(i * 4 + 2 * g0 + c, 1), :]), mt[:, c, :])
                    dve.drain()
                    for c in range(CT):
                        k = i * 4 + 2 * g0 + c
                        T_(row(mix_lo[:, ds(k, 1), :]), mt[:, c, :], row(mix[:, ds(k, 1), :]).bitcast(f32), ALU.subtract)
                    dve.drain()
                    dve.sem_inc(mix_done, 1)

            def residual(psum, t, gate_tile, tmp):
                xt, gt = row(x[:, ds(t, 1), :]), row(ada[:, ds(gate_tile, 1), :])
                STT(xt[:, 0:SEQ], psum[:, 0:SEQ], gt[:, 0:1], xt[:, 0:SEQ], ALU.mult, ALU.add)
                T_(tmp.rearrange("p (t b) -> p t b", b=DB), psum[:, SEQ:N].rearrange("p (t b) -> p t b", b=DB),
                   gt[:, 1:NC].unsqueeze(1).to_broadcast([P, TS, DB]), ALU.mult)
                dve.drain()
                return T_(xt[:, SEQ:], xt[:, SEQ:], tmp, ALU.add)

            dve.wait_ge(x_back, 16)
            for g in range(KT // CT):
                bs, _ = grp("wo", 3, g)
                wait_group(dve, "wo", g)
                for c in range(CT):
                    t = 2 * g + c
                    residual(bank[2 * bs + c], t, t + 2 * KT, mt[:, c, 0:NS]).then_inc(x_done, 1)
                dve.drain()
                dve.sem_inc(grp_free[bs], 1)
            scale_shift(1, 1)
            dve.drain()
            V.memset(fin[:, :, 0:FCONV - 1], 0.0)
            dve.wait_ge(const_in, 80)

            def ffn_gate(g, idx, half, i, per):
                bs, _ = grp("ffn", 4, g)
                wait_group(dve, "ffn", g, idx, per)
                for c in range(CT):
                    t = i * FC + 2 * half + c
                    conv(bank[2 * bs + c], c, fin, fy, fst, t, V_WF, FCONV, HI_F, 2 * FT, fpt)
                    dve.drain()
                    dve.sem_inc(conv_y, 1)
                dve.sem_inc(grp_free[bs], 1)

            def ffn_val(g, idx, half, i, per):
                bs, _ = grp("ffn", 4, g)
                wait_group(dve, "ffn", g, idx, per)
                for c in range(CT):
                    t = i * FC + 2 * half + c
                    dve.wait_ge(sil_done, t + 1)
                    conv(bank[2 * bs + c], c, fin, fy, fst, t + FT, V_WF, FCONV, HI_F, 2 * FT, fpt)
                    dve.drain()
                    STT(act_f[:, c, :], fy[:, c, :], vec[:, ds(t + FT + V_BF, 1)], fsil[:, c, :], ALU.add, ALU.mult)
                dve.drain()
                dve.sem_inc(grp_free[bs], 1)
                dst = (i & 1) * FC + 2 * half
                ah = act_hi[:, :, :, :].rearrange("p a c n -> p (a c) n")[:, ds(dst, CT), :]
                al = act_lo[:, :, :, :].rearrange("p a c n -> p (a c) n")[:, ds(dst, CT), :]
                CP(ah, act_f[:, :, :])
                dve.drain()
                T_(al, act_f[:, :, :], ah.bitcast(f32), ALU.subtract)
                dve.drain()
                dve.sem_inc(act_ready, 1)

            def ffn_down(name, sets, g, idx, per):
                for m in range(KT // CT):
                    bs, _ = grp(name, sets, g + m)
                    wait_group(dve, name, g + m, idx, per)
                    for c in range(CT):
                        residual(bank[2 * bs + c], 2 * m + c, 2 * m + c + 5 * KT, dtmp[:, :])
                        dve.drain()
                        dve.sem_inc(down_done, 1)
                    dve.sem_inc(grp_free[bs], 1)

            ffn_gate(0, 0, 0, 0, 0)
            ffn_val(1, 0, 0, 0, 0)
            ffn_gate(2, 0, 1, 0, 0)
            ffn_val(3, 0, 1, 0, 0)
            with dve.Fori(0, NCH - 1) as i:
                ffn_gate(4, i, 0, i + 1, 12)
                ffn_val(5, i, 0, i + 1, 12)
                ffn_down("ffn", 4, 6, i, 12)
                ffn_gate(14, i, 1, i + 1, 12)
                ffn_val(15, i, 1, i + 1, 12)
            ffn_down("last", 3, 0, 0, 0)

            dve.wait_ge(rs_ready, 3)
            with dve.Fori(0, KT // 2) as i:
                for s_ in range(2):
                    k = i * 2 + s_
                    xt = row(x[:, ds(k, 1), :])
                    last = STT(xt, xt, vec[:, ds(k + V_GF, 1)], rsb[:, :], ALU.mult, ALU.mult)
                dve.drain()
                dve.sem_inc(y_ready, 1)

        @block.tensor
        def _(pe):
            MM = nc.tensor.matmul
            row = lambda a: a.rearrange("p k n -> p (k n)")

            def tr(out, in_, n):
                return nc.tensor.transpose(out, in_, ident[0:n, 0:n])

            def wait_rest(name, j, i, per):
                _, cnt = split_at(name, j, i, per)
                if name != "ada1":
                    pe.wait_ge(lo_ready, cnt + (1 - LO_DVE))
                elif j % 2 == 0:
                    pe.wait_ge(lo_ready, i * (per // 2) + (j // 2 + 1))
                else:
                    pe.wait_ge(lo_dve, i * (per // 2) + (j // 2 + 1))

            def cond(name, g, sets, s_, i=0, per=0):
                j = 4 * g + s_
                if s_ == 0:
                    n0 = g + (2 * KT // CT if name == "ada2" else 0)
                    pe.wait_ge(cond_cp, i * per + (n0 + 3 - sets))
                r, _ = raw_at(name, j, i, 4 * per)
                q, n = split_at(name, j, i, 4 * per)
                out = bank[2 * (g % sets)]
                pe.wait_ge(hi_ready, n + 1)
                for k in range(KS):
                    MM(out[0:2 * NCP, 0:CT * P], cact[:, s_ * KS + k, :, :].rearrange("p m n -> p (m n)"), w_hi[q][:, k, :],
                       start=(s_ == 0 and k == 0), stop=False)
                wait_rest(name, j, i, 4 * per)
                for k in range(KS):
                    last = MM(out[0:NCP, 0:CT * P], cact[:, s_ * KS + k, 0, :], rest[r][:, k, :],
                              start=False, stop=(s_ * KS + k == KT - 1))
                    if k == 0:
                        last.then_inc(ring_free, 1)
                last.then_inc(raw_free[r], 1)

            def turn(name, g, sets, i=0, per=0):
                n0 = g + (2 * KT // CT if name == "ada2" else 0)
                bs, cnt = grp(name, sets, g, i, per)
                pe.wait_ge(cond_cp, i * per + (n0 + 3))
                pe.wait_ge(grp_free[bs], cnt + 1)
                for c in range(CT):
                    last = MM(bank[2 * bs + 1][:, c * NCP:(c + 1) * NCP], cond_t[:, c * P:(c + 1) * P],
                              cv["fold"][0:2 * NCP, :], start=True, stop=True)
                last.then_inc(cond_done, 1)

            def slot(name, j, hi_of, lo_of, banks, first, last_, i=0, per=0):
                r, _ = raw_at(name, j, i, per)
                q, cnt = split_at(name, j, i, per)
                pe.wait_ge(hi_ready, cnt + 1)
                for k in range(KS):
                    for c in range(CT):
                        w_ = w_hi[q][:, k, c * P:(c + 1) * P]
                        MM(banks[c][:, 0:N], w_, hi_of(k), start=(first and k == 0), stop=False)
                        ins = MM(banks[c][:, 0:N], w_, lo_of(k), start=False, stop=False)
                wait_rest(name, j, i, per)
                for k in range(KS):
                    for c in range(CT):
                        ins = MM(banks[c][:, 0:N], rest[r][:, k, c * P:(c + 1) * P], hi_of(k),
                                 start=False, stop=(last_ and k == KS - 1))
                        if k == 0 and c == 0:
                            ins.then_inc(ring_free, 1)
                ins.then_inc(raw_free[r], 1)

            def group(name, sets, g, j0, nslots, hi_t, lo_t, i=0, per_g=0, per_j=0, norm=None):
                bs, cnt = grp(name, sets, g, i, per_g)
                banks = (bank[2 * bs], bank[2 * bs + 1])
                pe.wait_ge(grp_free[bs], cnt + 1)
                for s_ in range(nslots):
                    if norm is not None:
                        pe.wait_ge(h_lo_ready, norm * KT + HB + (s_ + 1) * KS)
                        pe.wait_ge(h_hi_ready, norm * KT + (s_ + 1) * KS)
                    slot(name, j0 + s_, lambda k: hi_t(s_ * KS + k), lambda k: lo_t(s_ * KS + k), banks,
                         s_ == 0, s_ == nslots - 1, i, per_j)

            hh, hl = (lambda k: h_hi[:, k, :]), (lambda k: h_lo[:, k, :])

            def norm_part(n, s_, i=0):
                pe.wait_ge(sq_ready, 2 * i + (n * KT + s_ + 1))
                MM(bank[7][:, 0:N], ones, sq[:, s_ % 2, :], start=(s_ == 0), stop=(s_ == KT - 1)).then_inc(sq_used, 1)

            def norm_end(n):
                pe.wait_ge(sq_used, (n + 1) * KT + 2)
                pe.sem_inc(ssq_ready, 1)

            pe.wait_ge(c_ready, 2)

            def ada1_pair(first, i=0):
                for g in (first, first + 1):
                    for s_ in range(KT // KS):
                        cond("ada1", g, 2, s_, i, 2)
                        if s_ == 1 and g > 0:
                            turn("ada1", g - 1, 2, i, 2)
                    if g == 0:
                        pe.wait_ge(const_in, 48)
                    norm_part(0, g, i)

            ada1_pair(0)
            with pe.Fori(0, KT // CT - 2) as i:
                ada1_pair(2, i)
            ada1_pair(KT - 2)
            turn("ada1", KT - 1, 2)
            norm_end(0)
            group("small", 1, 0, 0, 4, hh, hl, norm=0)
            with pe.Fori(0, 6) as i:
                for g in range(2):
                    group("qkv", 2, g, 4 * g, 4, hh, hl, i, 2, 8)
            with pe.Fori(0, 2) as i:
                for g in range(2):
                    group("z", 2, g, 4 * g, 4, hh, hl, i, 2, 8)
            with pe.Fori(0, 4) as i:
                for g in range(2):
                    group("dsa", 2, g, 4 * g, 4, hh, hl, i, 2, 8)

            pe.wait_ge(row_act, 2)
            for g in (DSA_T // CT - 2, DSA_T // CT - 1):
                bs, cnt = grp("dsa", 2, g)
                pe.wait_ge(grp_free[bs], cnt + 2)
            for m, bk in ((0, 2), (3, 3)):
                for c in range(3):
                    w_ = P if c < 2 else NS
                    ins = tr(bank[bk][0:w_, c * H:(c + 1) * H], rows[:, m, c * P:c * P + w_], H)
            ins.then_inc(row_tr, 1)

            def head_sums(n, last_o):
                pe.wait_ge(G["rowm"], n)
                pe.wait_ge(G["sq"], n)
                if last_o:
                    MM(bank[7][:, 0:N], ones, sqb[:, 2, :], start=True, stop=True)
                MM(bank[2][:, 0:N], ones, sqb[:, 0, :], start=True, stop=True)
                MM(bank[3][:, 0:N], ones, sqb[:, 1, :], start=True, stop=True).then_inc(G["ssq"], 1)
                for m in range(3):
                    ins = MM(bank[4 + m][:, 0:N], ones[0:H, :], rows_m[:, m, :], start=True, stop=True)
                ins.then_inc(G["bc"], 1)

            head_sums(1, False)
            with pe.Fori(0, H) as h:
                def fill(n):
                    cond("ada2", n // 4, 1, n % 4, h, GA)
                pe.wait_ge(G["qk"], h + 1)
                for c in range(2):
                    MM(bank[2][:, c * 2 * P:(c + 1) * 2 * P].rearrange("p (m n) -> p m n", m=2), qk[:, 1, c * P:(c + 1) * P],
                       qk[:, :, c * P:(c + 1) * P], start=True, stop=True)
                MM(bank[3][0:NS, 0:2 * NS].rearrange("p (m n) -> p m n", m=2), qk[:, 1, SEQ:], qk[:, :, SEQ:],
                   start=True, stop=True).then_inc(G["gram"], 1)
                for c in range(2):
                    tr(bank[7][:, c * P:(c + 1) * P], qk[:, 1, c * P:(c + 1) * P], P)
                tr(bank[7][0:NS, 2 * P:3 * P], qk[:, 1, SEQ:], P).then_inc(G["kt"], 1)
                pe.wait_ge(G["sin"], h * 16 + 16)
                pe.wait_ge(G["br"], h + 1)
                for b in range(DB):
                    v2 = lambda a: a.rearrange("p m (t b) -> p m t b", b=DB)[:, :, :, b]
                    ins = MM(v2(bank[6][:, 0:2 * NS].rearrange("p (m n) -> p m n", m=2)), st_in[:, b, :], v2(qk[:, :, SEQ:]),
                             start=True, stop=True)
                ins.then_inc(G["kss"], 1)
                fill(0)
                pe.wait_ge(G["t1"], h + 1)
                for c in range(2):
                    tr(bank[3][:, c * P:(c + 1) * P], tt[:, c, :], P)
                tr(bank[3][0:NS, 2 * P:2 * P + NS], tt_s[:, 0, :], NS).then_inc(G["t1t"], 1)
                fill(1)
                for l in range(1, LV):
                    pe.wait_ge(G["t"], h * LV + l)
                    for c in range(2):
                        if l == 1 and c == 1:
                            MM(bank[4][0:NS, 2 * P:2 * P + NS], bt_s[:, :], tt_s[:, 1, :], start=True, stop=True)
                        ins = MM(bank[4][:, c * P:(c + 1) * P], bt_p[:, l % 2, c, :], tt[:, 2 + c, :], start=True, stop=True)
                    ins.then_inc(G["x"], 1)
                    fill(l + 1)
                    if l == 4:
                        turn("ada2", 0, 1, h, GA)
                    pe.wait_ge(G["xs"], h * (LV - 1) + l)
                    for c in range(2):
                        if l == 1 and c == 1:
                            MM(bank[3][0:NS, 0:NS], x_s[:, :], tt_s[:, 0, :], start=True, stop=True)
                        ins = MM(bank[5][:, c * P:(c + 1) * P], x_p[:, c, :], tt[:, c, :], start=True, stop=True)
                    if l < LV - 1:
                        for c in range(2):
                            ins = MM(bank[5][:, (2 + c) * P:(3 + c) * P], tt[:, c, :], x_p[:, c, :], start=True, stop=True)
                    ins.then_inc(G["dt"], 1)
                pe.wait_ge(G["t"], h * LV + LV)
                pe.wait_ge(G["kend"], h + 1)
                tr(bank[6][0:NS, P:2 * P], r_ts[:, :], P)
                tr(bank[6][:, 0:P], r_t[:, :], P).then_inc(G["rt"], 1)
                pe.wait_ge(G["rs"], h * 2 + 1)
                MM(bank[6][:, 0:P], tt[:, 0, :], r_p[:, :], start=True, stop=True)
                MM(bank[6][0:NS, P:2 * P], tt_s[:, 0, :], r_s[:, :], start=True, stop=True).then_inc(G["u"], 1)
                pe.wait_ge(G["us"], h * 2 + 1)
                MM(bank[3][:, 0:P], kend[:, 0, :], u_p[:, :], start=True, stop=True).then_inc(G["sa"], 1)
                MM(bank[2][:, 0:P], u_p[:, :], qkd_p[:, 0, :], start=True, stop=True)
                MM(bank[2][:, SEQ:N], u_s[:, :], qkd_s[:, :], start=True, stop=True)
                fill(8)
                pe.wait_ge(G["S1"], h + 1)
                MM(bank[4][:, 0:P], st_p[:, :], qk[:, 1, P:2 * P], start=True, stop=True).then_inc(G["ks"], 1)

                def sample_states(m):
                    for b in range(4):
                        ins = MM(bank[(5, 7)[m]][:, b * P:(b + 1) * P], kmask[:, 4 * m + b, :], u_s[:, :], start=True, stop=True)
                    ins.then_inc(G["ssm"], 1)

                sample_states(0)
                pe.wait_ge(G["rb"], h + 1)
                tr(bank[6][:, 0:P], r_t[:, :], P).then_inc(G["rt"], 1)
                sample_states(1)
                fill(9)
                turn("ada2", 1, 1, h, GA)
                pe.wait_ge(G["rs"], h * 2 + 2)
                MM(bank[6][:, 0:P], tt[:, 1, :], r_p[:, :], start=True, stop=True).then_inc(G["u"], 1)
                MM(bank[2][:, P:2 * P], st_p[:, :], qdec[:, :], start=True, stop=False)
                pe.wait_ge(G["us"], h * 2 + 2)
                MM(bank[3][:, 0:P], kend[:, 1, :], u_p[:, :], start=True, stop=True)
                MM(bank[2][:, P:2 * P], u_p[:, :], qkd_p[:, 1, :], start=False, stop=True).then_inc(G["sb"], 1)
                head_sums(h + 2, True)
                fill(10)
                fill(11)
                turn("ada2", 2, 1, h, GA)
            pe.wait_ge(G["dve"], 1)
            pe.wait_ge(G["br"], H + 1)

            turned = [(dsa[:, QH + m, :], 0) for m in range(KV)] + [(dsa[:, 12 + m, :], 1) for m in range(4)] + [(ikk[:, :], 1)]
            for n, (t_, kind) in enumerate(turned):
                if n >= 2:
                    pe.wait_ge(X["rotd"], n - 1)
                MM(bank[2 + n % 2][:, 0:N], rotm[:, kind, :], t_, start=True, stop=True).then_inc(X["rot"], 1)
            for c in range(2):
                for m in range(KV):
                    tr(bank[4][:, (c * KV + m) * P:(c * KV + m + 1) * P], dsa[:, QH + KV + m, c * P:(c + 1) * P], P)
            for m in range(KV):
                tr(bank[5][0:NS, m * P:(m + 1) * P], dsa[:, QH + KV + m, SEQ:], P)
            for c in range(3):
                w_ = P if c < 2 else NS
                ins = tr(bank[6][0:w_, c * IH:(c + 1) * IH], sm_iw[:, c * P:c * P + w_], IH)
            ins.then_inc(X["vt"], 1)
            pe.wait_ge(X["rotd"], len(turned))
            for n in range(3 * IH):
                if n >= 2:
                    pe.wait_ge(X["rel"], n - 1)
                h_ = n % IH
                pr = slice(ID * (h_ % 2), ID * (h_ % 2) + ID)
                if n < 2 * IH:
                    c = n // IH
                    ins = MM(bank[2 + n % 2][:, 0:SEQ], dsa[pr, 12 + h_ // 2, c * P:(c + 1) * P], ikk[pr, 0:SEQ], start=True, stop=True)
                else:
                    if n == 2 * IH:
                        pe.wait_ge(X["newk"], 1)
                    for q in range(DB // 2):
                        ins = MM(bank[2 + n % 2][0:NS, 0:L_S], iqm[:, h_, q, :], ik_c[:, q, :], start=(q == 0), stop=(q == DB // 2 - 1))
                ins.then_inc(X["idx"], 1)
            pe.wait_ge(X["rel"], 3 * IH)
            MM(bank[2][:, 0:N], rotm[:, 0, :], dsa[:, 0, :], start=True, stop=True).then_inc(X["rotq"], 1)
            with pe.Fori(0, QH) as h:
                def fill(n):
                    cond("ada2", GA * H, 1, n, h, XA)
                kv = (h >> 2).with_bounds(min_val=0, max_val=KV - 1)
                pe.wait_ge(X["q"], h + 1)
                kt_h = row(dsa[:, ds(kv + QH, 1), :])
                MM(bank[3][:, 0:P], q_r[:, 0:P], kt_h[:, 0:P], start=True, stop=True)
                MM(bank[3][:, P:P + SEQ], q_r[:, P:2 * P], kt_h[:, 0:SEQ], start=True, stop=True)
                for b in range(DB):
                    ins = MM(bank[4][0:NS, 0:L_S], q_m[:, b, :], row(kt_c[:, b, ds(kv, 1), :]), start=(b == 0), stop=(b == DB - 1))
                ins.then_inc(X["s"], 1)
                MM(bank[2][:, 0:N], rotm[:, 0, :], row(dsa[:, ds((h + 1) & (QH - 1), 1), :]), start=True, stop=True).then_inc(X["rotq"], 1)
                fill(0)
                pe.wait_ge(X["p"], h + 1)
                pe.wait_ge(X["pn"], h + 1)
                tr(bank[5][:, 0:P], s_p[:, 0:P], P)
                tr(bank[5][:, P:2 * P], s_p[:, P:2 * P], P)
                tr(bank[5][:, 2 * P:3 * P], s_p[:, 2 * P:3 * P], P)
                for g in range(2):
                    tr(bank[6][:, g * NS:(g + 1) * NS], s_s[:, g * PAGE:(g + 1) * PAGE], NS)
                tr(bank[6][0:NS, 2 * NS:3 * NS], pn[:, :], NS).then_inc(X["pt"], 1)
                fill(1)
                pe.wait_ge(X["pts"], h + 1)
                pe.wait_ge(X["ptm"], h + 1)
                vt = lambda c: vtok[:, c, ds(kv * HD, HD)]
                MM(bank[7][:, 0:P], p_t[:, 0, :], vt(0), start=True, stop=True)
                MM(bank[7][:, P:2 * P], p_t[:, 1, :], vt(0), start=True, stop=False)
                MM(bank[7][:, P:2 * P], p_t[:, 2, :], vt(1), start=False, stop=True)
                pe.wait_ge(X["q"], h + 2)
                for g in range(2):
                    for b in range(DB):
                        MM(bank[2][0:NS, 0:P], p_tm[:, g, b, :], v_c[:, b, g, ds(kv * HD, HD)], start=(g == 0 and b == 0), stop=False)
                MM(bank[2][0:NS, 0:P], pn_t[:, :], vtok_s[:, ds(kv * HD, HD)], start=False, stop=True).then_inc(X["o"], 1)
                fill(2)
                fill(3)
                pe.wait_ge(X["on"], h + 1)
                for c in range(2):
                    tr(bank[5][:, c * P:(c + 1) * P], o_n[:, c, :], P)
                tr(bank[5][:, SEQ:N], o_ns[:, :], NS).then_inc(X["ot"], 1)
                turn("ada2", GA * H, 1, h, XA)
            pe.wait_ge(X["end"], QH)

            oh, ol = (lambda k: og_hi[:, k, :]), (lambda k: og_lo[:, k, :])
            dh, dl = (lambda k: do_hi[:, k, :]), (lambda k: do_lo[:, k, :])
            with pe.Fori(0, 4) as i:
                for g0 in range(2):
                    j = 12 * g0
                    group("out", 4, 4 * g0, j, 4, hh, hl, i, 8, 24)
                    group("out", 4, 4 * g0 + 1, j + 4, 4, hh, hl, i, 8, 24)
                    group("out", 4, 4 * g0 + 2, j + 8, 2, oh, ol, i, 8, 24)
                    group("out", 4, 4 * g0 + 3, j + 10, 2, dh, dl, i, 8, 24)
            pe.wait_ge(mix_done, KT // CT + 1)
            mh, ml = (lambda k: mix[:, k, :]), (lambda k: mix_lo[:, k, :])
            for g in range(KT // CT):
                group("wo", 3, g, 4 * g, 4, mh, ml)
                for s_ in range(CT * g - CT, CT * g):
                    if s_ >= 0:
                        norm_part(1, s_)
            for s_ in range(KT - CT, KT):
                norm_part(1, s_)
            norm_end(1)

            def down(name, sets, g, j, chunk, i, per_g, per_j):
                pe.wait_ge(act_ready, chunk * 2 + 2)
                par = (chunk & 1) * FC
                ah = act_hi[:, :, :, :].rearrange("p a c n -> p (a c) n")
                al = act_lo[:, :, :, :].rearrange("p a c n -> p (a c) n")
                for m in range(KT // CT):
                    group(name, sets, g + m, j + m, 1, lambda k: row(ah[:, ds(par + k, 1), :]), lambda k: row(al[:, ds(par + k, 1), :]),
                          i, per_g, per_j)
                    for s_ in range(CT * m - 2 * CT, CT * m - CT):
                        if name == "last" and s_ >= 0:
                            norm_part(2, s_)

            for g in range(4):
                group("ffn", 4, g, 4 * g, 4, hh, hl, norm=None if g else 1)
            with pe.Fori(0, NCH - 1) as i:
                group("ffn", 4, 4, 16, 4, hh, hl, i, 12, 24)
                group("ffn", 4, 5, 20, 4, hh, hl, i, 12, 24)
                down("ffn", 4, 6, 24, i, i, 12, 24)
                group("ffn", 4, 14, 32, 4, hh, hl, i, 12, 24)
                group("ffn", 4, 15, 36, 4, hh, hl, i, 12, 24)
            down("last", 3, 0, 0, NCH - 1, 0, 0, 0)
            for s_ in range(KT - 2 * CT, KT):
                norm_part(2, s_)
            norm_end(2)


def slots_of(w, tiles):
    k, c = w.shape
    a = w.reshape(k // (KS * P), KS, P, c // (CT * P), CT * P)
    return a.transpose(3, 0, 2, 1, 4).reshape(c // (CT * P), k // (KS * P), P, SLOT)


def feature_major(a):
    t, f = a.shape
    return np.ascontiguousarray(a.reshape(t, f // P, P).transpose(2, 1, 0))


def columns(v):
    return v.reshape(-1, P).T


def kernel(**inputs):
    import concourse.bacc as bacc
    from concourse.bass_utils import run_bass_kernel_spmd

    I = {k: np.asarray(v) for k, v in inputs.items()}
    w_in = I["w_in"][0]
    cuts = np.cumsum([QKV_T * P, Z_T * P, H, H, QH * HD, KV * HD, KV * HD, IH * ID, ID, IH, D_MODEL, D_MODEL])
    qkv_w, z_w, a_w, b_w, dq_w, dk_w, dv_w, iq_w, ik_w, iw_w, gg_w, gd_w = np.split(w_in, cuts[:-1], axis=1)
    pad = lambda w, n: np.concatenate([w, np.zeros((D_MODEL, n - w.shape[1]), w.dtype)], 1)
    small = np.concatenate([ik_w, ik_w, pad(a_w, 32), pad(b_w, 32), pad(iw_w, 64)], 1)
    parts = {}
    flat = lambda a: a.reshape(-1, P, SLOT)
    ada_s = slots_of(I["w_ada"][0], None)
    half = 2 * KT // CT
    parts["ada1"], parts["ada2"] = flat(ada_s[:half]), flat(ada_s[half:])
    parts["qkv"], parts["z"] = flat(slots_of(qkv_w, None)), flat(slots_of(z_w, None))
    parts["dsa"] = flat(slots_of(np.concatenate([dq_w, dk_w, dv_w, iq_w], 1), None))
    parts["small"] = flat(slots_of(small, None))
    parts["out"] = flat(np.concatenate([slots_of(gg_w, None), slots_of(gd_w, None),
                                        slots_of(I["w_gdn_out"][0], None), slots_of(I["w_dsa_out"][0], None)], 1))
    parts["wo"] = flat(slots_of(I["w_o"][0], None))
    up, dn = slots_of(I["w_up"][0], None), slots_of(I["w_down"][0], None)
    seq = []
    for i in range(NCH):
        g0, v0 = up[2 * i], up[FT // 2 + 2 * i]
        g1, v1 = up[2 * i + 1], up[FT // 2 + 2 * i + 1]
        seq += [g0, v0] + ([dn[:, i - 1]] if i else []) + [g1, v1]
    parts["ffn"], parts["last"] = np.concatenate(seq), dn[:, NCH - 1]
    stream = np.concatenate([parts[n] for n, _ in PHASES])
    assert stream.shape == (NSLOTS, P, SLOT)

    time_major = lambda a: a.transpose(1, 0, 2).reshape(-1, a.shape[-1])
    c = constants()
    A = {
        "stream": stream,
        "x": feature_major(np.concatenate([I["x_prompt"][0], time_major(I["x_sample"])])).reshape(P, -1),
        "c": feature_major(np.concatenate([I["c_prompt"], I["c_sample"], np.zeros((NCP - NC, D_MODEL), np.float32)])).reshape(P, -1),
        "consts": np.concatenate([c[n].reshape(P, -1) for n in CONST_SIZE], 1),
        "vec": np.concatenate([columns(I["b_ada"][0]), columns(I["g_norm1"][0]), columns(I["g_norm2"][0]), columns(I["g_final"]),
                               columns(I["w_gdn_conv"][0]), columns(I["w_ffn_conv"][0]), columns(I["b_ffn_conv"][0]),
                               columns(I["g_gdn_norm"][0])], 1),
        "heads_v": np.stack([I["a_log"][0], I["dt_bias"][0]], 1),
        "ptab": I["page_table"].reshape(1, -1),
        "gdn_hist": feature_major(time_major(I["state_gdn_conv"][0])).reshape(P, -1),
        "ffn_hist": feature_major(time_major(I["state_ffn_conv"][0])).reshape(P, -1),
        "state": I["state_gdn"][0].transpose(1, 2, 0, 3).reshape(H, DK, DB * P),
        "ck": I["cache_k"][0].transpose(0, 3, 2, 1).reshape(NPOOL, HD, KV * PAGE),
        "cv": I["cache_v"][0].reshape(NPOOL, PAGE, KV * HD),
        "cik": I["cache_idx_k"][0].transpose(0, 2, 1),
    }
    outs = {"y": (P, KT * N), "k": (P, KV * N), "v": (P, KV * N), "ik": (ID, N), "state_p": (H, DK, P),
            "state_s": (H, DK, DB * P), "gdn_tail_p": (P, QKV_T * (CONV - 1)), "gdn_tail_s": (P, QKV_T * HI_S),
            "ffn_tail_p": (P, 2 * FT * (FCONV - 1)), "ffn_tail_s": (P, 2 * FT * HI_F)}
    nc = bacc.Bacc("TRN2", target_bir_lowering=False, num_devices=1)
    arrays, aps, oaps = {}, {}, {}
    for name, a in A.items():
        a = np.ascontiguousarray(a)
        arrays[f"in_{name}"] = a
        aps[name] = nc.dram_tensor(f"in_{name}", a.shape, mybir.dt.from_np(a.dtype), kind="ExternalInput").ap()
    for name, shape in outs.items():
        oaps[name] = nc.dram_tensor(f"out_{name}", shape, mybir.dt.float32, kind="ExternalOutput").ap()
    decoder_step(nc, aps, oaps)
    r = run_bass_kernel_spmd(nc, [arrays], core_ids=[0])
    o = {name: r.results[0][f"out_{name}"] for name in outs}

    def tokens(a, tiles):
        return a.reshape(-1, tiles, N).transpose(2, 1, 0).reshape(N, -1)

    def split(a):
        return a[:SEQ], a[SEQ:].reshape(TS, DB, -1).transpose(1, 0, 2)

    def tails(a, n_cols):
        t = a.reshape(P, -1, n_cols)
        return t.transpose(2, 1, 0).reshape(n_cols, -1)

    yp, ys = split(tokens(o["y"], KT))
    kp, ks = split(tokens(o["k"], KV))
    vp, vs = split(tokens(o["v"], KV))
    ip, isa = split(tokens(o["ik"], 1))
    gs = tails(o["gdn_tail_s"], HI_S).reshape(CONV - 1, DB, -1).transpose(1, 0, 2)
    fs = tails(o["ffn_tail_s"], HI_F).reshape(FCONV - 1, DB, -1).transpose(1, 0, 2)
    ss = o["state_s"].reshape(H, DK, DB, P).transpose(2, 0, 1, 3)
    c_ = np.ascontiguousarray
    return (c_(yp[None]), c_(ys),
            c_(kp.reshape(1, 1, SEQ, KV, HD)), c_(vp.reshape(1, 1, SEQ, KV, HD)), c_(ip[None, None]),
            c_(o["state_p"][None, None]), c_(tails(o["gdn_tail_p"], CONV - 1)[None, None]),
            c_(tails(o["ffn_tail_p"], FCONV - 1)[None, None]),
            c_(ks.reshape(1, DB, TS, KV, HD)), c_(vs.reshape(1, DB, TS, KV, HD)), c_(isa[None]),
            c_(ss[None]), c_(gs[None]), c_(fs[None]))
```
